# Optimizing a Trainium2 kernel written in Bass

```python
import math
import jax, jax.numpy as jnp
from jax import lax
import numpy as np

D_MODEL = 1024
BATCH = 1
SEQ = 256
DEPTH = 2

CTX_LEN = 256
GRID_W = 64
N_HEADS = 8
HEAD_DIM = 64
V_DIM = 2 * HEAD_DIM
QK_W = N_HEADS * 2 * HEAD_DIM
ATTN_WIDTH = N_HEADS * V_DIM
N_FGROUPS = 4
FGROUP_DIM = 128
FOURIER_WIDTH = N_FGROUPS * FGROUP_DIM
F_OFF = 2 * QK_W + ATTN_WIDTH
G_OFF = F_OFF + FOURIER_WIDTH
IN_WIDTH = G_OFF + 2 * D_MODEL
D_FF = 2816
AXIS_DIM = HEAD_DIM // 2
ROPE_BASE = 10000.0
Q_BLOCK = 128
N_MOD = 9
EPS = 1e-6


def rms_norm(x, g):
    xf = x.astype(jnp.float32)
    y = xf * lax.rsqrt(jnp.mean(xf * xf, axis=-1, keepdims=True) + EPS)
    return (y * g.astype(jnp.float32)).astype(x.dtype)

def adaln_mod(cond, w_mod, b_mod):
    m = jax.nn.silu(cond) @ w_mod + b_mod
    return m.reshape(cond.shape[:-1] + (N_MOD, D_MODEL))

def modulate(x, m, i):
    shift = m[:, 3 * i][:, None]
    scale = m[:, 3 * i + 1][:, None]
    return x * (1 + scale) + shift

def swiglu(u, w_in, w_out):
    a, b = jnp.split(u @ w_in, 2, axis=-1)
    return (jax.nn.silu(a) * b) @ w_out

def ffn_sublayer(x, m, i, g, w_in, w_out):
    u = modulate(rms_norm(x, g), m, i)
    return x + 0.5 * m[:, 3 * i + 2][:, None] * swiglu(u, w_in, w_out)

def split_qkv(p):
    B, S = p.shape[:2]
    q = p[..., :QK_W].reshape(B, S, N_HEADS, 2, HEAD_DIM)
    k = p[..., QK_W:2 * QK_W].reshape(B, S, N_HEADS, 2, HEAD_DIM)
    v = p[..., 2 * QK_W:F_OFF].reshape(B, S, N_HEADS, V_DIM)
    return q, k, v

def rope_tables(S):
    ROWS = S // GRID_W
    row = jnp.broadcast_to(jnp.arange(ROWS, dtype=jnp.int32)[:, None], (ROWS, GRID_W)).reshape(S)
    col = jnp.broadcast_to(jnp.arange(GRID_W, dtype=jnp.int32)[None, :], (ROWS, GRID_W)).reshape(S)
    inv = 1.0 / (ROPE_BASE ** (jnp.arange(0, AXIS_DIM, 2, dtype=jnp.float32) / AXIS_DIM))

    def tab(pos):
        ang = pos.astype(jnp.float32)[:, None] * inv[None, :]
        ang = jnp.concatenate([ang, ang], axis=-1)
        return jnp.cos(ang), jnp.sin(ang)

    cr, sr = tab(row)
    cc, sc = tab(col)
    return cr, sr, cc, sc

def rotate(xh, cos, sin):
    cos = cos[None, :, None, None, :].astype(xh.dtype)
    sin = sin[None, :, None, None, :].astype(xh.dtype)
    x1, x2 = jnp.split(xh, 2, axis=-1)
    return xh * cos + jnp.concatenate([-x2, x1], axis=-1) * sin

def apply_rope2d(x, tabs):
    cr, sr, cc, sc = tabs
    return jnp.concatenate([rotate(x[..., :AXIS_DIM], cr, sr),
                            rotate(x[..., AXIS_DIM:], cc, sc)], axis=-1)

def diff_attend(q, k, v, lam):
    s = jnp.einsum("bqhcd,bkhcd->bhcqk", q, k).astype(jnp.float32) * (HEAD_DIM ** -0.5)
    p = jax.nn.softmax(s, axis=-1)
    a = p[:, :, 0] - lam * p[:, :, 1]
    return jnp.einsum("bhqk,bkhe->bqhe", a.astype(v.dtype), v)

def latent_diff_attention(q, k_all, v_all, lam):
    B, S = q.shape[:2]
    nb = S // Q_BLOCK
    qb = jnp.moveaxis(q.reshape(B, nb, Q_BLOCK, N_HEADS, 2, HEAD_DIM), 1, 0)
    out = lax.map(lambda blk: diff_attend(blk, k_all, v_all, lam), qb)
    return jnp.moveaxis(out, 0, 1).reshape(B, S, N_HEADS, V_DIM)

def fourier_mix(f):
    B, S = f.shape[:2]
    fg = f.reshape(B, S, N_FGROUPS, FGROUP_DIM).astype(jnp.float32)
    y = jnp.fft.fft2(fg, axes=(1, 3), norm="ortho").real
    return y.reshape(B, S, FOURIER_WIDTH).astype(f.dtype)

def mixer_merge(attn_heads, f, g_logits, lam_init, subln_g, w_attn_out, w_four_out, b_gate, w_o):
    B, S = attn_heads.shape[:2]
    a = (rms_norm(attn_heads, subln_g) * (1 - lam_init)).reshape(B, S, ATTN_WIDTH) @ w_attn_out
    fr = fourier_mix(f) @ w_four_out
    ga, gf = jnp.split(g_logits, 2, axis=-1)
    merged = jax.nn.sigmoid(ga + b_gate[0]) * a + jax.nn.sigmoid(gf + b_gate[1]) * fr
    return merged @ w_o

def first_inputs(seed: int = 0) -> dict:
    key = jax.random.key(seed)
    ks = jax.random.split(key, 20)
    f32 = jnp.float32
    D = D_MODEL

    def nrm(k, shape, scale):
        return jax.random.normal(k, shape, f32) * scale

    return {
        "x": nrm(ks[0], (BATCH, SEQ, D), 1.0),
        "c": nrm(ks[1], (BATCH, D), 1.0),
        "ctx": nrm(ks[2], (BATCH, CTX_LEN, D), 1.0),
        "c_ctx": nrm(ks[3], (D,), 1.0),
        "w_mod": nrm(ks[4], (DEPTH, D, N_MOD * D), 0.5 * D ** -0.5),
        "b_mod": nrm(ks[5], (DEPTH, N_MOD * D), 0.01),
        "norm_g": 1.0 + nrm(ks[6], (DEPTH, 3, D), 0.1),
        "ffn_w_in": nrm(ks[7], (DEPTH, 2, D, 2 * D_FF), D ** -0.5),
        "ffn_w_out": nrm(ks[8], (DEPTH, 2, D_FF, D), D_FF ** -0.5),
        "w_in": nrm(ks[9], (DEPTH, D, IN_WIDTH), D ** -0.5),
        "b_gate": nrm(ks[10], (DEPTH, 2, D), 0.01),
        "lam_params": nrm(ks[11], (DEPTH, 4, HEAD_DIM), 0.1),
        "subln_g": 1.0 + nrm(ks[12], (DEPTH, V_DIM), 0.1),
        "w_attn_out": nrm(ks[13], (DEPTH, ATTN_WIDTH, D), ATTN_WIDTH ** -0.5),
        "w_four_out": nrm(ks[14], (DEPTH, FOURIER_WIDTH, D), FOURIER_WIDTH ** -0.5),
        "w_o": nrm(ks[15], (DEPTH, D, D), D ** -0.5),
        "final_g": 1.0 + nrm(ks[16], (D,), 0.1),
    }

def first_block(x, c, ctx, c_ctx, w_mod, b_mod, norm_g, ffn_w_in, ffn_w_out, w_in, b_gate,
              lam_params, subln_g, w_attn_out, w_four_out, w_o, final_g):
    S = x.shape[1]
    tabs = rope_tables(S)
    x_lat = x
    x_ctx = ctx
    for l in range(DEPTH):
        last = l == DEPTH - 1
        lam_init = 0.8 - 0.6 * math.exp(-0.3 * l)
        lp = lam_params[l].astype(jnp.float32)
        lam = jnp.exp(jnp.sum(lp[0] * lp[1])) - jnp.exp(jnp.sum(lp[2] * lp[3])) + lam_init

        m_lat = adaln_mod(c, w_mod[l], b_mod[l])
        m_ctx = adaln_mod(c_ctx, w_mod[l], b_mod[l])[None]

        x_lat = ffn_sublayer(x_lat, m_lat, 0, norm_g[l, 0], ffn_w_in[l, 0], ffn_w_out[l, 0])
        x_ctx = ffn_sublayer(x_ctx, m_ctx, 0, norm_g[l, 0], ffn_w_in[l, 0], ffn_w_out[l, 0])

        u_lat = modulate(rms_norm(x_lat, norm_g[l, 1]), m_lat, 1)
        u_ctx = modulate(rms_norm(x_ctx, norm_g[l, 1]), m_ctx, 1)
        p_lat = u_lat @ w_in[l]
        q_l, k_l, v_l = split_qkv(p_lat)
        q_l = apply_rope2d(q_l, tabs)
        k_l = apply_rope2d(k_l, tabs)
        if last:
            kv_c = u_ctx @ w_in[l][:, QK_W:F_OFF]
            B = kv_c.shape[0]
            k_c = kv_c[..., :QK_W].reshape(B, CTX_LEN, N_HEADS, 2, HEAD_DIM)
            v_c = kv_c[..., QK_W:].reshape(B, CTX_LEN, N_HEADS, V_DIM)
        else:
            p_ctx = u_ctx @ w_in[l]
            q_c, k_c, v_c = split_qkv(p_ctx)

        k_all = jnp.concatenate([k_c, k_l], axis=1)
        v_all = jnp.concatenate([v_c, v_l], axis=1)
        attn_l = latent_diff_attention(q_l, k_all, v_all, lam)
        mix_l = mixer_merge(attn_l, p_lat[..., F_OFF:G_OFF], p_lat[..., G_OFF:], lam_init,
                            subln_g[l], w_attn_out[l], w_four_out[l], b_gate[l], w_o[l])
        x_lat = x_lat + m_lat[:, 5][:, None] * mix_l

        if not last:
            attn_c = diff_attend(q_c, k_c, v_c, lam)
            mix_c = mixer_merge(attn_c, p_ctx[..., F_OFF:G_OFF], p_ctx[..., G_OFF:], lam_init,
                                subln_g[l], w_attn_out[l], w_four_out[l], b_gate[l], w_o[l])
            x_ctx = x_ctx + m_ctx[:, 5][:, None] * mix_c
            x_ctx = ffn_sublayer(x_ctx, m_ctx, 2, norm_g[l, 2], ffn_w_in[l, 1], ffn_w_out[l, 1])

        x_lat = ffn_sublayer(x_lat, m_lat, 2, norm_g[l, 2], ffn_w_in[l, 1], ffn_w_out[l, 1])

    return rms_norm(x_lat, final_g)


DEPTH_2 = 1

HEAD_DIM_A = 64
WIDTH_A = D_MODEL // 2
N_HEADS_A = WIDTH_A // HEAD_DIM_A
HEAD_DIM_B = 64
WIDTH_B = D_MODEL // 2
N_HEADS_B = WIDTH_B // HEAD_DIM_B
CONV_K = 5
CHUNK = 64
N_DIR = 2
N_GROUPS = 4
EXPERTS_PER_GROUP = 8
N_EXPERTS = N_GROUPS * EXPERTS_PER_GROUP
TOP_K = 2
D_EXPERT = D_MODEL // 4
N_MOD_2 = 6
NEG_INF = -1e30

SPLIT_WIDTHS = (3 * WIDTH_A, WIDTH_A, 2 * N_DIR * N_HEADS_A,
                2 * WIDTH_B, WIDTH_B, WIDTH_B, 2 * N_DIR * N_HEADS_B, 2 * D_MODEL)
D_IN = sum(SPLIT_WIDTHS)
SPLIT_POINTS = tuple(sum(SPLIT_WIDTHS[: i + 1]) for i in range(len(SPLIT_WIDTHS) - 1))


def rmsnorm(x, g):
    xf = x.astype(jnp.float32)
    y = xf * lax.rsqrt(jnp.mean(xf * xf, axis=-1, keepdims=True) + EPS)
    return y * g.astype(jnp.float32)

def l2norm(t):
    return t * lax.rsqrt(jnp.sum(t * t, axis=-1, keepdims=True) + EPS)

def head_layernorm(t, g):
    mu = jnp.mean(t, axis=-1, keepdims=True)
    tc = t - mu
    return tc * lax.rsqrt(jnp.mean(tc * tc, axis=-1, keepdims=True) + EPS) * g

def centred_conv(x, w):
    c = x.shape[-1]
    return lax.conv_general_dilated(
        x, w[:, None, :].astype(x.dtype), window_strides=(1,),
        padding=[(CONV_K // 2, CONV_K // 2)],
        dimension_numbers=("NWC", "WIO", "NWC"), feature_group_count=c)

def chunk_heads(t):
    b, s, h, d = t.shape
    return t.reshape(b, s // CHUNK, CHUNK, h, d).transpose(0, 3, 1, 2, 4)

def chunk_scalar(t):
    b, s, h = t.shape
    return t.reshape(b, s // CHUNK, CHUNK, h).transpose(0, 3, 1, 2)

def unchunk(t):
    b, h, n, l, d = t.shape
    return t.transpose(0, 2, 3, 1, 4).reshape(b, n * l, h, d)

def flip_seq(t):
    return jnp.flip(t, axis=1)

def gated_delta_chunked(q, k, v, g, beta):
    L = q.shape[-2]
    dv = v.shape[-1]
    b, h, n, _, dk = k.shape
    tri_incl = jnp.tril(jnp.ones((L, L), dtype=bool))
    tri_strict = jnp.tril(jnp.ones((L, L), dtype=bool), -1)
    g_cum = jnp.cumsum(g, axis=-1)
    decay = jnp.exp(jnp.where(tri_incl, g_cum[..., :, None] - g_cum[..., None, :], NEG_INF))
    k_beta = k * beta[..., None]
    lower = jnp.where(tri_strict, jnp.einsum("bhnid,bhnjd->bhnij", k_beta, k) * decay, 0.0)
    lhs = lower + jnp.eye(L, dtype=lower.dtype)
    rhs = jnp.concatenate([v * beta[..., None], k_beta * jnp.exp(g_cum)[..., None]], axis=-1)
    sol = lax.linalg.triangular_solve(lhs, rhs, left_side=True, lower=True, unit_diagonal=True)
    u, w = sol[..., :dv], sol[..., dv:]
    k_to_end = k * jnp.exp(g_cum[..., -1:] - g_cum)[..., None]
    chunk_decay = jnp.exp(g_cum[..., -1])

    def step(state, xs):
        u_c, w_c, kd_c, cd_c = xs
        v_new = u_c - jnp.einsum("bhlk,bhkv->bhlv", w_c, state)
        state_next = state * cd_c[..., None, None] + jnp.einsum("bhlk,bhlv->bhkv", kd_c, v_new)
        return state_next, (state, v_new)

    s0 = jnp.zeros((b, h, dk, dv), jnp.float32)
    xs = tuple(jnp.moveaxis(t, 2, 0) for t in (u, w, k_to_end, chunk_decay))
    _, (s_prev, v_new) = lax.scan(step, s0, xs)
    s_prev = jnp.moveaxis(s_prev, 0, 2)
    v_new = jnp.moveaxis(v_new, 0, 2)
    intra = jnp.einsum("bhnid,bhnjd->bhnij", q, k) * decay
    return (jnp.einsum("bhnlk,bhnkv->bhnlv", q * jnp.exp(g_cum)[..., None], s_prev)
            + jnp.einsum("bhnij,bhnjv->bhniv", intra, v_new))

def mlstm_chunked(q, k, v, i_pre, f_pre):
    L = q.shape[-2]
    b, h, n, _, dk = k.shape
    dv = v.shape[-1]
    tri_incl = jnp.tril(jnp.ones((L, L), dtype=bool))
    bcum = jnp.cumsum(jax.nn.log_sigmoid(f_pre), axis=-1)
    b_last = bcum[..., -1]
    a_end = b_last[..., None] - bcum + i_pre

    def step(carry, xs):
        c_st, n_st, m_st = carry
        k_c, v_c, a_c, bl_c = xs
        m_next = jnp.maximum(bl_c + m_st, jnp.max(a_c, axis=-1))
        scale_prev = jnp.exp(bl_c + m_st - m_next)
        wgt = jnp.exp(a_c - m_next[..., None])
        c_next = c_st * scale_prev[..., None, None] + jnp.einsum("bhlk,bhlv->bhkv", k_c * wgt[..., None], v_c)
        n_next = n_st * scale_prev[..., None] + jnp.einsum("bhl,bhlk->bhk", wgt, k_c)
        return (c_next, n_next, m_next), (c_st, n_st, m_st)

    init = (jnp.zeros((b, h, dk, dv), jnp.float32), jnp.zeros((b, h, dk), jnp.float32),
            jnp.zeros((b, h), jnp.float32))
    xs = tuple(jnp.moveaxis(t, 2, 0) for t in (k, v, a_end, b_last))
    _, (c_prev, n_prev, m_prev) = lax.scan(step, init, xs)
    c_prev = jnp.moveaxis(c_prev, 0, 2)
    n_prev = jnp.moveaxis(n_prev, 0, 2)
    m_prev = jnp.moveaxis(m_prev, 0, 2)
    log_d = jnp.where(tri_incl, bcum[..., :, None] - bcum[..., None, :] + i_pre[..., None, :], NEG_INF)
    log_inter = bcum + m_prev[..., None]
    m_t = jnp.maximum(log_inter, jnp.max(log_d, axis=-1))
    d_mat = jnp.exp(log_d - m_t[..., None])
    inter_w = jnp.exp(log_inter - m_t)
    qk = jnp.einsum("bhntd,bhnsd->bhnts", q, k) * d_mat
    num = (jnp.einsum("bhnts,bhnsv->bhntv", qk, v)
           + inter_w[..., None] * jnp.einsum("bhntk,bhnkv->bhntv", q, c_prev))
    den = jnp.sum(qk, axis=-1) + inter_w * jnp.einsum("bhntk,bhnk->bhnt", q, n_prev)
    return num / jnp.maximum(jnp.abs(den), jnp.exp(-m_t))[..., None]

def run_gdn(q, k, v, g, beta):
    return unchunk(gated_delta_chunked(chunk_heads(q), chunk_heads(k), chunk_heads(v),
                                       chunk_scalar(g), chunk_scalar(beta)))

def run_mlstm(q, k, v, i_pre, f_pre):
    return unchunk(mlstm_chunked(chunk_heads(q), chunk_heads(k), chunk_heads(v),
                                 chunk_scalar(i_pre), chunk_scalar(f_pre)))

def hybrid_mixer(h, w_in, gdn_conv_w, gdn_a_log, gdn_dt_bias, gdn_norm_g,
                 mlstm_conv_w, mlstm_i_bias, mlstm_f_bias, mlstm_norm_g,
                 w_branch_a, w_branch_b, w_out):
    bsz, s, _ = h.shape
    proj = jnp.einsum("bsd,de->bse", h, w_in.astype(jnp.float32))
    a_qkv, a_z, a_gates, b_qk, b_v, b_o, b_gates, merge = jnp.split(proj, SPLIT_POINTS, axis=-1)

    a_qkv = jax.nn.silu(centred_conv(a_qkv, gdn_conv_w.astype(jnp.float32)))
    aq, ak, av = jnp.split(a_qkv, 3, axis=-1)
    aq = l2norm(aq.reshape(bsz, s, N_HEADS_A, HEAD_DIM_A)) * (HEAD_DIM_A ** -0.5)
    ak = l2norm(ak.reshape(bsz, s, N_HEADS_A, HEAD_DIM_A))
    av = av.reshape(bsz, s, N_HEADS_A, HEAD_DIM_A)
    a_gates = jnp.moveaxis(a_gates.reshape(bsz, s, N_DIR, 2, N_HEADS_A), 2, 0)
    g = -jnp.exp(gdn_a_log.astype(jnp.float32))[:, None, None, :] * jax.nn.softplus(
        a_gates[..., 0, :] + gdn_dt_bias.astype(jnp.float32)[:, None, None, :])
    beta = jax.nn.sigmoid(a_gates[..., 1, :])
    o_a = (run_gdn(aq, ak, av, g[0], beta[0])
           + flip_seq(run_gdn(flip_seq(aq), flip_seq(ak), flip_seq(av), flip_seq(g[1]), flip_seq(beta[1]))))
    o_a = rmsnorm(o_a, gdn_norm_g) * jax.nn.silu(a_z.reshape(bsz, s, N_HEADS_A, HEAD_DIM_A))
    o_a = o_a.reshape(bsz, s, WIDTH_A)

    b_qk = jax.nn.silu(centred_conv(b_qk, mlstm_conv_w.astype(jnp.float32)))
    bq, bk = jnp.split(b_qk, 2, axis=-1)
    bq = bq.reshape(bsz, s, N_HEADS_B, HEAD_DIM_B)
    bk = bk.reshape(bsz, s, N_HEADS_B, HEAD_DIM_B) * (HEAD_DIM_B ** -0.5)
    bv = b_v.reshape(bsz, s, N_HEADS_B, HEAD_DIM_B)
    b_gates = jnp.moveaxis(b_gates.reshape(bsz, s, N_DIR, 2, N_HEADS_B), 2, 0)
    i_pre = b_gates[..., 0, :] + mlstm_i_bias.astype(jnp.float32)[:, None, None, :]
    f_pre = b_gates[..., 1, :] + mlstm_f_bias.astype(jnp.float32)[:, None, None, :]
    h_b = (run_mlstm(bq, bk, bv, i_pre[0], f_pre[0])
           + flip_seq(run_mlstm(flip_seq(bq), flip_seq(bk), flip_seq(bv), flip_seq(i_pre[1]), flip_seq(f_pre[1]))))
    h_b = head_layernorm(h_b, mlstm_norm_g.astype(jnp.float32).reshape(N_HEADS_B, HEAD_DIM_B))
    h_b = (h_b * jax.nn.sigmoid(b_o.reshape(bsz, s, N_HEADS_B, HEAD_DIM_B))).reshape(bsz, s, WIDTH_B)

    gate_a, gate_b = jnp.split(jax.nn.sigmoid(merge), 2, axis=-1)
    y = (gate_a * jnp.einsum("bse,ed->bsd", o_a, w_branch_a.astype(jnp.float32))
         + gate_b * jnp.einsum("bse,ed->bsd", h_b, w_branch_b.astype(jnp.float32)))
    return jnp.einsum("bsd,de->bse", y, w_out.astype(jnp.float32))

def hierarchical_moe(h, router_group, router_expert, w_gate, w_up, w_down):
    bsz, s, d = h.shape
    ht = h.reshape(bsz * s, d)
    group_logits = ht @ router_group.astype(jnp.float32)
    group_probs = jax.nn.softmax(group_logits, axis=-1)
    p_group, g_sel = lax.top_k(group_probs, 1)
    expert_logits = (ht @ router_expert.astype(jnp.float32)).reshape(-1, N_GROUPS, EXPERTS_PER_GROUP)
    in_group = jnp.take_along_axis(expert_logits, g_sel[:, :, None], axis=1)[:, 0]
    top_vals, top_idx = lax.top_k(in_group, TOP_K)
    top_w = jax.nn.softmax(top_vals, axis=-1) * p_group
    expert_id = g_sel * EXPERTS_PER_GROUP + top_idx
    combine = jnp.sum(jax.nn.one_hot(expert_id, N_EXPERTS, dtype=jnp.float32) * top_w[..., None], axis=1)
    y = jnp.zeros_like(ht)
    for grp in range(N_GROUPS):
        sl = slice(grp * EXPERTS_PER_GROUP, (grp + 1) * EXPERTS_PER_GROUP)
        hg = jnp.einsum("td,edf->tef", ht, w_gate[sl].astype(jnp.float32))
        hu = jnp.einsum("td,edf->tef", ht, w_up[sl].astype(jnp.float32))
        act = jax.nn.silu(hg) * hu * combine[:, sl, None]
        y = y + jnp.einsum("tef,efd->td", act, w_down[sl].astype(jnp.float32))
    return y.reshape(bsz, s, d)

def second_inputs(seed: int = 0) -> dict:
    key = jax.random.key(seed)
    ks = jax.random.split(key, 24)
    nrm = lambda k, shape, scale: jax.random.normal(k, shape, jnp.float32) * scale
    gain = lambda k, shape: 1.0 + 0.02 * jax.random.normal(k, shape, jnp.float32)
    dt = jnp.exp(jax.random.uniform(ks[9], (DEPTH_2, N_DIR, N_HEADS_A), jnp.float32,
                                    np.log(1e-3), np.log(1e-1)))
    return {
        "x": nrm(ks[0], (BATCH, SEQ, D_MODEL), 1.0),
        "c": nrm(ks[1], (BATCH, D_MODEL), 1.0),
        "ada_w": nrm(ks[2], (DEPTH_2, D_MODEL, N_MOD_2 * D_MODEL), 0.5 * D_MODEL ** -0.5),
        "ada_b": nrm(ks[3], (DEPTH_2, N_MOD_2 * D_MODEL), 0.01),
        "norm_mix_g": gain(ks[4], (DEPTH_2, D_MODEL)),
        "norm_ffn_g": gain(ks[5], (DEPTH_2, D_MODEL)),
        "w_in": nrm(ks[6], (DEPTH_2, D_MODEL, D_IN), D_MODEL ** -0.5),
        "gdn_conv_w": nrm(ks[7], (DEPTH_2, CONV_K, 3 * WIDTH_A), CONV_K ** -0.5),
        "gdn_a_log": jnp.log(jax.random.uniform(ks[8], (DEPTH_2, N_DIR, N_HEADS_A), jnp.float32, 1.0, 16.0)),
        "gdn_dt_bias": jnp.log(jnp.expm1(dt)),
        "gdn_norm_g": gain(ks[10], (DEPTH_2, HEAD_DIM_A)),
        "mlstm_conv_w": nrm(ks[11], (DEPTH_2, CONV_K, 2 * WIDTH_B), CONV_K ** -0.5),
        "mlstm_i_bias": nrm(ks[12], (DEPTH_2, N_DIR, N_HEADS_B), 0.1),
        "mlstm_f_bias": 3.0 + 3.0 * jax.random.uniform(ks[13], (DEPTH_2, N_DIR, N_HEADS_B), jnp.float32),
        "mlstm_norm_g": gain(ks[14], (DEPTH_2, WIDTH_B)),
        "w_branch_a": nrm(ks[15], (DEPTH_2, WIDTH_A, D_MODEL), WIDTH_A ** -0.5),
        "w_branch_b": nrm(ks[16], (DEPTH_2, WIDTH_B, D_MODEL), WIDTH_B ** -0.5),
        "w_out": nrm(ks[17], (DEPTH_2, D_MODEL, D_MODEL), D_MODEL ** -0.5),
        "router_group": nrm(ks[18], (DEPTH_2, D_MODEL, N_GROUPS), D_MODEL ** -0.5),
        "router_expert": nrm(ks[19], (DEPTH_2, D_MODEL, N_EXPERTS), D_MODEL ** -0.5),
        "w_gate": nrm(ks[20], (DEPTH_2, N_EXPERTS, D_MODEL, D_EXPERT), D_MODEL ** -0.5),
        "w_up": nrm(ks[21], (DEPTH_2, N_EXPERTS, D_MODEL, D_EXPERT), D_MODEL ** -0.5),
        "w_down": nrm(ks[22], (DEPTH_2, N_EXPERTS, D_EXPERT, D_MODEL), D_EXPERT ** -0.5),
        "final_norm_g": gain(ks[23], (D_MODEL,)),
    }

def second_block(x, c, ada_w, ada_b, norm_mix_g, norm_ffn_g, w_in, gdn_conv_w, gdn_a_log,
              gdn_dt_bias, gdn_norm_g, mlstm_conv_w, mlstm_i_bias, mlstm_f_bias, mlstm_norm_g,
              w_branch_a, w_branch_b, w_out, router_group, router_expert, w_gate, w_up, w_down,
              final_norm_g):
    out_dtype = x.dtype
    h_res = x.astype(jnp.float32)
    c_act = jax.nn.silu(c.astype(jnp.float32))
    for l in range(DEPTH_2):
        mod = c_act @ ada_w[l].astype(jnp.float32) + ada_b[l].astype(jnp.float32)
        sh1, sc1, gt1, sh2, sc2, gt2 = [m[:, None, :] for m in jnp.split(mod, N_MOD_2, axis=-1)]
        hn = rmsnorm(h_res, norm_mix_g[l]) * (1.0 + sc1) + sh1
        h_res = h_res + gt1 * hybrid_mixer(
            hn, w_in[l], gdn_conv_w[l], gdn_a_log[l], gdn_dt_bias[l], gdn_norm_g[l],
            mlstm_conv_w[l], mlstm_i_bias[l], mlstm_f_bias[l], mlstm_norm_g[l],
            w_branch_a[l], w_branch_b[l], w_out[l])
        hn = rmsnorm(h_res, norm_ffn_g[l]) * (1.0 + sc2) + sh2
        h_res = h_res + gt2 * hierarchical_moe(hn, router_group[l], router_expert[l],
                                               w_gate[l], w_up[l], w_down[l])
    return rmsnorm(h_res, final_norm_g).astype(out_dtype)


def setup_inputs(seed=0):
    out = dict(first_inputs(seed))
    for name, value in second_inputs(seed + 1).items():
        if name != "x":
            out[name + "_2"] = value
    return out


def reference(
    x, c, ctx, c_ctx, w_mod, b_mod, norm_g, ffn_w_in, ffn_w_out, w_in, b_gate, lam_params,
    subln_g, w_attn_out, w_four_out, w_o, final_g, c_2, ada_w_2, ada_b_2, norm_mix_g_2,
    norm_ffn_g_2, w_in_2, gdn_conv_w_2, gdn_a_log_2, gdn_dt_bias_2, gdn_norm_g_2,
    mlstm_conv_w_2, mlstm_i_bias_2, mlstm_f_bias_2, mlstm_norm_g_2, w_branch_a_2, w_branch_b_2,
    w_out_2, router_group_2, router_expert_2, w_gate_2, w_up_2, w_down_2, final_norm_g_2,
):
    x = first_block(
        x, c, ctx, c_ctx, w_mod, b_mod, norm_g, ffn_w_in, ffn_w_out, w_in, b_gate, lam_params,
        subln_g, w_attn_out, w_four_out, w_o, final_g,
    )
    return second_block(
        x, c_2, ada_w_2, ada_b_2, norm_mix_g_2, norm_ffn_g_2, w_in_2, gdn_conv_w_2, gdn_a_log_2,
        gdn_dt_bias_2, gdn_norm_g_2, mlstm_conv_w_2, mlstm_i_bias_2, mlstm_f_bias_2,
        mlstm_norm_g_2, w_branch_a_2, w_branch_b_2, w_out_2, router_group_2, router_expert_2,
        w_gate_2, w_up_2, w_down_2, final_norm_g_2,
    )


_drawn_inputs = setup_inputs


def setup_inputs(seed=0):
    import zlib

    import numpy as np

    out = dict(_drawn_inputs(seed))
    spreads = {}
    factors = {'b_mod': 3.855,
     'b_gate': 8.0,
     'lam_params': 3.078,
     'subln_g': 2.938,
     'ada_b_2': 4.746,
     'norm_mix_g_2': 8.0,
     'norm_ffn_g_2': 8.0,
     'gdn_norm_g_2': 8.0,
     'mlstm_i_bias_2': 64.0,
     'mlstm_f_bias_2': 3.054,
     'mlstm_norm_g_2': 64.0,
     'final_norm_g_2': 8.107}
    for name, (base, spread) in spreads.items():
        noise = np.random.default_rng([zlib.crc32(name.encode()), seed]).standard_normal(out[name].shape)
        drawn = base * np.exp(spread * noise) if base else spread * noise
        out[name] = __import__('jax').numpy.asarray(drawn.astype(out[name].dtype))
    for name, factor in factors.items():
        out[name] = (out[name] * factor).astype(out[name].dtype)
    return out
```

```python
import math
from contextlib import ExitStack

import numpy as np
import concourse.bass as bass
from concourse import mybir

ALU = mybir.AluOpType
ACT = mybir.ActivationFunctionType
AX = mybir.AxisListType
F32 = mybir.dt.float32

STOP = 99
D = 1024
DFF = 2816
SLOTS = 4
SLOTW = 4096
EPS = 1e-6
NEG = -1e30

COLS = {}
_n = 0
for _k, _w in (("c", 8), ("cx", 8), ("c2", 8), ("bmod0", 72), ("bmod1", 72), ("g0", 24), ("g1", 24),
               ("bg0", 16), ("bg1", 16), ("sub0", 1), ("sub1", 1), ("fin", 8), ("ada", 48), ("nmix", 8),
               ("nffn", 8), ("cva", 60), ("cvb", 40), ("gdn", 1), ("mln", 4), ("fin2", 8), ("rows", 4),
               ("lam0", 4), ("lam1", 4)):
    COLS[_k] = (_n, _w)
    _n += _w
NCOL = _n

C0 = {"ident": (0, 128), "ones": (128, 128), "bones": (256, 128)}
C1 = {"rot": (0, 128), "cos": (128, 256), "sin": (384, 256), "dft": (640, 256), "cs": (896, 512), "ss": (1408, 512)}
C2 = {"neg": (0, 256), "strict": (256, 256), "lvl": (512, 6 * 256), "g8": (2048, 8), "g4": (2056, 4)}
NC0, NC1, NC2 = 384, 1920, 2060


def consts():
    f = np.float32
    c0 = np.zeros((128, NC0), f)
    c0[:, 0:128] = np.eye(128)
    c0[:, 128:256] = 1
    c0[:64, 256:320] = 1
    c0[64:, 320:384] = 1
    c1 = np.zeros((128, NC1), f)
    r = np.zeros((128, 128), f)
    for b in range(0, 128, 32):
        for i in range(16):
            r[b + 16 + i, b + i] = -1
            r[b + i, b + 16 + i] = 1
    c1[:, 0:128] = r
    inv = (1.0 / (f(10000.0) ** (np.arange(0, 32, 2, dtype=f) / f(32)))).astype(f)
    t = np.arange(256)
    for half, pos in ((0, t // 64), (1, t % 64)):
        ang = pos.astype(f)[:, None] * inv[None, :]
        ang = np.concatenate([ang, ang], axis=-1).T
        for comp in (0, 64):
            c1[comp + 32 * half:comp + 32 * half + 32, 128:384] = np.cos(ang)
            c1[comp + 32 * half:comp + 32 * half + 32, 384:640] = np.sin(ang)
    d = np.arange(128)
    a = 2 * np.pi * ((d[:, None] * d[None, :]) % 128) / 128
    c1[:, 640:768] = np.cos(a)
    c1[:, 768:896] = np.sin(a)
    s = np.arange(256)
    b = 2 * np.pi * ((s[:, None] * s[None, :]) % 256) / 256
    sc = 1 / math.sqrt(256 * 128)
    c1[:, 896:1408] = (np.cos(b) * sc).reshape(2, 128, 256).transpose(1, 0, 2).reshape(128, 512)
    c1[:, 1408:1920] = (-np.sin(b) * sc).reshape(2, 128, 256).transpose(1, 0, 2).reshape(128, 512)
    c2 = np.zeros((128, NC2), f)
    j, i = np.meshgrid(np.arange(128), np.arange(128), indexing="ij")
    same = (i // 64) == (j // 64)
    for dr in range(2):
        ok = same & ((i >= j) if dr == 0 else (i <= j))
        c2[:, dr * 128:dr * 128 + 128] = np.where(ok, 0, NEG)
        c2[:, 256 + dr * 128:384 + dr * 128] = (ok & (i != j))
        for lv in range(6):
            w = 1 << lv
            blk = (i // (2 * w)) == (j // (2 * w))
            hi_i, hi_j = (i // w) % 2 == 1, (j // w) % 2 == 1
            m = blk & (hi_i & ~hi_j if dr == 0 else ~hi_i & hi_j)
            o = 512 + lv * 256 + dr * 128
            c2[:, o:o + 128] = m
    c2[:, 2048:2056] = np.arange(8, 0, -1)
    c2[:, 2056:2060] = np.arange(4, 0, -1)
    return c0, c1, c2


class Eng:

    def __init__(self, eng, sem, link):
        self.eng, self.sem, self.linked = eng, sem, link
        self.ops, self.n, self.seen = [], 0, {}

    def wait(self, *toks):
        for t in toks:
            if t is None:
                continue
            if isinstance(t, list):
                self.wait(*t)
                continue
            s, v = t
            if self.seen.get(id(s), 0) < v:
                self.seen[id(s)] = v
                self.ops.append((None, s, v, None))

    @property
    def last(self):
        return (self.sem, self.n) if self.n else None

    def __call__(self, fn, *args, w=(), sig=True, **kw):
        self.wait(*w)
        if self.linked:
            self.wait(self.last)
        self.ops.append((fn, args, kw, (self.sem, 1) if sig else None))
        if sig:
            self.n += 1
        return (self.sem, self.n)

    def dma(self, fn, out, in_, sem, w=()):
        self.wait(*w)
        self.ops.append((fn, (out, in_), {}, (sem, 16)))

    def emit(self, e):
        for fn, a, k, s in self.ops:
            if fn is None:
                e.wait_ge(a, k)
            else:
                ins = fn(*a, **k)
                if s is not None:
                    ins.then_inc(*s)


class Pool:

    def __init__(self, tiles):
        self.tiles, self.rel, self.i = tiles, [[] for _ in tiles], 0

    def take(self):
        b = self.i
        self.i = (b + 1) % len(self.tiles)
        r = self.rel[b]
        assert r is not None, "taken before it was given back"
        self.rel[b] = None
        return self.tiles[b], r, b

    def give(self, b, *toks):
        self.rel[b] = list(toks)


def program(nc, ws, cols_d, c0_d, c1_d, c2_d, out_d, plan):
    with ExitStack() as ctx:
        def sb(name, shape):
            return ctx.enter_context(nc.sbuf_tensor(name, shape, F32))

        def sem(name):
            return ctx.enter_context(nc.semaphore(name))

        V = Eng(nc.vector, sem("s_v"), True)
        A = Eng(nc.scalar, sem("s_a"), True)
        P = Eng(nc.tensor, sem("s_p"), False)
        S = Eng(nc.sync, sem("s_s"), False)
        s_c = sem("s_c")
        s_c2 = sem("s_c2")
        s_out = sem("s_out")
        s_w = [sem(f"s_w{i}") for i in range(SLOTS)]

        vec, act, pe = nc.vector, nc.scalar, nc.tensor

        X = sb("X", [128, 8, 512])
        U = sb("U", [128, 8, 512])
        wr = [sb(f"wr{i}", [128, SLOTW]) for i in range(SLOTS)]
        BIG = sb("BIG", [128, 24000])
        CA = sb("CA", [128, NC2])
        CC = sb("CC", [128, NC0])
        K = sb("K", [128, NCOL])
        M = sb("M", [128, 2, 2, 72])
        M2 = sb("M2", [128, 48])
        SC = sb("SC", [128, 3, 8])
        AB = sb("AB", [128, 2, 8])
        GT = sb("GT", [128, 2, 8])
        RS = sb("RS", [128, 512])
        st = sb("st", [128, 64])
        eps = sb("eps", [128, 1])
        acc = Pool([sb(f"acc{i}", [128, 512]) for i in range(2)])
        rot = Pool([sb(f"rot{i}", [128, 512]) for i in range(4)])
        ps = Pool([ctx.enter_context(nc.psum_tensor(f"ps{i}", [128, 512], F32)) for i in range(8)])

        off = [0]

        def big(n, *shape):
            a = BIG[:, off[0]:off[0] + n]
            off[0] += n
            if len(shape) == 2:
                a = a.rearrange("p (a b) -> p a b", b=shape[1])
            elif len(shape) == 3:
                a = a.rearrange("p (a b c) -> p a b c", b=shape[1], c=shape[2])
            elif len(shape) == 4:
                a = a.rearrange("p (a b c d) -> p a b c d", b=shape[1], c=shape[2], d=shape[3])
            return a

        def col(k, i=0, n=None):
            o, w = COLS[k]
            return K[:, o + i:o + (w if n is None else i + n)]

        ident, ones, bones = CC[:, 0:128], CC[:, 128:256], CC[:, 256:384]

        wn = [0, 0]
        wrel = [None] * SLOTS
        wtok = []

        def load(width):
            n = wn[0]
            wn[0] += 1
            s = n % SLOTS
            assert n < SLOTS or wrel[s] is not None, n
            S.dma(nc.sync.dma_start, wr[s][:, 0:width],
                  ws[wn[1]:wn[1] + 128 * width].rearrange("(p w) -> p w", p=128), s_w[s],
                  w=[wrel[s]] if n >= SLOTS else [])
            wrel[s] = None
            wn[1] += 128 * width
            wtok.append((s_w[s], 16 * (n // SLOTS + 1)))
            return n

        def weight(key, width):
            plan.append(key)
            n = load(width)
            return wr[n % SLOTS][:, 0:width], wtok[n], n % SLOTS

        def used(slot, *toks):
            wrel[slot] = list(toks)

        def group(out, pairs, w=(), start=True, stop=True):
            for n, (l, r) in enumerate(pairs):
                t = P(pe.matmul, out, l, r, start=(start and n == 0), stop=(stop and n == len(pairs) - 1),
                      skip_group_check=True, w=w if n == 0 else (), sig=(n == len(pairs) - 1))
            return t

        def transp(out, in_, w=(), sig=True):
            k = in_.shape[0]
            return P(pe.transpose, out, in_, CC[0:k, 0:k], w=w, sig=sig)

        S.dma(nc.sync.dma_start, K[:, :], cols_d, s_c)
        S.dma(nc.sync.dma_start, CC[:, :], c0_d, s_c)
        c_tok = (s_c, 16 * 4)
        ctok0 = c_tok
        S.dma(nc.sync.dma_start, CA[:, 0:NC1], c1_d, s_c)
        S.dma(nc.sync.dma_start, X[:, :, :].rearrange("p a b -> p (a b)"),
              ws[0:128 * 4096].rearrange("(p w) -> p w", p=128), s_c)
        wn[1] = 128 * 4096
        plan.append(("x",))

        V(vec.memset, eps[:, :], EPS)
        for i, k in enumerate(("c", "cx", "c2")):
            sc_tok = A(act.activation, SC[:, i, :], col(k), ACT.Silu, w=[c_tok])
        V.wait(c_tok)
        P.wait(c_tok)
        x_tok = c_tok

        def mod_steps(key, conds, dst, bias):
            wc, wt, slot = weight(key, 4096)
            wc = wc.rearrange("p (k n) -> p k n", k=8)
            for c in conds:
                a, r, ab = acc.take()
                V(vec.tensor_scalar, a[:, :], wc[:, 0, :], SC[:, c, 0:1], None, ALU.mult, w=[wt, sc_tok] + r)
                yield
                for k in range(1, 8):
                    t = V(vec.scalar_tensor_tensor, out=a[:, :], in0=wc[:, k, :], scalar=SC[:, c, k:k + 1],
                          in1=a[:, :], op0=ALU.mult, op1=ALU.add)
                    if k % 4 == 3:
                        if k == 7 and c == conds[-1]:
                            used(slot, t)
                        yield
                b, br, bi = ps.take()
                for q in range(4):
                    t = P(pe.matmul, b[:, q:q + 1], a[:, q * 128:q * 128 + 128], ones[:, 0:1], start=True, stop=True,
                          skip_group_check=True, w=[t] + br if q == 0 else (), sig=q == 3)
                acc.give(ab, t)
                t = V(vec.tensor_tensor, dst(c), b[:, 0:4], bias, ALU.add, w=[t])
                ps.give(bi, t)
                yield

        def layer_mod(l, lo, hi):
            for ch in range(lo, hi):
                yield from mod_steps(("wmod", l, ch), [0, 1], lambda c, ch=ch: M[:, l, c, ch * 4:ch * 4 + 4],
                                     col(f"bmod{l}", ch * 4, 4))

        def ada_mod():
            for ch in range(12):
                yield from mod_steps(("ada", ch), [2], lambda c, ch=ch: M2[:, ch * 4:ch * 4 + 4],
                                     col("ada", ch * 4, 4))

        fill = [None]

        def filler(n=1):
            for _ in range(n):
                if fill[0] is not None:
                    try:
                        next(fill[0])
                    except StopIteration:
                        fill[0] = None

        def drain_fill():
            while fill[0] is not None:
                filler()

        u_rel = [None]

        def norm(gcol, scale, shift, segs):
            T = segs[-1][1]
            b, br, bi = ps.take()
            for k in range(8):
                q, r, qi = rot.take()
                t = A(act.activation, q[:, 0:T], X[:, k, 0:T], ACT.Square, w=[x_tok] + r)
                t = P(pe.matmul, b[:, 0:T], ones, q[:, 0:T], start=k == 0, stop=k == 7, w=[t] + br)
                rot.give(qi, t)
            q, r, qi = rot.take()
            t = A(act.activation, q[:, 0:T], b[:, 0:T], ACT.Sqrt, scale=1.0 / D, bias=eps[:, :], w=[t] + r)
            ps.give(bi, t)
            V(vec.reciprocal, RS[:, 0:T], q[:, 0:T], w=[t])
            rot.give(qi, V.last)
            nseg = len(segs)
            if scale is not None:
                V(vec.scalar_tensor_tensor, out=AB[:, 0:nseg, :], in0=scale, scalar=1.0,
                  in1=gcol.unsqueeze(1).to_broadcast([128, nseg, 8]), op0=ALU.add, op1=ALU.mult, w=[u_rel[0]])
            for k in range(8):
                for c, (lo, hi) in enumerate(segs):
                    s = AB[:, c, k:k + 1] if scale is not None else gcol[:, k:k + 1]
                    t = V(vec.scalar_tensor_tensor, out=U[:, k, lo:hi], in0=X[:, k, lo:hi], scalar=s,
                          in1=RS[:, lo:hi], op0=ALU.mult, op1=ALU.mult, w=[u_rel[0]])
                    if shift is not None:
                        t = A(act.activation, U[:, k, lo:hi], U[:, k, lo:hi], ACT.Identity,
                              bias=shift[:, c, k:k + 1], w=[t])
            return t

        def add_x(j, b, gate, segs, w):
            for c, (lo, hi) in enumerate(segs):
                t = V(vec.scalar_tensor_tensor, out=X[:, j, lo:hi], in0=b[:, lo:hi], scalar=gate[:, c, j:j + 1],
                      in1=X[:, j, lo:hi], op0=ALU.mult, op1=ALU.add, w=w)
            return t

        def ffn(l, f, segs, per=4):
            nonlocal x_tok
            T = segs[-1][1]
            n = len(segs)
            i = 2 * f
            ml = M[:, l, 0:n, :]
            ut = norm(col(f"g{l}", 8 * i, 8), ml[:, :, (3 * i + 1) * 8:(3 * i + 2) * 8],
                      ml[:, :, 3 * i * 8:(3 * i + 1) * 8], segs)
            off[0] = 0
            h = big(22 * 512, 22, 512)
            for c in range(11):
                wc, wt, slot = weight(("fin", l, f, c), 4096)
                wc = wc.rearrange("p (k n) -> p k n", k=8)
                for q in range(2):
                    a, ar, ai = ps.take()
                    group(a[:, 0:T], [(wc[:, k, q * 128:q * 128 + 128], U[:, k, 0:T]) for k in range(8)],
                          w=[wt, ut] + ar)
                    s, sr, si = rot.take()
                    t = A(act.activation, s[:, 0:T], a[:, 0:T], ACT.Silu, w=[P.last] + sr)
                    ps.give(ai, t)
                    b, br, bi = ps.take()
                    tp = group(b[:, 0:T], [(wc[:, k, 256 + q * 128:384 + q * 128], U[:, k, 0:T]) for k in range(8)],
                               w=br)
                    ht = V(vec.tensor_tensor, h[:, 2 * c + q, 0:T], b[:, 0:T], s[:, 0:T], ALU.mult, w=[t, tp])
                    ps.give(bi, ht)
                    rot.give(si, ht)
                    filler(per)
                used(slot, P.last)
            u_rel[0] = P.last
            V(vec.tensor_scalar, GT[:, 0:n, :], ml[:, :, (3 * i + 2) * 8:(3 * i + 3) * 8], 0.5, None, ALU.mult)
            for j in range(8):
                wc, wt, slot = weight(("fout", l, f, j), 22 * 128)
                wc = wc.rearrange("p (k n) -> p k n", k=22)
                b, br, bi = ps.take()
                tp = group(b[:, 0:T], [(wc[:, k, :], h[:, k, 0:T]) for k in range(22)], w=[wt, ht] + br)
                used(slot, tp)
                filler(per)
                t = add_x(j, b, GT, segs, [tp])
                ps.give(bi, t)
            x_tok = t

        LAT = [(0, 256)]
        BOTH = [(0, 256), (256, 512)]

        def mixer(l):
            nonlocal x_tok
            last = l == 1
            lam_init = 0.8 - 0.6 * math.exp(-0.3 * l)
            ml = M[:, l, :, :]
            ut = norm(col(f"g{l}", 8, 8), ml[:, :, 32:40], ml[:, :, 24:32], BOTH)
            qT_ = 256 if last else 512
            segs = LAT if last else BOTH
            off[0] = 0
            qT = big(4096, 8, 512)
            kT = big(4096, 8, 512)
            Vt = big(4096, 4, 1024)
            fT = big(2048, 4, 512)
            PA = [big(512) for _ in range(8)]
            aT = [big(1024, 4, 256) for _ in range(2)]
            cos, sin, rm = CA[:, 128:384], CA[:, 384:640], CA[:, 0:128]
            ls = st[:, 0:2]
            o = COLS[f"lam{l}"][0]
            V(vec.tensor_tensor, st[:, 0:2], K[:, o:o + 4:2], K[:, o + 1:o + 4:2], ALU.mult)
            b, br, bi = ps.take()
            t = group(b[:, 0:2], [(ones, ls)], w=[V.last] + br)
            t = A(act.activation, st[:, 2:4], b[:, 0:2], ACT.Exp, w=[t])
            ps.give(bi, t)
            V(vec.tensor_tensor, st[:, 4:5], st[:, 2:3], st[:, 3:4], ALU.subtract, w=[t])
            V(vec.tensor_scalar, st[:, 5:6], st[:, 4:5], lam_init, -1.0, ALU.add, ALU.mult)
            nlam = st[:, 5:6]
            V(vec.tensor_scalar, st[:, 6:7], col(f"sub{l}"), 1 - lam_init, None, ALU.mult)
            subg = st[:, 6:7]
            for qk, dst, T in ((0, qT, qT_), (1, kT, 512)):
                for c in range(2):
                    wc, wt, slot = weight(("win", l, qk * 1024 + c * 512, 512), 4096)
                    wc = wc.rearrange("p (k n) -> p k n", k=8)
                    for q in range(4):
                        h = 4 * c + q
                        b, br, bi = ps.take()
                        t = group(b[:, 0:T], [(wc[:, k, q * 128:q * 128 + 128], U[:, k, 0:T]) for k in range(8)],
                                  w=[wt, ut] + br)
                        r, rr, ri = rot.take()
                        t = A(act.copy, r[:, 0:256], b[:, 0:256], w=[t] + rr)
                        if T == 512:
                            t = A(act.copy, dst[:, h, 256:512], b[:, 256:512])
                        ps.give(bi, t)
                        b, br, bi = ps.take()
                        tp = group(b[:, 0:256], [(rm, r[:, 0:256])], w=[t] + br)
                        V(vec.tensor_tensor, dst[:, h, 0:256], r[:, 0:256], cos, ALU.mult, w=[t])
                        V(vec.tensor_tensor, r[:, 256:512], b[:, 0:256], sin, ALU.mult, w=[tp])
                        ps.give(bi, V.last)
                        V(vec.tensor_tensor, dst[:, h, 0:256], dst[:, h, 0:256], r[:, 256:512], ALU.add)
                        rot.give(ri, V.last)
                    used(slot, P.last)
                    filler(4)
            qk_tok = V.last
            for c in range(2):
                wc, wt, slot = weight(("win", l, 2048 + c * 512, 512), 4096)
                wc = wc.rearrange("p (k n) -> p k n", k=8)
                for tt in range(4):
                    b, br, bi = ps.take()
                    t = group(b[:, :], [(U[:, k, tt * 128:tt * 128 + 128], wc[:, k, :]) for k in range(8)],
                              w=[wt] + br)
                    t = A(act.copy, Vt[:, tt, c * 512:c * 512 + 512], b[:, :], w=[t])
                    ps.give(bi, t)
                used(slot, P.last)
                filler(4)
            v_tok = A.last
            wc, wt, slot = weight(("win", l, 3072, 512), 4096)
            wc = wc.rearrange("p (k n) -> p k n", k=8)
            for q in range(4):
                b, br, bi = ps.take()
                t = group(b[:, 0:qT_], [(wc[:, k, q * 128:q * 128 + 128], U[:, k, 0:qT_]) for k in range(8)],
                          w=[wt] + br)
                t = A(act.copy, fT[:, q, 0:qT_], b[:, 0:qT_], w=[t])
                ps.give(bi, t)
            used(slot, P.last)
            f_tok = A.last
            jobs = [(h, s) for h in range(8) for s in range(len(segs))]
            pa_rel = [[None] for _ in range(8)]
            at_rel = [[None], [None]]
            state = {}

            def scores(n):
                h, s = jobs[n]
                klo, khi = (0, 512) if s == 0 else (256, 512)
                nk = khi - klo
                for qb in range(2):
                    for c in range(2):
                        b, br, bi = ps.take()
                        q0 = s * 256 + qb * 128
                        tp = group(b[:, 0:nk], [(qT[64 * c:64 * c + 64, h, q0:q0 + 128],
                                                 kT[64 * c:64 * c + 64, h, klo:khi])], w=[qk_tok] + br)
                        pi = (n % 2) * 4 + qb * 2 + c
                        z = 16 + (n % 2) * 16 + qb * 8 + c
                        V(vec.tensor_reduce, st[:, z:z + 1], b[:, 0:nk], AX.X, ALU.max, w=[tp])
                        V(vec.tensor_scalar, st[:, z + 2:z + 3], st[:, z:z + 1], -0.125, None, ALU.mult)
                        t = A(act.activation, PA[pi][:, 0:nk], b[:, 0:nk], ACT.Exp, bias=st[:, z + 2:z + 3],
                              scale=0.125, accum_out=st[:, z + 4:z + 5], w=[V.last] + pa_rel[pi])
                        ps.give(bi, t)
                for qb in range(2):
                    z = 16 + (n % 2) * 16 + qb * 8
                    p0, p1 = PA[(n % 2) * 4 + qb * 2], PA[(n % 2) * 4 + qb * 2 + 1]
                    V(vec.reciprocal, st[:, z:z + 2], st[:, z + 4:z + 6], w=[t])
                    V(vec.tensor_tensor, st[:, z + 6:z + 7], st[:, z + 1:z + 2], nlam, ALU.mult)
                    V(vec.tensor_scalar, p1[:, 0:nk], p1[:, 0:nk], st[:, z + 6:z + 7], None, ALU.mult)
                    V(vec.scalar_tensor_tensor, out=p0[:, 0:nk], in0=p0[:, 0:nk], scalar=st[:, z:z + 1],
                      in1=p1[:, 0:nk], op0=ALU.mult, op1=ALU.add)
                state[n] = V.last

            def turn(n):
                h, s = jobs[n]
                kt0, nkt = (0, 4) if s == 0 else (2, 2)
                for qb in range(2):
                    pi = (n % 2) * 4 + qb * 2
                    b, br, bi = ps.take()
                    for k in range(nkt):
                        tp = transp(b[:, k * 128:k * 128 + 128], PA[pi][:, k * 128:k * 128 + 128],
                                    w=[state[n]] + br, sig=k == nkt - 1)
                    pa_rel[pi] = [tp]
                    pa_rel[pi + 1] = [state[n]]
                    t = A(act.copy, aT[n % 2][:, 0:nkt, qb * 128:qb * 128 + 128],
                          b[:, 0:nkt * 128].rearrange("p (a b) -> p a b", b=128), w=[tp] + at_rel[n % 2])
                    ps.give(bi, t)
                b, br, bi = ps.take()
                tp = group(b[:, 0:256], [(Vt[:, kt0 + k, h * 128:h * 128 + 128], aT[n % 2][:, k, :])
                                         for k in range(nkt)], w=[t, v_tok] + br)
                at_rel[n % 2] = [tp]
                t = A(act.copy, qT[:, h, s * 256:s * 256 + 256], b[:, 0:256], w=[tp])
                ps.give(bi, t)

            for n in range(len(jobs)):
                scores(n)
                if n:
                    turn(n - 1)
            turn(len(jobs) - 1)
            at_tok = A.last
            for h in range(8):
                q, r, qi = rot.take()
                t = A(act.activation, q[:, 0:qT_], qT[:, h, 0:qT_], ACT.Square, w=r)
                b, br, bi = ps.take()
                tp = group(b[:, 0:qT_], [(ones, q[:, 0:qT_])], w=[t] + br)
                t = A(act.activation, q[:, 0:qT_], b[:, 0:qT_], ACT.Sqrt, scale=1.0 / 128, bias=eps[:, :], w=[tp])
                ps.give(bi, t)
                V(vec.reciprocal, q[:, 0:qT_], q[:, 0:qT_], w=[t])
                an_tok = V(vec.scalar_tensor_tensor, out=qT[:, h, 0:qT_], in0=qT[:, h, 0:qT_], scalar=subg,
                           in1=q[:, 0:qT_], op0=ALU.mult, op1=ALU.mult)
                rot.give(qi, an_tok)
            frT = Vt[:, 0:2, :].rearrange("p a (b t) -> p (a b) t", t=512)
            fr_free = P.last
            cs = CA[:, 896:1408].rearrange("p (a b) -> p a b", b=256)
            ss = CA[:, 1408:1920].rearrange("p (a b) -> p a b", b=256)
            for s in range(len(segs)):
                for g in range(4):
                    b, br, bi = ps.take()
                    for tt in range(2):
                        tp = group(b[:, tt * 256:tt * 256 + 256],
                                   [(fT[:, g, s * 256 + tt * 128:s * 256 + tt * 128 + 128], CA[:, 640:896])],
                                   w=[f_tok] + br)
                    r, rr, ri = rot.take()
                    t = A(act.copy, r[:, :], b[:, :], w=[tp] + rr)
                    ps.give(bi, t)
                    b, br, bi = ps.take()
                    tp = group(b[:, 0:256], [(r[:, 0:128], cs[:, 0, :]), (r[:, 128:256], ss[:, 0, :]),
                                             (r[:, 256:384], cs[:, 1, :]), (r[:, 384:512], ss[:, 1, :])],
                               w=[t] + br)
                    rot.give(ri, tp)
                    fr_tok = A(act.copy, frT[:, g, s * 256:s * 256 + 256], b[:, 0:256], w=[tp, fr_free])
                    ps.give(bi, fr_tok)
            mg = kT
            T = qT_
            for jj in range(4):
                w1, t1, s1 = weight(("wgate", l, jj), 4096)
                w2, t2, s2 = weight(("wbr", l, jj), 3072)
                w1 = w1.rearrange("p (k n) -> p k n", k=8)
                w2 = w2.rearrange("p (k n) -> p k n", k=12)
                for q in range(2):
                    j = 2 * jj + q
                    cq = slice(q * 128, q * 128 + 128)
                    b, br, bi = ps.take()
                    t = group(b[:, 0:T], [(w1[:, k, cq], U[:, k, 0:T]) for k in range(8)], w=[t1] + br)
                    ga, gr, gi = rot.take()
                    t = A(act.activation, ga[:, 0:T], b[:, 0:T], ACT.Sigmoid, bias=col(f"bg{l}", j, 1), w=[t] + gr)
                    ps.give(bi, t)
                    b, br, bi = ps.take()
                    t = group(b[:, 0:T], [(w1[:, k, 256 + q * 128:384 + q * 128], U[:, k, 0:T]) for k in range(8)],
                              w=br)
                    gf, gr, gj = rot.take()
                    t = A(act.activation, gf[:, 0:T], b[:, 0:T], ACT.Sigmoid, bias=col(f"bg{l}", 8 + j, 1),
                          w=[t] + gr)
                    ps.give(bi, t)
                    b, br, bi = ps.take()
                    tp = group(b[:, 0:T], [(w2[:, k, cq], qT[:, k, 0:T]) for k in range(8)], w=[t2, an_tok] + br)
                    V(vec.tensor_tensor, ga[:, 0:T], b[:, 0:T], ga[:, 0:T], ALU.mult, w=[tp, t])
                    ps.give(bi, V.last)
                    b, br, bi = ps.take()
                    tp = group(b[:, 0:T], [(w2[:, 8 + k, cq], frT[:, k, 0:T]) for k in range(4)], w=[fr_tok] + br)
                    V(vec.tensor_tensor, gf[:, 0:T], b[:, 0:T], gf[:, 0:T], ALU.mult, w=[tp])
                    ps.give(bi, V.last)
                    m_tok = V(vec.tensor_tensor, mg[:, j, 0:T], ga[:, 0:T], gf[:, 0:T], ALU.add)
                    rot.give(gi, m_tok)
                    rot.give(gj, m_tok)
                    filler(2)
                used(s1, P.last)
                used(s2, P.last)
            u_rel[0] = P.last
            for c in range(2):
                wc, wt, slot = weight(("wo", l, c), 4096)
                wc = wc.rearrange("p (k n) -> p k n", k=8)
                for q in range(4):
                    b, br, bi = ps.take()
                    tp = group(b[:, 0:T], [(wc[:, k, q * 128:q * 128 + 128], mg[:, k, 0:T]) for k in range(8)],
                               w=[wt, m_tok] + br)
                    t = add_x(4 * c + q, b, ml[:, :, 40:48], segs, [tp])
                    ps.give(bi, t)
                used(slot, P.last)
            x_tok = t

        fill[0] = layer_mod(0, 0, 6)
        drain_fill()
        if STOP > 0:
            fill[0] = layer_mod(0, 6, 18)
            ffn(0, 0, BOTH)
            drain_fill()
        if STOP > 1:
            mixer(0)
        if STOP > 2:
            fill[0] = layer_mod(1, 0, 18)
            ffn(0, 1, BOTH, per=5)
            drain_fill()
            fill[0] = ada_mod()
            ffn(1, 0, BOTH)
            drain_fill()
            mixer(1)
            ffn(1, 1, LAT)
            norm(col("fin"), None, None, LAT)
            for k in range(8):
                x_tok = V(vec.tensor_copy, X[:, k, 0:256], U[:, k, 0:256], w=[A.last])
            u_rel[0] = P.last

        if STOP > 3:
            S.dma(nc.sync.dma_start, CA[:, :], c2_d, s_c2, w=[P.last, V.last])
            c2t = (s_c2, 16)
            V.wait(c2t)
            P.wait(c2t)
            off[0] = 0
            qf = big(1024, 4, 256)
            kf = big(1024, 4, 256)
            ktok = big(1024, 2, 512)
            vtok = big(2048, 2, 1024)
            zf = big(1024, 4, 256)
            intra = big(4096, 8, 512)
            LT = big(2048, 4, 512)
            TA = big(2048, 4, 512)
            TT = big(2048, 4, 512)
            UU = [big(512) for _ in range(2)]
            uv = big(2048, 2, 2, 512)
            SP = big(2048, 4, 512)
            KD = [a_[:, :] for a_ in acc.tiles]
            kb = SP.rearrange("p a (b t) -> p (a b) t", t=256)
            oaT = big(1024, 4, 256)
            wT = X[:, :, 256:512]
            qg = U[:, :, 256:512]
            neg = CA[:, 0:256].rearrange("p (d i) -> p d i", d=2)
            strict = CA[:, 256:512].rearrange("p (d i) -> p d i", d=2)
            lvl = CA[:, 512:2048].rearrange("p (l d i) -> p l d i", l=6, d=2)
            CT = big(640, 2, 5, 64)
            EX = big(32, 8, 4)
            XP = Pool([big(260) for i in range(2)])
            R2 = big(256)[0:64, :]
            assert off[0] <= 24000, off[0]
            for xp in XP.tiles:
                V(vec.memset, xp[:, 0:2], 0.0)
                V(vec.memset, xp[:, 258:260], 0.0)
            rows8 = uv.rearrange("p a b c -> p (a b c)")[0:64, :].rearrange("p (r t) -> p r t", t=256)
            R = [rows8[:, i, :] for i in range(2)] + [R2] + [rows8[:, i, :] for i in range(2, 8)] \
                + [RS[0:64, 0:256], RS[0:64, 256:512]]
            m2 = M2[:, :].rearrange("p (a c k) -> p a c k", c=1, k=8)
            ut = norm(col("nmix"), m2[:, 1], m2[:, 0], LAT)

            def conv_tile(wc, q, wt, ck, j, dst, head_norm, scl):
                b, br, bi = ps.take()
                t = group(b[:, 0:256], [(wc[:, k, q * 128:q * 128 + 128], U[:, k, 0:256]) for k in range(8)],
                          w=[wt, ut] + br)
                xp, xr, xi = XP.take()
                t = A(act.copy, xp[:, 2:258], b[:, 0:256], w=[t] + xr)
                ps.give(bi, t)
                r, rr, ri = rot.take()
                V(vec.tensor_scalar, r[:, 0:256], xp[:, 0:256], col(ck, j * 5, 1), None, ALU.mult, w=[t] + rr)
                for i in range(1, 5):
                    t = V(vec.scalar_tensor_tensor, out=r[:, 0:256], in0=xp[:, i:i + 256],
                          scalar=col(ck, j * 5 + i, 1), in1=r[:, 0:256], op0=ALU.mult, op1=ALU.add)
                XP.give(xi, t)
                t = A(act.activation, dst, r[:, 0:256], ACT.Silu, w=[t])
                if head_norm:
                    t = A(act.activation, r[:, 0:256], dst, ACT.Square)
                    b, br, bi = ps.take()
                    t = group(b[:, 0:256], [(bones, r[:, 0:256])], w=[t] + br)
                    t = A(act.activation, r[:, 256:512], b[:, 0:256], ACT.Sqrt, bias=eps[:, :], w=[t])
                    ps.give(bi, t)
                    V(vec.reciprocal, r[:, 256:512], r[:, 256:512], w=[t])
                    t = V(vec.scalar_tensor_tensor, out=dst, in0=dst, scalar=scl, in1=r[:, 256:512],
                          op0=ALU.mult, op1=ALU.mult)
                elif scl != 1.0:
                    t = V(vec.tensor_scalar, dst, dst, scl, None, ALU.mult, w=[t])
                rot.give(ri, t)
                return t

            def to_tokens(src, dst, w):
                for tt in range(2):
                    b, br, bi = ps.take()
                    for f in range(4):
                        tp = transp(b[:, f * 128:f * 128 + 128], src[:, f, tt * 128:tt * 128 + 128],
                                    w=w + br, sig=f == 3)
                    t = A(act.copy, dst(tt), b[:, :] if dst(tt).free_size() == 512 and len(dst(tt).shape) == 2
                          else b[:, :].rearrange("p (h e) -> p h e", e=64), w=[tp])
                    ps.give(bi, t)
                return t

            def gate_rows(kb_, dst, wc, wt):
                b, br, bi = ps.take()
                t = group(b[0:64, 0:256], [(wc[:, k, kb_ * 64:kb_ * 64 + 64], U[:, k, 0:256]) for k in range(8)],
                          w=[wt, ut] + br)
                return b[0:64, 0:256], t, bi

            def softplus_rows(dst, src, tmp):
                V(vec.tensor_scalar, tmp, src, -1.0, None, ALU.mult)
                t = V(vec.tensor_tensor, tmp, tmp, src, ALU.min)
                A(act.activation, tmp, tmp, ACT.Exp, w=[t])
                t = A(act.activation, tmp, tmp, ACT.Ln, bias=1.0)
                V(vec.scalar_tensor_tensor, out=dst, in0=src, scalar=0.0, in1=tmp, op0=ALU.max, op1=ALU.add, w=[t])

            def scan(dst, src, op):
                for dr in range(2):
                    p = slice(32 * dr, 32 * dr + 32)
                    for n in range(4):
                        s, d_ = src[p, 64 * n:64 * n + 64], dst[p, 64 * n:64 * n + 64]
                        if dr:
                            s, d_ = s[:, ::-1], d_[:, ::-1]
                        if op is ALU.add:
                            V(vec.tensor_tensor_scan, d_, s, s, 0.0, ALU.add, ALU.bypass)
                        else:
                            V(vec.tensor_tensor_scan, d_, s, s, -3e38, ALU.max, ALU.max)

            def last_of(row, dr):
                r = row[32 * dr:32 * dr + 32, :].rearrange("p (n l) -> p n l", l=64)
                return r[:, :, 63:64] if dr == 0 else r[:, :, 0:1]

            def chunks(row, dr):
                return row[32 * dr:32 * dr + 32, :].rearrange("p (n l) -> p n l", l=64)

            def to_cols(rows, w):
                for tt in range(2):
                    b, br, bi = ps.take()
                    for i, r in enumerate(rows):
                        tp = transp(b[:, i * 64:i * 64 + 64], r[:, tt * 128:tt * 128 + 128], w=w + br,
                                    sig=i == len(rows) - 1)
                    t = A(act.copy, CT[:, tt, 0:len(rows), :],
                          b[:, 0:64 * len(rows)].rearrange("p (a b) -> p a b", b=64), w=[tp])
                    ps.give(bi, t)
                return t

            def row_all(out, row, dr, h, w, sig=True):
                r = 32 * dr + h
                return P(pe.matmul, out, CC[0:64, r:r + 1].to_broadcast([64, 128]), row, start=True, stop=True,
                         skip_group_check=True, w=w, sig=sig)

            def row_pair(out, row, dr, f, w, sig=True):
                r = 32 * dr + 2 * f
                P(pe.matmul, out[0:64], CC[0:64, r:r + 1].to_broadcast([64, 64]), row, start=True,
                  stop=True, skip_group_check=True, w=w, sig=False)
                return P(pe.matmul, out[64:128], CC[0:64, r + 1:r + 2].to_broadcast([64, 64]), row, start=True,
                         stop=True, skip_group_check=True, sig=sig)

            def decay(h, row, ci, w):
                b, br, bi = ps.take()
                for dr in range(2):
                    tp = row_all(b[:, dr * 256:dr * 256 + 256], row, dr, h, w + br, sig=dr == 1)
                r, rr, ri = rot.take()
                for dr in range(2):
                    for tt in range(2):
                        o = dr * 256 + tt * 128
                        t = V(vec.scalar_tensor_tensor, out=r[:, o:o + 128], in0=b[:, o:o + 128],
                              scalar=CT[:, tt, ci, 32 * dr + h:32 * dr + h + 1], in1=neg[:, dr, :],
                              op0=ALU.subtract, op1=ALU.add, w=[tp] + rr)
                ps.give(bi, t)
                t = A(act.activation, r[:, :], r[:, :], ACT.Exp, w=[t])
                return r, t, ri

            def scaled_pairs(dst, src, row, w, wd):
                for f in range(4):
                    b, br, bi = ps.take()
                    for dr in range(2):
                        tp = row_pair(b[:, dr * 256:dr * 256 + 256], row, dr, f, w + br, sig=dr == 1)
                    for dr in range(2):
                        t = V(vec.tensor_tensor, dst[:, 2 * f + dr, :], b[:, dr * 256:dr * 256 + 256], src[:, f, :],
                              ALU.mult, w=[tp] + wd)
                    ps.give(bi, t)
                return t

            for c, (dst, hn, scl) in enumerate(((qf, True, 0.125), (kf, True, 1.0), (None, False, 1.0))):
                wc, wt, slot = weight(("win2", c * 512, 512), 4096)
                wc = wc.rearrange("p (k n) -> p k n", k=8)
                d_ = zf if dst is None else dst
                for q in range(4):
                    t = conv_tile(wc, q, wt, "cva", c * 4 + q, d_[:, q, :], hn, scl)
                used(slot, P.last)
                if c == 1:
                    to_tokens(kf, lambda tt: ktok[:, tt, :], [t])
                if c == 2:
                    to_tokens(zf, lambda tt: vtok[:, tt, 0:512], [t])
            zt_rel = P.last
            wc, wt, slot = weight(("win2", 1536, 512), 4096)
            wc = wc.rearrange("p (k n) -> p k n", k=8)
            for q in range(4):
                b, br, bi = ps.take()
                t = group(b[:, 0:256], [(wc[:, k, q * 128:q * 128 + 128], U[:, k, 0:256]) for k in range(8)],
                          w=[wt] + br)
                t = A(act.activation, zf[:, q, :], b[:, 0:256], ACT.Silu, w=[t, zt_rel])
                ps.give(bi, t)
            used(slot, P.last)
            gw, gt, gslot = weight(("gates2",), 2048)
            gw = gw.rearrange("p (k n) -> p k n", k=8)
            rw = COLS["rows"][0]
            rows = [K[0:64, rw + i:rw + i + 1] for i in range(4)]
            bg, t, bi = gate_rows(0, None, gw, gt)
            V(vec.tensor_scalar, R[0], bg, rows[1], None, ALU.add, w=[t])
            ps.give(bi, V.last)
            bg, t, bi = gate_rows(1, None, gw, gt)
            t = A(act.activation, R[1], bg, ACT.Sigmoid, w=[t])
            ps.give(bi, t)
            for i, dd in ((2, R[9]), (3, R[10])):
                bg, t, bi = gate_rows(i, None, gw, gt)
                V(vec.tensor_scalar, dd, bg, rows[i], None, ALU.add, w=[t])
                ps.give(bi, V.last)
            used(gslot, P.last)
            softplus_rows(R[2], R[0], R[3])
            t = A(act.activation, st[0:64, 8:9], rows[0], ACT.Exp)
            V(vec.tensor_scalar, R[0], R[2], st[0:64, 8:9], -1.0, ALU.mult, ALU.mult, w=[t])
            scan(R[2], R[0], ALU.add)
            for dr in range(2):
                V(vec.tensor_tensor, chunks(R[3], dr), last_of(R[2], dr).to_broadcast([32, 4, 64]), chunks(R[2], dr),
                  ALU.subtract)
            A(act.activation, R[4], R[2], ACT.Exp, w=[V.last])
            t = A(act.activation, R[3], R[3], ACT.Exp)
            V(vec.tensor_tensor, R[5], R[1], R[4], ALU.mult, w=[t])
            r_tok = V.last
            ct_tok = to_cols([R[2], R[1], R[5], R[3]], [A.last, V.last])
            V.wait(ct_tok)

            qg_tok = scaled_pairs(qg, qf, R[4], [r_tok, t], [u_rel[0]])
            kb_tok = scaled_pairs(kb, kf, R[1], [r_tok, t], [])
            b, br, bi = ps.take()
            V(vec.tensor_copy, R[6][:, 0:4], R[4][:, 0:256:64])
            V(vec.tensor_copy, R[6][0:32, 0:4], R[4][0:32, 63:256:64])
            for dr in range(2):
                for f in range(4):
                    o = (dr * 4 + f) * 4
                    tp = row_pair(b[:, o:o + 4], R[6][:, 0:4], dr, f, [V.last] + br, sig=dr == 1 and f == 3)
            ex_tok = V(vec.tensor_copy, EX[:, :, :], b[:, 0:32].rearrange("p (a n) -> p a n", n=4), w=[tp])
            ps.give(bi, ex_tok)

            def idx(h):
                return h // 2, slice(64 * (h % 2), 64 * (h % 2) + 64)

            for grp in range(2):
                ht = {}
                for hh in range(4):
                    h = grp * 4 + hh
                    f, pp = idx(h)
                    dt_, dtt, ri = decay(h, R[2], 0, [r_tok])
                    bq, br, bqi = ps.take()
                    for tt in range(2):
                        tk = slice(tt * 128, tt * 128 + 128)
                        tp = P(pe.matmul, bq[:, tk], kf[pp, f, tk], qf[pp, f, tk], start=True, stop=True,
                               skip_group_check=True, w=[qg_tok, kb_tok] + br, sig=tt == 1)
                    for dr in range(2):
                        V(vec.tensor_tensor, intra[:, h, dr * 256:dr * 256 + 256], bq[:, 0:256],
                          dt_[:, dr * 256:dr * 256 + 256], ALU.mult, w=[tp, dtt])
                    ps.give(bqi, V.last)
                    bk, br, bki = ps.take()
                    for dr in range(2):
                        for tt in range(2):
                            tk = slice(tt * 128, tt * 128 + 128)
                            tp = P(pe.matmul, bk[:, dr * 256 + tt * 128:dr * 256 + tt * 128 + 128], kf[pp, f, tk],
                                   kb[pp, 2 * f + dr, tk], start=True, stop=True, skip_group_check=True,
                                   w=br, sig=dr == 1 and tt == 1)
                    V(vec.tensor_tensor, dt_[:, :], bk[:, :], dt_[:, :], ALU.mult, w=[tp])
                    ps.give(bki, V.last)
                    lt = LT[:, hh, :].rearrange("p (d t i) -> p d t i", d=2, t=2)
                    for dr in range(2):
                        V(vec.tensor_tensor, lt[:, dr], dt_[:, dr * 256:dr * 256 + 256].rearrange(
                            "p (t i) -> p t i", t=2), strict[:, dr, :].unsqueeze(1).to_broadcast([128, 2, 128]),
                          ALU.mult, w=[ht.get("lt")])
                    rot.give(ri, V.last)
                    tt4 = TT[:, hh, :].rearrange("p (d t i) -> p d t i", d=2, t=2)
                    for dr in range(2):
                        V(vec.tensor_tensor, tt4[:, dr], lt[:, dr],
                          lvl[:, 0, dr, :].unsqueeze(1).to_broadcast([128, 2, 128]), ALU.mult)
                    V(vec.tensor_tensor, TT[:, hh, :].rearrange("p (a i) -> p a i", i=128),
                      ident.unsqueeze(1).to_broadcast([128, 4, 128]),
                      TT[:, hh, :].rearrange("p (a i) -> p a i", i=128), ALU.subtract)
                    b, br, bi = ps.take()
                    for a in range(4):
                        tp = transp(b[:, a * 128:a * 128 + 128], TT[:, hh, a * 128:a * 128 + 128],
                                    w=[V.last] + br, sig=a == 3)
                    t = A(act.copy, TA[:, hh, :], b[:, :], w=[tp])
                    ps.give(bi, t)
                    ht[hh] = t
                uu_rel = [[None], [None]]
                for lv in range(1, 6):
                    for hh in range(4):
                        r, rr, ri = rot.take()
                        lt = LT[:, hh, :].rearrange("p (d t i) -> p d t i", d=2, t=2)
                        rv = r[:, :].rearrange("p (d t i) -> p d t i", d=2, t=2)
                        for dr in range(2):
                            V(vec.tensor_tensor, rv[:, dr], lt[:, dr],
                              lvl[:, lv, dr, :].unsqueeze(1).to_broadcast([128, 2, 128]), ALU.mult, w=rr)
                        b, br, bi = ps.take()
                        for a in range(4):
                            s_ = slice(a * 128, a * 128 + 128)
                            tp = P(pe.matmul, b[:, s_], r[:, s_], TA[:, hh, s_], start=True, stop=True,
                                   skip_group_check=True, w=[V.last, ht[hh]] + br, sig=a == 3)
                        rot.give(ri, tp)
                        uu = UU[hh % 2]
                        t = A(act.copy, uu, b[:, :], w=[tp] + uu_rel[hh % 2])
                        ps.give(bi, t)
                        b2, br2, bi2 = ps.take()
                        for a in range(4):
                            s_ = slice(a * 128, a * 128 + 128)
                            tp2 = P(pe.matmul, b2[:, s_], uu[:, s_], TT[:, hh, s_], start=True, stop=True,
                                    skip_group_check=True, w=[t] + br2, sig=a == 3)
                        if lv < 5:
                            b, br, bi = ps.take()
                            for a in range(4):
                                s_ = slice(a * 128, a * 128 + 128)
                                tp = P(pe.matmul, b[:, s_], TT[:, hh, s_], uu[:, s_], start=True, stop=True,
                                       skip_group_check=True, w=br, sig=a == 3)
                            V(vec.tensor_tensor, TA[:, hh, :], TA[:, hh, :], b[:, :], ALU.subtract, w=[tp])
                            ps.give(bi, V.last)
                        uu_rel[hh % 2] = [P.last]
                        V(vec.tensor_tensor, TT[:, hh, :], TT[:, hh, :], b2[:, :], ALU.subtract, w=[P.last])
                        ps.give(bi2, V.last)
                        ht[hh] = V.last
                for hh in range(4):
                    h = grp * 4 + hh
                    f, pp = idx(h)
                    r, rr, ri = rot.take()
                    rhs = r[:, :].rearrange("p (x d t e) -> p x d t e", x=2, d=2, t=2)
                    for dr in range(2):
                        c_ = 32 * dr + h
                        for tt in range(2):
                            V(vec.tensor_scalar, rhs[:, 0, dr, tt, :], vtok[:, tt, h * 64:h * 64 + 64],
                              CT[:, tt, 1, c_:c_ + 1], None, ALU.mult, w=rr)
                            V(vec.tensor_scalar, rhs[:, 1, dr, tt, :], ktok[:, tt, h * 64:h * 64 + 64],
                              CT[:, tt, 2, c_:c_ + 1], None, ALU.mult)
                    b, br, bi = ps.take()
                    b2, br2, bi2 = ps.take()
                    for dr in range(2):
                        for tt in range(2):
                            a = dr * 2 + tt
                            s_ = slice(a * 128, a * 128 + 128)
                            P(pe.matmul, b[:, a * 64:a * 64 + 64], TT[:, hh, s_], rhs[:, 0, dr, tt, :], start=True,
                              stop=True, skip_group_check=True, w=[V.last] + br, sig=False)
                            tp = P(pe.matmul, b2[pp, s_], rhs[:, 1, dr, tt, :], TT[:, hh, s_], start=True,
                                   stop=True, skip_group_check=True, w=br2, sig=a == 3)
                    rot.give(ri, tp)
                    t = A(act.copy, uv[:, :, :, h * 64:h * 64 + 64].rearrange("p d t e -> p (d t) e"),
                          b[:, 0:256].rearrange("p (a e) -> p a e", e=64), w=[tp])
                    ps.give(bi, t)
                    t = A(act.copy, wT[pp, 2 * f:2 * f + 2, :],
                          b2[pp, :].rearrange("p (d t) -> p d t", d=2), w=[x_tok])
                    ps.give(bi2, t)
                    ht["lt"] = tp
            uv_tok = A.last
            V(vec.memset, SP[:, 0, :], 0.0, w=[P.last])
            kd_rel = [[None], [None]]

            def kend(s, ci):
                kd = KD[s % 2]
                for dr in range(2):
                    n = s if dr == 0 else 3 - s
                    tt, pb = n // 2, slice(64 * (n % 2), 64 * (n % 2) + 64)
                    V(vec.tensor_tensor, kd[pb, :].rearrange("p (h e) -> p h e", e=64),
                      ktok[pb, tt, :].rearrange("p (h e) -> p h e", e=64),
                      CT[pb, tt, ci, 32 * dr:32 * dr + 8].unsqueeze(2).to_broadcast([64, 8, 64]), ALU.mult,
                      w=kd_rel[s % 2])
                return kd

            for s in range(4):
                kd = kend(s, 3)
                if s > 0:
                    for par in range(2):
                        b, br, bi = ps.take()
                        for dr in range(2):
                            n = s if dr == 0 else 3 - s
                            pb = slice(64 * (n % 2), 64 * (n % 2) + 64)
                            pp = slice(64 * par, 64 * par + 64)
                            for f in range(4):
                                tp = P(pe.matmul, b[pb, f * 64:f * 64 + 64], wT[pp, 2 * f + dr, 64 * n:64 * n + 64],
                                       SP[pp, s, (dr * 4 + f) * 64:(dr * 4 + f) * 64 + 64], start=True, stop=True,
                                       skip_group_check=True, w=[V.last, uv_tok] + br, sig=f == 3)
                        for dr in range(2):
                            n = s if dr == 0 else 3 - s
                            tt, pb = n // 2, slice(64 * (n % 2), 64 * (n % 2) + 64)
                            uh = uv[pb, dr, tt, :].rearrange("p (f r e) -> p f r e", r=2, e=64)[:, :, par, :]
                            V(vec.tensor_tensor, uh, uh, b[pb, 0:256].rearrange("p (f e) -> p f e", e=64),
                              ALU.subtract, w=[tp])
                        ps.give(bi, V.last)
                if s < 3:
                    for dr in range(2):
                        b, br, bi = ps.take()
                        n = s if dr == 0 else 3 - s
                        tt, pb = n // 2, slice(64 * (n % 2), 64 * (n % 2) + 64)
                        for h in range(8):
                            f, pp = idx(h)
                            tp = P(pe.matmul, b[pp, f * 64:f * 64 + 64], kd[pb, h * 64:h * 64 + 64],
                                   uv[pb, dr, tt, h * 64:h * 64 + 64], start=True, stop=True,
                                   skip_group_check=True, w=[V.last, uv_tok] + br, sig=h == 7)
                        V(vec.tensor_tensor, SP[:, s + 1, dr * 256:dr * 256 + 256].rearrange("p (f e) -> p f e", e=64),
                          SP[:, s, dr * 256:dr * 256 + 256].rearrange("p (f e) -> p f e", e=64),
                          EX[:, dr * 4:dr * 4 + 4, n:n + 1].to_broadcast([128, 4, 64]), ALU.mult)
                        V(vec.tensor_tensor, SP[:, s + 1, dr * 256:dr * 256 + 256],
                          SP[:, s + 1, dr * 256:dr * 256 + 256], b[:, 0:256], ALU.add, w=[tp])
                        ps.give(bi, V.last)
                    kd_rel[s % 2] = [tp]
            sp_tok = V.last
            for f in range(4):
                b, br, bi = ps.take()
                first = {0: True, 1: True}
                for par in range(2):
                    h = 2 * f + par
                    pp = slice(64 * par, 64 * par + 64)
                    for tt in range(2):
                        for dr in range(2):
                            P(pe.matmul, b[pp, tt * 128:tt * 128 + 128], uv[:, dr, tt, h * 64:h * 64 + 64],
                              intra[:, h, dr * 256 + tt * 128:dr * 256 + tt * 128 + 128],
                              start=(tt == 0 and dr == 0), stop=False, skip_group_check=True,
                              w=[sp_tok] + br, sig=False)
                    for dr in range(2):
                        for n in range(4):
                            s = n if dr == 0 else 3 - n
                            if s == 0:
                                continue
                            o = (dr * 4 + f) * 64
                            tp = P(pe.matmul, b[pp, 64 * n:64 * n + 64], SP[pp, s, o:o + 64],
                                   qg[pp, 2 * f + dr, 64 * n:64 * n + 64], start=False, stop=True,
                                   skip_group_check=True)
                r, rr, ri = rot.take()
                A(act.copy, oaT[:, f, :], b[:, 0:256], w=[tp] + rr)
                t = A(act.activation, r[:, 0:256], oaT[:, f, :], ACT.Square)
                ps.give(bi, t)
                b, br, bi = ps.take()
                t = group(b[:, 0:256], [(bones, r[:, 0:256])], w=[t] + br)
                t = A(act.activation, r[:, 256:512], b[:, 0:256], ACT.Sqrt, scale=1.0 / 64, bias=eps[:, :], w=[t])
                ps.give(bi, t)
                V(vec.reciprocal, r[:, 256:512], r[:, 256:512], w=[t])
                V(vec.scalar_tensor_tensor, out=oaT[:, f, :], in0=oaT[:, f, :], scalar=col("gdn"),
                  in1=r[:, 256:512], op0=ALU.mult, op1=ALU.mult)
                V(vec.tensor_tensor, oaT[:, f, :], oaT[:, f, :], zf[:, f, :], ALU.mult)
                rot.give(ri, V.last)
            a_done = [V.last, P.last, A.last]

            A.wait(*a_done)
            V.wait(*a_done)
            SB = BIG[:, 5120 + 1024 + 4096:5120 + 1024 + 4096 + 4096].rearrange("p (s x) -> p s x", s=4)
            hbT = BIG[:, 5120 + 1024 + 8192:5120 + 1024 + 8192 + 1024].rearrange("p (f t) -> p f t", t=256)
            for c, (dst, scl) in enumerate(((qf, 1.0), (kf, 0.125))):
                wc, wt, slot = weight(("win2", 2080 + c * 512, 512), 4096)
                wc = wc.rearrange("p (k n) -> p k n", k=8)
                for q in range(4):
                    t = conv_tile(wc, q, wt, "cvb", c * 4 + q, dst[:, q, :], False, scl)
                used(slot, P.last)
            to_tokens(kf, lambda tt: ktok[:, tt, :], [t])
            wc, wt, slot = weight(("win2", 3104, 512), 4096)
            wc = wc.rearrange("p (k n) -> p k n", k=8)
            vau = vtok.rearrange("p t (h e) -> p t h e", e=128)
            for tt in range(2):
                b, br, bi = ps.take()
                t = group(b[:, :], [(U[:, k, tt * 128:tt * 128 + 128], wc[:, k, :]) for k in range(8)],
                          w=[wt] + br)
                t = A(act.copy, vau[:, tt, :, 0:64], b[:, :].rearrange("p (h e) -> p h e", e=64), w=[t])
                ps.give(bi, t)
                V(vec.memset, vau[:, tt, :, 64:128], 1.0)
            used(slot, P.last)
            wc, wt, slot = weight(("win2", 3616, 512), 4096)
            wc = wc.rearrange("p (k n) -> p k n", k=8)
            for q in range(4):
                b, br, bi = ps.take()
                t = group(b[:, 0:256], [(wc[:, k, q * 128:q * 128 + 128], U[:, k, 0:256]) for k in range(8)],
                          w=[wt] + br)
                t = A(act.activation, zf[:, q, :], b[:, 0:256], ACT.Sigmoid, w=[t])
                ps.give(bi, t)
            used(slot, P.last)
            V(vec.tensor_scalar, R[0], R[10], -1.0, None, ALU.mult)
            softplus_rows(R[2], R[0], R[3])
            V(vec.tensor_scalar, R[0], R[2], -1.0, None, ALU.mult)
            scan(R[1], R[0], ALU.add)
            V(vec.tensor_tensor, R[2], R[9], R[1], ALU.subtract)
            scan(R[3], R[2], ALU.max)
            MP = R[10]
            V(vec.memset, MP[:, 0:16], 0.0)
            for s in range(4):
                for dr in range(2):
                    n = s if dr == 0 else 3 - s
                    p = slice(32 * dr, 32 * dr + 32)
                    lc = 64 * n + (63 if dr == 0 else 0)
                    V(vec.tensor_tensor, MP[p, 4 + n:5 + n], MP[p, n:n + 1], R[3][p, lc:lc + 1], ALU.max)
                    V(vec.tensor_tensor, MP[p, 4 + n:5 + n], MP[p, 4 + n:5 + n], R[1][p, lc:lc + 1], ALU.add)
                    nn = n + 1 if dr == 0 else n - 1
                    if 0 <= nn < 4:
                        V(vec.tensor_copy, MP[p, nn:nn + 1], MP[p, 4 + n:5 + n])

            def mb(o, p=slice(0, 64)):
                return MP[p, o:o + 4].unsqueeze(2).to_broadcast([p.stop - p.start, 4, 64])

            def ch(r, p=slice(0, 64)):
                return r[p, :].rearrange("p (n l) -> p n l", l=64)

            V(vec.tensor_tensor, ch(R[3]), mb(0), ch(R[3]), ALU.max)
            V(vec.tensor_tensor, ch(R[4]), mb(0), ch(R[3]), ALU.subtract)
            V(vec.tensor_tensor, R[5], R[1], R[3], ALU.add)
            for dr in range(2):
                p = slice(32 * dr, 32 * dr + 32)
                V(vec.tensor_copy, MP[p, 8:12], last_of(R[1], dr).rearrange("p n o -> p (n o)"))
            V(vec.tensor_tensor, MP[:, 12:16], MP[:, 8:12], MP[:, 4:8], ALU.subtract)
            V(vec.tensor_tensor, ch(R[6]), mb(12), ch(R[2]), ALU.add)
            V(vec.tensor_tensor, MP[:, 16:20], MP[:, 12:16], MP[:, 0:4], ALU.add)
            V(vec.tensor_scalar, R[7], R[3], -1.0, None, ALU.mult)
            V(vec.tensor_scalar, R[8], R[2], -1.0, None, ALU.mult)
            A(act.activation, R[4], R[4], ACT.Exp, w=[V.last])
            A(act.activation, R[5], R[5], ACT.Exp, scale=-1.0)
            A(act.activation, R[6], R[6], ACT.Exp)
            t = A(act.activation, MP[:, 20:24], MP[:, 16:20], ACT.Exp)
            V.wait(t)
            r_tok = [V.last, t]
            ct_tok = to_cols([R[8], R[6]], [V.last, t])
            V.wait(ct_tok)
            qi_tok = scaled_pairs(qg, qf, R[4], r_tok, [])
            b, br, bi = ps.take()
            for dr in range(2):
                for f in range(4):
                    o = (dr * 4 + f) * 4
                    tp = row_pair(b[:, o:o + 4], MP[:, 20:24], dr, f, r_tok + br, sig=dr == 1 and f == 3)
            V(vec.tensor_copy, EX[:, :, :], b[:, 0:32].rearrange("p (a n) -> p a n", n=4), w=[tp])
            ps.give(bi, V.last)
            for h in range(8):
                f, pp = idx(h)
                dt_, dtt, ri = decay(h, R[7], 0, r_tok)
                bq, br, bqi = ps.take()
                for tt in range(2):
                    tk = slice(tt * 128, tt * 128 + 128)
                    tp = P(pe.matmul, bq[:, tk], kf[pp, f, tk], qf[pp, f, tk], start=True, stop=True,
                           skip_group_check=True, w=[qi_tok] + br, sig=tt == 1)
                for dr in range(2):
                    V(vec.tensor_tensor, intra[:, h, dr * 256:dr * 256 + 256], bq[:, 0:256],
                      dt_[:, dr * 256:dr * 256 + 256], ALU.mult, w=[tp, dtt])
                ps.give(bqi, V.last)
                rot.give(ri, V.last)
            V(vec.memset, SB[:, 0, :], 0.0)
            kd_rel = [[None], [None]]
            for s in range(3):
                kd = kend(s, 1)
                for dr in range(2):
                    n = s if dr == 0 else 3 - s
                    tt, pb = n // 2, slice(64 * (n % 2), 64 * (n % 2) + 64)
                    b, br, bi = ps.take()
                    for h in range(8):
                        f, pp = idx(h)
                        tp = P(pe.matmul, b[pp, f * 128:f * 128 + 128], kd[pb, h * 64:h * 64 + 64],
                               vau[pb, tt, h, :], start=True, stop=True, skip_group_check=True,
                               w=[V.last] + br, sig=h == 7)
                    V(vec.tensor_tensor, SB[:, s + 1, dr * 512:dr * 512 + 512].rearrange("p (f e) -> p f e", e=128),
                      SB[:, s, dr * 512:dr * 512 + 512].rearrange("p (f e) -> p f e", e=128),
                      EX[:, dr * 4:dr * 4 + 4, n:n + 1].to_broadcast([128, 4, 128]), ALU.mult)
                    V(vec.tensor_tensor, SB[:, s + 1, dr * 512:dr * 512 + 512],
                      SB[:, s + 1, dr * 512:dr * 512 + 512], b[:, :], ALU.add, w=[tp])
                    ps.give(bi, V.last)
                kd_rel[s % 2] = [tp]
            sp_tok = V.last
            for f in range(4):
                bg, br, bgi = ps.take()
                for dr in range(2):
                    tg = row_pair(bg[:, dr * 256:dr * 256 + 256], R[5], dr, f, r_tok + br, sig=dr == 1)
                for dr in range(2):
                    b, br, bi = ps.take()
                    for par in range(2):
                        h = 2 * f + par
                        pp = slice(64 * par, 64 * par + 64)
                        for x in range(2):
                            vs = slice(64 * x, 64 * x + 64)
                            for tt in range(2):
                                P(pe.matmul, b[pp, x * 256 + tt * 128:x * 256 + tt * 128 + 128], vau[:, tt, h, vs],
                                  intra[:, h, dr * 256 + tt * 128:dr * 256 + tt * 128 + 128],
                                  start=(x == 0 and tt == 0), stop=False, skip_group_check=True,
                                  w=[sp_tok] + br, sig=False)
                            for n in range(4):
                                s = n if dr == 0 else 3 - n
                                if s == 0:
                                    continue
                                o = dr * 512 + f * 128 + 64 * x
                                tp = P(pe.matmul, b[pp, x * 256 + 64 * n:x * 256 + 64 * n + 64],
                                       SB[pp, s, o:o + 64], qg[pp, 2 * f + dr, 64 * n:64 * n + 64],
                                       start=False, stop=True, skip_group_check=True)
                    r, rr, ri = rot.take()
                    t = A(act.activation, r[:, 0:256], b[:, 256:512], ACT.Abs, w=[tp] + rr)
                    V(vec.tensor_tensor, r[:, 0:256], bg[:, dr * 256:dr * 256 + 256], r[:, 0:256], ALU.max,
                      w=[t, tg])
                    V(vec.reciprocal, r[:, 0:256], r[:, 0:256])
                    dst = hbT[:, f, :] if dr == 0 else r[:, 0:256]
                    V(vec.tensor_tensor, dst, b[:, 0:256], r[:, 0:256], ALU.mult)
                    ps.give(bi, V.last)
                    if dr == 1:
                        V(vec.tensor_tensor, hbT[:, f, :], hbT[:, f, :], r[:, 0:256], ALU.add)
                    rot.give(ri, V.last)
                ps.give(bgi, V.last)
                b, br, bi = ps.take()
                tp = group(b[:, 0:256], [(bones, hbT[:, f, :])], w=[V.last] + br)
                V(vec.scalar_tensor_tensor, out=hbT[:, f, :], in0=b[:, 0:256], scalar=-1.0 / 64, in1=hbT[:, f, :],
                  op0=ALU.mult, op1=ALU.add, w=[tp])
                r, rr, ri = rot.take()
                t = A(act.activation, r[:, 0:256], hbT[:, f, :], ACT.Square, w=[V.last] + rr)
                tp = group(b[:, 256:512], [(bones, r[:, 0:256])], w=[t])
                t = A(act.activation, r[:, 256:512], b[:, 256:512], ACT.Sqrt, scale=1.0 / 64, bias=eps[:, :], w=[tp])
                ps.give(bi, t)
                V(vec.reciprocal, r[:, 256:512], r[:, 256:512], w=[t])
                V(vec.scalar_tensor_tensor, out=hbT[:, f, :], in0=hbT[:, f, :], scalar=col("mln", f, 1),
                  in1=r[:, 256:512], op0=ALU.mult, op1=ALU.mult)
                V(vec.tensor_tensor, hbT[:, f, :], hbT[:, f, :], zf[:, f, :], ALU.mult)
                rot.give(ri, V.last)
            b_tok = V.last
            ym = BIG[:, 0:2048].rearrange("p (k t) -> p k t", t=256)
            for jj in range(4):
                w1, t1, s1 = weight(("gate2", jj), 4096)
                w2, t2, s2 = weight(("br2", jj), 2048)
                w1 = w1.rearrange("p (k n) -> p k n", k=8)
                w2 = w2.rearrange("p (k n) -> p k n", k=8)
                for q in range(2):
                    j = 2 * jj + q
                    gg = []
                    for x in range(2):
                        b, br, bi = ps.take()
                        t = group(b[:, 0:256], [(w1[:, k, 256 * x + q * 128:256 * x + q * 128 + 128],
                                                 U[:, k, 0:256]) for k in range(8)], w=[t1] + br)
                        g, gr, gi = rot.take()
                        t = A(act.activation, g[:, 0:256], b[:, 0:256], ACT.Sigmoid, w=[t] + gr)
                        ps.give(bi, t)
                        b, br, bi = ps.take()
                        src = oaT if x == 0 else hbT
                        tp = group(b[:, 0:256], [(w2[:, 4 * x + k, q * 128:q * 128 + 128], src[:, k, :])
                                                 for k in range(4)], w=[t2, b_tok] + br)
                        V(vec.tensor_tensor, g[:, 0:256], b[:, 0:256], g[:, 0:256], ALU.mult, w=[tp, t])
                        ps.give(bi, V.last)
                        gg.append((g, gi))
                    y_tok = V(vec.tensor_tensor, ym[:, j, :], gg[0][0][:, 0:256], gg[1][0][:, 0:256], ALU.add)
                    for g, gi in gg:
                        rot.give(gi, y_tok)
                used(s1, P.last)
                used(s2, P.last)
            u_rel[0] = P.last
            for c in range(2):
                wc, wt, slot = weight(("wout2", c), 4096)
                wc = wc.rearrange("p (k n) -> p k n", k=8)
                for q in range(4):
                    b, br, bi = ps.take()
                    tp = group(b[:, 0:256], [(wc[:, k, q * 128:q * 128 + 128], ym[:, k, :]) for k in range(8)],
                               w=[wt, y_tok] + br)
                    x_tok = add_x(4 * c + q, b, m2[:, 2], LAT, [tp])
                    ps.give(bi, x_tok)
                used(slot, P.last)
        if STOP > 4:
            ut = norm(col("nffn"), m2[:, 4], m2[:, 3], LAT)
            V.wait(P.last)
            off[0] = 0
            CB = big(32 * 256, 32, 256)
            AC = Pool([big(512, 2, 256) for _ in range(3)])
            rt = big(512)
            cmb = big(64, 2, 32)
            cT = big(256)
            wc, wt, slot = weight(("router",), 288)
            wc = wc.rearrange("p (k n) -> p k n", k=8)
            g8, g4 = CA[:, 2048:2056], CA[:, 2056:2060]
            for tt in range(2):
                b, br, bi = ps.take()
                tp = group(b[:, 0:36], [(U[:, k, tt * 128:tt * 128 + 128], wc[:, k, :]) for k in range(8)],
                           w=[wt, ut] + br)
                L = rt[:, 0:36]
                V(vec.tensor_copy, L, b[:, 0:36], w=[tp])
                ps.give(bi, V.last)
                mx, nm, sm, pg = rt[:, 40:41], rt[:, 41:42], rt[:, 42:43], rt[:, 43:44]
                V(vec.tensor_reduce, mx, L[:, 0:4], AX.X, ALU.max)
                V(vec.tensor_scalar, nm, mx, -1.0, None, ALU.mult)
                t = A(act.activation, rt[:, 44:48], L[:, 0:4], ACT.Exp, bias=nm, accum_out=sm, w=[V.last])
                V(vec.reciprocal, pg, sm, w=[t])

                def first_max(dst, src, m, gn, n, tmp, tm):
                    V(vec.tensor_scalar, tmp, src, m, None, ALU.is_equal)
                    V(vec.tensor_tensor, tmp, tmp, gn, ALU.mult)
                    V(vec.tensor_reduce, tm, tmp, AX.X, ALU.max)
                    V(vec.tensor_scalar, dst, gn, tm, None, ALU.is_equal)

                gs = rt[:, 48:52]
                first_max(gs, L[:, 0:4], mx, g4, 4, rt[:, 52:56], rt[:, 56:57])
                ing = rt[:, 64:72]
                V(vec.tensor_scalar, ing, L[:, 4:12], gs[:, 0:1], None, ALU.mult)
                for g in range(1, 4):
                    V(vec.scalar_tensor_tensor, out=ing, in0=L[:, 4 + 8 * g:12 + 8 * g], scalar=gs[:, g:g + 1],
                      in1=ing, op0=ALU.mult, op1=ALU.add)
                v1, v2, o1, o2 = rt[:, 72:73], rt[:, 73:74], rt[:, 80:88], rt[:, 88:96]
                V(vec.tensor_reduce, v1, ing, AX.X, ALU.max)
                first_max(o1, ing, v1, g8, 8, rt[:, 96:104], rt[:, 104:105])
                rest = rt[:, 112:120]
                V(vec.scalar_tensor_tensor, out=rest, in0=o1, scalar=-3.0e38, in1=ing, op0=ALU.mult, op1=ALU.add)
                V(vec.tensor_reduce, v2, rest, AX.X, ALU.max)
                first_max(o2, rest, v2, g8, 8, rt[:, 96:104], rt[:, 104:105])
                e_, d1, w1_, w2_ = rt[:, 120:121], rt[:, 121:122], rt[:, 122:123], rt[:, 123:124]
                V(vec.tensor_tensor, e_, v2, v1, ALU.subtract)
                t = A(act.activation, e_, e_, ACT.Exp, w=[V.last])
                V(vec.tensor_scalar, d1, e_, 1.0, None, ALU.add, w=[t])
                V(vec.reciprocal, d1, d1)
                V(vec.tensor_tensor, w1_, d1, pg, ALU.mult)
                V(vec.tensor_tensor, w2_, w1_, e_, ALU.mult)
                V(vec.tensor_scalar, o1, o1, w1_, None, ALU.mult)
                V(vec.scalar_tensor_tensor, out=o1, in0=o2, scalar=w2_, in1=o1, op0=ALU.mult, op1=ALU.add)
                for g in range(4):
                    V(vec.tensor_scalar, cmb[:, tt, 8 * g:8 * g + 8], o1, gs[:, g:g + 1], None, ALU.mult)
                b, br, bi = ps.take()
                tp = transp(b[0:32, 0:128], cmb[:, tt, :], w=[V.last] + br)
                t = A(act.copy, cT[0:32, tt * 128:tt * 128 + 128], b[0:32, 0:128], w=[tp])
                ps.give(bi, t)
            used(slot, P.last)
            for e2 in range(16):
                b, br, bi = ps.take()
                for x in range(2):
                    e_ = 2 * e2 + x
                    tp = P(pe.matmul, b[:, x * 256:x * 256 + 256], CC[0:32, e_:e_ + 1].to_broadcast([32, 128]),
                           cT[0:32, 0:256], start=True, stop=True, skip_group_check=True, w=[t] + br, sig=x == 1)
                cb_tok = A(act.copy, CB[:, 2 * e2:2 * e2 + 2, :], b[:, :].rearrange("p (a t) -> p a t", a=2), w=[tp])
                ps.give(bi, cb_tok)
            accb = []
            for i in range(4):
                b, br, bi = ps.take()
                accb.append((b, br))
            pm = Pool([ps.tiles[(ps.i + i) % 8] for i in range(4)])
            for i in range(4):
                pm.rel[i] = ps.rel[(ps.i + i) % 8]
            accw = [r for _, r in accb]

            def down(e_, ac, ai, at, wd, s1, s2, w2t):
                for j in range(8):
                    o = (j % 2) * 256
                    for q in range(2):
                        tp = P(pe.matmul, accb[j // 2][0][:, o:o + 256], wd[:, q, j * 128:j * 128 + 128], ac[:, q, :],
                               start=(e_ == 0 and q == 0 and j % 2 == 0), stop=(e_ == 31 and q == 1),
                               skip_group_check=True, w=[at, w2t] + accw, sig=(j == 7 and q == 1))
                AC.give(ai, tp)
                if s2 is not None:
                    used(s2, tp)
                return tp

            pend = None
            for e_ in range(32):
                w1, t1, s1 = weight(("eup", e_), 4096)
                w1 = w1.rearrange("p (k n) -> p k n", k=8)
                if e_ % 2 == 0:
                    wdn, wdt, wds = weight(("edn", e_ // 2), 4096)
                    wdn = wdn.rearrange("p (x q n) -> p x q n", x=2, q=2)
                ac, acr, ai = AC.take()
                for q in range(2):
                    b, br, bi = pm.take()
                    group(b[:, 0:256], [(w1[:, k, q * 128:q * 128 + 128], U[:, k, 0:256]) for k in range(8)],
                          w=[t1, ut] + br)
                    s, sr, si = rot.take()
                    t = A(act.activation, s[:, 0:256], b[:, 0:256], ACT.Silu, w=[P.last] + sr)
                    pm.give(bi, t)
                    V(vec.tensor_tensor, s[:, 0:256], s[:, 0:256], CB[:, e_, :], ALU.mult, w=[t, cb_tok])
                    b, br, bi = pm.take()
                    tp = group(b[:, 0:256], [(w1[:, k, 256 + q * 128:384 + q * 128], U[:, k, 0:256])
                                             for k in range(8)], w=br)
                    at = V(vec.tensor_tensor, ac[:, q, :], b[:, 0:256], s[:, 0:256], ALU.mult, w=[tp] + acr)
                    pm.give(bi, at)
                    rot.give(si, at)
                used(s1, P.last)
                if pend is not None:
                    down(*pend)
                pend = (e_, ac, ai, at, wdn[:, e_ % 2], s1, wds if e_ % 2 else None, wdt)
            tp = down(*pend)
            for j in range(8):
                o = (j % 2) * 256
                x_tok = V(vec.scalar_tensor_tensor, out=X[:, j, 0:256], in0=accb[j // 2][0][:, o:o + 256],
                          scalar=m2[:, 5, 0, j:j + 1], in1=X[:, j, 0:256], op0=ALU.mult, op1=ALU.add, w=[tp])
            for i in range(4):
                ps.rel[(ps.i + i) % 8] = pm.rel[i]
            for i in range(4):
                ps.rel[(ps.i + 4 + i) % 8] = [x_tok]
            u_rel[0] = P.last
            norm(col("fin2"), None, None, LAT)
        src = U if STOP > 4 else X
        S.dma(nc.sync.dma_start, out_d.rearrange("p (k t) -> p k t", k=8), src[:, :, 0:256], s_out,
              w=[V.last, A.last, P.last])
        S.wait((s_out, 16))

        block = ctx.enter_context(nc.Block())

        @block.sync
        def _(e):
            S.emit(e)

        @block.vector
        def _(e):
            V.emit(e)

        @block.scalar
        def _(e):
            A.emit(e)

        @block.tensor
        def _(e):
            P.emit(e)


def colv(v):
    return np.ascontiguousarray(v.reshape(-1, 128).T)


def tile(w, cs):
    return w.reshape(-1, 128, w.shape[-1])[:, :, cs].transpose(1, 0, 2)


def pack(key, I):
    k = key[0]
    if k == "x":
        x = I["x"][0].T.reshape(8, 128, 256)
        c = I["ctx"][0].T.reshape(8, 128, 256)
        return np.concatenate([x, c], axis=2).transpose(1, 0, 2)
    if k == "wmod":
        return tile(I["w_mod"][key[1]], slice(key[2] * 512, key[2] * 512 + 512))
    if k == "ada":
        return tile(I["ada_w_2"][0], slice(key[1] * 512, key[1] * 512 + 512))
    if k == "fin":
        w = I["ffn_w_in"][key[1], key[2]]
        c = key[3] * 256
        return np.concatenate([tile(w, slice(c, c + 256)), tile(w, slice(DFF + c, DFF + c + 256))], axis=2)
    if k == "fout":
        return tile(I["ffn_w_out"][key[1], key[2]], slice(key[3] * 128, key[3] * 128 + 128))
    if k == "win":
        return tile(I["w_in"][key[1]], slice(key[2], key[2] + key[3]))
    if k == "wgate":
        c = 3584 + key[2] * 256
        w = I["w_in"][key[1]]
        return np.concatenate([tile(w, slice(c, c + 256)), tile(w, slice(c + 1024, c + 1280))], axis=2)
    if k == "wbr":
        s = slice(key[2] * 256, key[2] * 256 + 256)
        return np.concatenate([tile(I["w_attn_out"][key[1]], s), tile(I["w_four_out"][key[1]], s)], axis=1)
    if k == "wo":
        return tile(I["w_o"][key[1]], slice(key[2] * 512, key[2] * 512 + 512))
    w2 = I["w_in_2"][0]
    if k == "win2":
        return tile(w2, slice(key[1], key[1] + key[2]))
    if k == "gates2":
        o = np.zeros((128, 8, 4, 64), np.float32)
        for kind, base in ((0, 2048), (1, 2056), (2, 4128), (3, 4136)):
            for dr in range(2):
                o[:, :, kind, 32 * dr:32 * dr + 8] = tile(w2, slice(base + 16 * dr, base + 16 * dr + 8))
        return o
    if k == "gate2":
        c = 4160 + key[1] * 256
        return np.concatenate([tile(w2, slice(c, c + 256)), tile(w2, slice(c + 1024, c + 1280))], axis=2)
    if k == "br2":
        s = slice(key[1] * 256, key[1] * 256 + 256)
        return np.concatenate([tile(I["w_branch_a_2"][0], s), tile(I["w_branch_b_2"][0], s)], axis=1)
    if k == "wout2":
        return tile(I["w_out_2"][0], slice(key[1] * 512, key[1] * 512 + 512))
    if k == "router":
        s = slice(None)
        return np.concatenate([tile(I["router_group_2"][0], s), tile(I["router_expert_2"][0], s)], axis=2)
    if k == "eup":
        s = slice(None)
        return np.concatenate([tile(I["w_gate_2"][0, key[1]], s), tile(I["w_up_2"][0, key[1]], s)], axis=2)
    if k == "edn":
        s = slice(None)
        return np.stack([tile(I["w_down_2"][0, 2 * key[1] + x], s) for x in range(2)], axis=1)
    raise KeyError(key)


def columns(I):
    o = np.zeros((128, NCOL), np.float32)

    def put(k, v):
        a, w = COLS[k]
        o[:v.shape[0], a:a + w] = v

    def rows(v):
        r = np.zeros((64, 1), np.float32)
        r[0:8, 0], r[32:40, 0] = v[0], v[1]
        return r

    put("c", colv(I["c"][0]))
    put("cx", colv(I["c_ctx"]))
    put("c2", colv(I["c_2"][0]))
    for l in range(2):
        put(f"bmod{l}", colv(I["b_mod"][l]))
        put(f"g{l}", colv(I["norm_g"][l]))
        put(f"bg{l}", colv(I["b_gate"][l]))
        put(f"sub{l}", colv(I["subln_g"][l]))
        put(f"lam{l}", I["lam_params"][l].T)
    put("fin", colv(I["final_g"]))
    put("ada", colv(I["ada_b_2"][0]))
    put("nmix", colv(I["norm_mix_g_2"][0]))
    put("nffn", colv(I["norm_ffn_g_2"][0]))
    put("cva", I["gdn_conv_w_2"][0].reshape(5, 12, 128).transpose(2, 1, 0).reshape(128, 60))
    put("cvb", I["mlstm_conv_w_2"][0].reshape(5, 8, 128).transpose(2, 1, 0).reshape(128, 40))
    put("gdn", np.concatenate([I["gdn_norm_g_2"][0]] * 2)[:, None])
    put("mln", colv(I["mlstm_norm_g_2"][0]))
    put("fin2", colv(I["final_norm_g_2"]))
    put("rows", np.concatenate([rows(I[n][0]) for n in ("gdn_a_log_2", "gdn_dt_bias_2", "mlstm_i_bias_2",
                                                        "mlstm_f_bias_2")], axis=1))
    return o


WORDS = 110923776


def kernel(**inputs):
    import concourse.bacc as _bacc
    from concourse.bass_utils import run_bass_kernel_spmd as _run

    I = {k: np.asarray(v) for k, v in inputs.items()}
    nc = _bacc.Bacc("TRN2", target_bir_lowering=False, num_devices=1, dynamic_dma_scratch_size=4096)
    small = {"cols": columns(I)}
    small["c0"], small["c1"], small["c2"] = consts()
    ws = nc.dram_tensor("ws", (WORDS,), F32, kind="ExternalInput").ap()
    aps = {k: nc.dram_tensor(k, v.shape, F32, kind="ExternalInput").ap() for k, v in small.items()}
    out = nc.dram_tensor("out", (128, 2048), F32, kind="ExternalOutput").ap()
    plan = []
    program(nc, ws, aps["cols"], aps["c0"], aps["c1"], aps["c2"], out, plan)
    w = np.empty((WORDS,), np.float32)
    n = 0
    for key in plan:
        a = pack(key, I)
        w[n:n + a.size] = a.reshape(-1)
        n += a.size
    assert n == WORDS, n
    r = _run(nc, [{"ws": w, **small}], core_ids=[0])
    y = r.results[0]["out"].reshape(128, 8, 256).transpose(2, 1, 0).reshape(1, 256, 1024)
    return np.ascontiguousarray(y)
```

```python
import math
from contextlib import ExitStack

import numpy as np
import concourse.bass as bass
from concourse import mybir

ALU = mybir.AluOpType
ACT = mybir.ActivationFunctionType
AX = mybir.AxisListType
F32 = mybir.dt.float32

STOP = 99
START = 1
PASSES = 2
D = 1024
DFF = 2816
SLOTS = 4
SLOTW = 4096
EPS = 1e-6
NEG = -1e30

COLS = {}
_n = 0
for _k, _w in (("c", 8), ("cx", 8), ("c2", 8), ("bmod0", 72), ("bmod1", 72), ("g0", 24), ("g1", 24),
               ("bg0", 16), ("bg1", 16), ("sub0", 1), ("sub1", 1), ("fin", 8), ("ada", 48), ("nmix", 8),
               ("nffn", 8), ("cva", 60), ("cvb", 40), ("gdn", 1), ("mln", 4), ("fin2", 8), ("rows", 4),
               ("lam0", 4), ("lam1", 4)):
    COLS[_k] = (_n, _w)
    _n += _w
NCOL = _n

C0 = {"ident": (0, 128), "ones": (128, 128), "bones": (256, 128)}
C1 = {"rot": (0, 128), "cos": (128, 256), "sin": (384, 256), "dft": (640, 256), "cs": (896, 512), "ss": (1408, 512)}
C2 = {"neg": (0, 256), "strict": (256, 256), "lvl": (512, 6 * 256), "g8": (2048, 8), "g4": (2056, 4)}
NC0, NC1, NC2 = 384, 1920, 2060


def consts():
    f = np.float32
    c0 = np.zeros((128, NC0), f)
    c0[:, 0:128] = np.eye(128)
    c0[:, 128:256] = 1
    c0[:64, 256:320] = 1
    c0[64:, 320:384] = 1
    c1 = np.zeros((128, NC1), f)
    r = np.zeros((128, 128), f)
    for b in range(0, 128, 32):
        for i in range(16):
            r[b + 16 + i, b + i] = -1
            r[b + i, b + 16 + i] = 1
    c1[:, 0:128] = r
    inv = (1.0 / (f(10000.0) ** (np.arange(0, 32, 2, dtype=f) / f(32)))).astype(f)
    t = np.arange(256)
    for half, pos in ((0, t // 64), (1, t % 64)):
        ang = pos.astype(f)[:, None] * inv[None, :]
        ang = np.concatenate([ang, ang], axis=-1).T
        for comp in (0, 64):
            c1[comp + 32 * half:comp + 32 * half + 32, 128:384] = np.cos(ang)
            c1[comp + 32 * half:comp + 32 * half + 32, 384:640] = np.sin(ang)
    d = np.arange(128)
    a = 2 * np.pi * ((d[:, None] * d[None, :]) % 128) / 128
    c1[:, 640:768] = np.cos(a)
    c1[:, 768:896] = np.sin(a)
    s = np.arange(256)
    b = 2 * np.pi * ((s[:, None] * s[None, :]) % 256) / 256
    sc = 1 / math.sqrt(256 * 128)
    c1[:, 896:1408] = (np.cos(b) * sc).reshape(2, 128, 256).transpose(1, 0, 2).reshape(128, 512)
    c1[:, 1408:1920] = (-np.sin(b) * sc).reshape(2, 128, 256).transpose(1, 0, 2).reshape(128, 512)
    c2 = np.zeros((128, NC2), f)
    j, i = np.meshgrid(np.arange(128), np.arange(128), indexing="ij")
    same = (i // 64) == (j // 64)
    for dr in range(2):
        ok = same & ((i >= j) if dr == 0 else (i <= j))
        c2[:, dr * 128:dr * 128 + 128] = np.where(ok, 0, NEG)
        c2[:, 256 + dr * 128:384 + dr * 128] = (ok & (i != j))
        for lv in range(6):
            w = 1 << lv
            blk = (i // (2 * w)) == (j // (2 * w))
            hi_i, hi_j = (i // w) % 2 == 1, (j // w) % 2 == 1
            m = blk & (hi_i & ~hi_j if dr == 0 else ~hi_i & hi_j)
            o = 512 + lv * 256 + dr * 128
            c2[:, o:o + 128] = m
    c2[:, 2048:2056] = np.arange(8, 0, -1)
    c2[:, 2056:2060] = np.arange(4, 0, -1)
    return c0, c1, c2


class Eng:

    def __init__(self, eng, sem, link):
        self.eng, self.sem, self.linked = eng, sem, link
        self.ops, self.n, self.seen, self.count = [], 0, {}, 0

    def wait(self, *toks):
        for t in toks:
            if t is None:
                continue
            if isinstance(t, list):
                self.wait(*t)
                continue
            s, v = t
            if self.seen.get(id(s), 0) < v:
                self.seen[id(s)] = v
                self.ops.append((None, s, v, None))

    @property
    def last(self):
        return (self.sem, self.n) if self.n else None

    def __call__(self, fn, *args, w=(), sig=True, **kw):
        self.wait(*w)
        if self.linked:
            self.wait(self.last)
        self.ops.append((fn, args, kw, (self.sem, 1) if sig else None))
        self.count += PASSES
        if sig:
            self.n += 1
        return (self.sem, self.n)

    def dma(self, fn, out, in_, sem, w=()):
        self.wait(*w)
        self.ops.append((fn, (out, in_), {}, (sem, 16)))

    def emit(self, e):
        for fn, a, k, s in self.ops:
            if fn is None:
                e.wait_ge(a, k)
            else:
                ins = fn(*a, **k)
                if s is not None:
                    ins.then_inc(*s)


class Pool:

    def __init__(self, tiles):
        self.tiles, self.rel, self.i = tiles, [[] for _ in tiles], 0

    def take(self):
        b = self.i
        self.i = (b + 1) % len(self.tiles)
        r = self.rel[b]
        assert r is not None, "taken before it was given back"
        self.rel[b] = None
        return self.tiles[b], r, b

    def give(self, b, *toks):
        self.rel[b] = list(toks)


def program(nc, ws, cols_d, c0_d, c1_d, c2_d, out_d, plan):
    with ExitStack() as ctx:
        def sb(name, shape):
            return ctx.enter_context(nc.sbuf_tensor(name, shape, F32))

        def sem(name):
            return ctx.enter_context(nc.semaphore(name))

        V = Eng(nc.vector, sem("s_v"), True)
        A = Eng(nc.scalar, sem("s_a"), True)
        P = Eng(nc.tensor, sem("s_p"), False)
        S = Eng(nc.sync, sem("s_s"), False)
        s_c = sem("s_c")
        s_c2 = sem("s_c2")
        s_out = sem("s_out")
        s_w = [sem(f"s_w{i}") for i in range(SLOTS)]

        vec, act, pe = nc.vector, nc.scalar, nc.tensor

        X = sb("X", [128, 8, 512])
        U = sb("U", [128, 8, 512])
        wr = [sb(f"wr{i}", [128, SLOTW]) for i in range(SLOTS)]
        BIG = sb("BIG", [128, 24000])
        CA = sb("CA", [128, NC2])
        CC = sb("CC", [128, NC0])
        K = sb("K", [128, NCOL])
        M = sb("M", [128, 2, 2, 72])
        M2 = sb("M2", [128, 48])
        SC = sb("SC", [128, 3, 8])
        AB = sb("AB", [128, 2, 8])
        GT = sb("GT", [128, 2, 8])
        RS = sb("RS", [128, 512])
        st = sb("st", [128, 64])
        eps = sb("eps", [128, 1])
        acc = Pool([sb(f"acc{i}", [128, 512]) for i in range(2)])
        rot = Pool([sb(f"rot{i}", [128, 512]) for i in range(4)])
        ps = Pool([ctx.enter_context(nc.psum_tensor(f"ps{i}", [128, 512], F32)) for i in range(7)])
        NB = ctx.enter_context(nc.psum_tensor("nb", [128, 512], F32))

        off = [0]

        def big(n, *shape):
            a = BIG[:, off[0]:off[0] + n]
            off[0] += n
            if len(shape) == 2:
                a = a.rearrange("p (a b) -> p a b", b=shape[1])
            elif len(shape) == 3:
                a = a.rearrange("p (a b c) -> p a b c", b=shape[1], c=shape[2])
            elif len(shape) == 4:
                a = a.rearrange("p (a b c d) -> p a b c d", b=shape[1], c=shape[2], d=shape[3])
            return a

        def col(k, i=0, n=None):
            o, w = COLS[k]
            return K[:, o + i:o + (w if n is None else i + n)]

        ident, ones, bones = CC[:, 0:128], CC[:, 128:256], CC[:, 256:384]

        wn = [0, 0]
        wrel = [None] * SLOTS
        wtok = []

        def load(width):
            n = wn[0]
            wn[0] += 1
            s = n % SLOTS
            assert n < SLOTS or wrel[s] is not None, n
            S.dma(nc.sync.dma_start, wr[s][:, 0:width],
                  ws[wn[1]:wn[1] + 128 * width].rearrange("(p w) -> p w", p=128), s_w[s],
                  w=[wrel[s]] if n >= SLOTS else [])
            wrel[s] = None
            wn[1] += 128 * width
            wtok.append((s_w[s], 16 * (n // SLOTS + 1)))
            return n

        def weight(key, width):
            plan.append(key)
            n = load(width)
            return wr[n % SLOTS][:, 0:width], wtok[n], n % SLOTS

        def used(slot, *toks):
            wrel[slot] = list(toks)

        def group(out, pairs, w=(), wk=None):
            for n, (l, r) in enumerate(pairs):
                ww = list(w) if n == 0 else []
                if wk is not None:
                    ww.append(wk[n])
                t = P(pe.matmul, out, l, r, start=n == 0, stop=n == len(pairs) - 1,
                      skip_group_check=True, w=ww, sig=(n == len(pairs) - 1))
            return t

        def interleave(gens, window, apart=0):
            gens, live, turns = iter(gens), [], apart
            while True:
                turns += 1
                while len(live) < window and (turns > apart or not live):
                    turns = 0 if apart else turns
                    g = next(gens, None)
                    if g is None:
                        break
                    live.append(g)
                if not live:
                    return
                for g in list(live):
                    if next(g, "end") == "end":
                        live.remove(g)

        def transp(out, in_, w=(), sig=True):
            k = in_.shape[0]
            return P(pe.transpose, out, in_, CC[0:k, 0:k], w=w, sig=sig)

        S.dma(nc.sync.dma_start, K[:, :], cols_d, s_c)
        S.dma(nc.sync.dma_start, CC[:, :], c0_d, s_c)
        c_tok = (s_c, 16 * 4)
        ctok0 = c_tok
        S.dma(nc.sync.dma_start, CA[:, 0:NC1], c1_d, s_c)
        S.dma(nc.sync.dma_start, X[:, :, :].rearrange("p a b -> p (a b)"),
              ws[0:128 * 4096].rearrange("(p w) -> p w", p=128), s_c)
        wn[1] = 128 * 4096
        plan.append(("x",))

        V(vec.memset, eps[:, :], EPS)
        for i, k in enumerate(("c", "cx", "c2")):
            sc_tok = A(act.activation, SC[:, i, :], col(k), ACT.Silu, w=[c_tok])
        V.wait(c_tok)
        P.wait(c_tok)
        x_tok = c_tok

        def mod_steps(key, conds, dst, bias):
            wc, wt, slot = weight(key, 4096)
            wc = wc.rearrange("p (k n) -> p k n", k=8)
            for c in conds:
                if acc.rel[acc.i] is None:
                    folds.pop(0)()
                a, r, ab = acc.take()
                V(vec.tensor_scalar, a[:, :], wc[:, 0, :], SC[:, c, 0:1], None, ALU.mult, w=[wt, sc_tok] + r)
                yield
                for k in range(1, 8):
                    t = V(vec.scalar_tensor_tensor, out=a[:, :], in0=wc[:, k, :], scalar=SC[:, c, k:k + 1],
                          in1=a[:, :], op0=ALU.mult, op1=ALU.add)
                    if k % 4 == 3:
                        if k == 7 and c == conds[-1]:
                            used(slot, t)
                        yield

                def fold(c=c, a=a, ab=ab, t=t):
                    b, br, bi = ps.take()
                    for q in range(4):
                        t = P(pe.matmul, b[:, q:q + 1], a[:, q * 128:q * 128 + 128], ones[:, 0:1], start=True,
                              stop=True, skip_group_check=True, w=[t] + br if q == 0 else (), sig=q == 3)
                    acc.give(ab, t)
                    t = V(vec.tensor_tensor, dst(c), b[:, 0:4], bias, ALU.add, w=[t])
                    ps.give(bi, t)

                folds.append(fold)

        def layer_mod(l, lo, hi):
            for ch in range(lo, hi):
                yield from mod_steps(("wmod", l, ch), [0, 1], lambda c, ch=ch: M[:, l, c, ch * 4:ch * 4 + 4],
                                     col(f"bmod{l}", ch * 4, 4))

        def ada_mod():
            for ch in range(12):
                yield from mod_steps(("ada", ch), [2], lambda c, ch=ch: M2[:, ch * 4:ch * 4 + 4],
                                     col("ada", ch * 4, 4))

        fill = [None]
        folds = []
        marks = []

        def mark(k):
            marks.append([k, P.count])

        def filler(n=1):
            while folds:
                folds.pop(0)()
            for _ in range(n):
                if fill[0] is not None:
                    try:
                        next(fill[0])
                    except StopIteration:
                        fill[0] = None

        def drain_fill():
            while fill[0] is not None or folds:
                filler()

        u_rel = [None]

        sqs = [0]
        nb_rel = [None]
        sq_pend = []

        def flush_square():
            while sq_pend:
                sq_pend.pop(0)()

        def square(k, T):
            q, r, qi = rot.take()
            t = A(act.activation, q[:, 0:T], X[:, k, 0:T], ACT.Square, w=[x_tok] + r)

            def add():
                tp = P(pe.matmul, NB[:, 0:T], ones, q[:, 0:T], start=k == 0, stop=k == 7, skip_group_check=True,
                       w=[t, nb_rel[0]])
                rot.give(qi, tp)

            flush_square()
            sq_pend.append(add)
            sqs[0] = k + 1

        def norm(gcol, scale, shift, segs):
            T = segs[-1][1]
            for k in range(sqs[0], 8):
                square(k, T)
            flush_square()
            sqs[0] = 0
            q, r, qi = rot.take()
            t = A(act.activation, q[:, 0:T], NB[:, 0:T], ACT.Sqrt, scale=1.0 / D, bias=eps[:, :], w=[P.last] + r)
            nb_rel[0] = t
            V(vec.reciprocal, RS[:, 0:T], q[:, 0:T], w=[t])
            rot.give(qi, V.last)
            nseg = len(segs)
            if scale is not None:
                V(vec.scalar_tensor_tensor, out=AB[:, 0:nseg, :], in0=scale, scalar=1.0,
                  in1=gcol.unsqueeze(1).to_broadcast([128, nseg, 8]), op0=ALU.add, op1=ALU.mult, w=[u_rel[0]])
            toks = []
            for k in range(8):
                for c, (lo, hi) in enumerate(segs):
                    s = AB[:, c, k:k + 1] if scale is not None else gcol[:, k:k + 1]
                    t = V(vec.scalar_tensor_tensor, out=U[:, k, lo:hi], in0=X[:, k, lo:hi], scalar=s,
                          in1=RS[:, lo:hi], op0=ALU.mult, op1=ALU.mult, w=[u_rel[0]])
                    if shift is not None:
                        t = A(act.activation, U[:, k, lo:hi], U[:, k, lo:hi], ACT.Identity,
                              bias=shift[:, c, k:k + 1], w=[t])
                toks.append(t)
            return toks

        def add_x(j, b, gate, segs, w):
            for c, (lo, hi) in enumerate(segs):
                t = V(vec.scalar_tensor_tensor, out=X[:, j, lo:hi], in0=b[:, lo:hi], scalar=gate[:, c, j:j + 1],
                      in1=X[:, j, lo:hi], op0=ALU.mult, op1=ALU.add, w=w)
            return t

        def ffn(l, f, segs, per=4):
            nonlocal x_tok
            T = segs[-1][1]
            n = len(segs)
            i = 2 * f
            ml = M[:, l, 0:n, :]
            ut = norm(col(f"g{l}", 8 * i, 8), ml[:, :, (3 * i + 1) * 8:(3 * i + 2) * 8],
                      ml[:, :, 3 * i * 8:(3 * i + 1) * 8], segs)
            off[0] = 0
            h = big(22 * 512, 22, 512)
            for c in range(11):
                wc, wt, slot = weight(("fin", l, f, c), 4096)
                wc = wc.rearrange("p (k n) -> p k n", k=8)
                for q in range(2):
                    a, ar, ai = ps.take()
                    group(a[:, 0:T], [(wc[:, k, q * 128:q * 128 + 128], U[:, k, 0:T]) for k in range(8)],
                          w=[wt] + ar, wk=ut)
                    s, sr, si = rot.take()
                    t = A(act.activation, s[:, 0:T], a[:, 0:T], ACT.Silu, w=[P.last] + sr)
                    ps.give(ai, t)
                    b, br, bi = ps.take()
                    tp = group(b[:, 0:T], [(wc[:, k, 256 + q * 128:384 + q * 128], U[:, k, 0:T]) for k in range(8)],
                               w=br)
                    ht = V(vec.tensor_tensor, h[:, 2 * c + q, 0:T], b[:, 0:T], s[:, 0:T], ALU.mult, w=[t, tp])
                    ps.give(bi, ht)
                    rot.give(si, ht)
                    filler(per)
                used(slot, P.last)
            u_rel[0] = P.last
            V(vec.tensor_scalar, GT[:, 0:n, :], ml[:, :, (3 * i + 2) * 8:(3 * i + 3) * 8], 0.5, None, ALU.mult)
            for j in range(8):
                wc, wt, slot = weight(("fout", l, f, j), 22 * 128)
                wc = wc.rearrange("p (k n) -> p k n", k=22)
                b, br, bi = ps.take()
                tp = group(b[:, 0:T], [(wc[:, k, :], h[:, k, 0:T]) for k in range(22)], w=[wt, ht] + br)
                used(slot, tp)
                filler(per)
                x_tok = add_x(j, b, GT, segs, [tp])
                ps.give(bi, x_tok)
                square(j, T)

        LAT = [(0, 256)]
        BOTH = [(0, 256), (256, 512)]

        def mixer(l):
            nonlocal x_tok
            last = l == 1
            lam_init = 0.8 - 0.6 * math.exp(-0.3 * l)
            ml = M[:, l, :, :]
            ut = norm(col(f"g{l}", 8, 8), ml[:, :, 32:40], ml[:, :, 24:32], BOTH)
            qT_ = 256 if last else 512
            segs = LAT if last else BOTH
            off[0] = 0
            qT = big(4096, 8, 512)
            kT = big(4096, 8, 512)
            Vt = big(4096, 4, 1024)
            fT = big(2048, 4, 512)
            PA = [big(512) for _ in range(8)]
            aT = [big(1024, 4, 256) for _ in range(2)]
            cos, sin, rm = CA[:, 128:384], CA[:, 384:640], CA[:, 0:128]
            ls = st[:, 0:2]
            o = COLS[f"lam{l}"][0]
            V(vec.tensor_tensor, st[:, 0:2], K[:, o:o + 4:2], K[:, o + 1:o + 4:2], ALU.mult)
            b, br, bi = ps.take()
            t = group(b[:, 0:2], [(ones, ls)], w=[V.last] + br)
            t = A(act.activation, st[:, 2:4], b[:, 0:2], ACT.Exp, w=[t])
            ps.give(bi, t)
            V(vec.tensor_tensor, st[:, 4:5], st[:, 2:3], st[:, 3:4], ALU.subtract, w=[t])
            V(vec.tensor_scalar, st[:, 5:6], st[:, 4:5], lam_init, -1.0, ALU.add, ALU.mult)
            nlam = st[:, 5:6]
            V(vec.tensor_scalar, st[:, 6:7], col(f"sub{l}"), 1 - lam_init, None, ALU.mult)
            subg = st[:, 6:7]
            for qk, dst, T in ((0, qT, qT_), (1, kT, 512)):
                for c in range(2):
                    wc, wt, slot = weight(("win", l, qk * 1024 + c * 512, 512), 4096)
                    wc = wc.rearrange("p (k n) -> p k n", k=8)
                    for q in range(4):
                        h = 4 * c + q
                        b, br, bi = ps.take()
                        t = group(b[:, 0:T], [(wc[:, k, q * 128:q * 128 + 128], U[:, k, 0:T]) for k in range(8)],
                                  w=[wt] + br, wk=ut)
                        r, rr, ri = rot.take()
                        t = A(act.copy, r[:, 0:256], b[:, 0:256], w=[t] + rr)
                        if T == 512:
                            t = A(act.copy, dst[:, h, 256:512], b[:, 256:512])
                        ps.give(bi, t)
                        b, br, bi = ps.take()
                        tp = group(b[:, 0:256], [(rm, r[:, 0:256])], w=[t] + br)
                        V(vec.tensor_tensor, dst[:, h, 0:256], r[:, 0:256], cos, ALU.mult, w=[t])
                        V(vec.tensor_tensor, r[:, 256:512], b[:, 0:256], sin, ALU.mult, w=[tp])
                        ps.give(bi, V.last)
                        V(vec.tensor_tensor, dst[:, h, 0:256], dst[:, h, 0:256], r[:, 256:512], ALU.add)
                        rot.give(ri, V.last)
                    used(slot, P.last)
                    filler(4)
            qk_tok = V.last
            for c in range(2):
                wc, wt, slot = weight(("win", l, 2048 + c * 512, 512), 4096)
                wc = wc.rearrange("p (k n) -> p k n", k=8)
                for tt in range(4):
                    b, br, bi = ps.take()
                    t = group(b[:, :], [(U[:, k, tt * 128:tt * 128 + 128], wc[:, k, :]) for k in range(8)],
                              w=[wt] + br)
                    t = A(act.copy, Vt[:, tt, c * 512:c * 512 + 512], b[:, :], w=[t])
                    ps.give(bi, t)
                used(slot, P.last)
                filler(4)
            v_tok = A.last
            wc, wt, slot = weight(("win", l, 3072, 512), 4096)
            wc = wc.rearrange("p (k n) -> p k n", k=8)
            for q in range(4):
                b, br, bi = ps.take()
                t = group(b[:, 0:qT_], [(wc[:, k, q * 128:q * 128 + 128], U[:, k, 0:qT_]) for k in range(8)],
                          w=[wt] + br)
                t = A(act.copy, fT[:, q, 0:qT_], b[:, 0:qT_], w=[t])
                ps.give(bi, t)
            used(slot, P.last)
            f_tok = A.last
            jobs = [(h, s) for h in range(8) for s in range(len(segs))]
            pa_rel = [[None] for _ in range(8)]
            at_rel = [[None], [None]]
            state = {}

            def scores(n):
                h, s = jobs[n]
                klo, khi = (0, 512) if s == 0 else (256, 512)
                nk = khi - klo
                for qb in range(2):
                    for c in range(2):
                        b, br, bi = ps.take()
                        q0 = s * 256 + qb * 128
                        tp = group(b[:, 0:nk], [(qT[64 * c:64 * c + 64, h, q0:q0 + 128],
                                                 kT[64 * c:64 * c + 64, h, klo:khi])], w=[qk_tok] + br)
                        pi = (n % 2) * 4 + qb * 2 + c
                        z = 16 + (n % 2) * 16 + qb * 8 + c
                        V(vec.tensor_reduce, st[:, z:z + 1], b[:, 0:nk], AX.X, ALU.max, w=[tp])
                        V(vec.tensor_scalar, st[:, z + 2:z + 3], st[:, z:z + 1], -0.125, None, ALU.mult)
                        t = A(act.activation, PA[pi][:, 0:nk], b[:, 0:nk], ACT.Exp, bias=st[:, z + 2:z + 3],
                              scale=0.125, accum_out=st[:, z + 4:z + 5], w=[V.last] + pa_rel[pi])
                        ps.give(bi, t)
                for qb in range(2):
                    z = 16 + (n % 2) * 16 + qb * 8
                    p0, p1 = PA[(n % 2) * 4 + qb * 2], PA[(n % 2) * 4 + qb * 2 + 1]
                    V(vec.reciprocal, st[:, z:z + 2], st[:, z + 4:z + 6], w=[t])
                    V(vec.tensor_tensor, st[:, z + 6:z + 7], st[:, z + 1:z + 2], nlam, ALU.mult)
                    V(vec.tensor_scalar, p1[:, 0:nk], p1[:, 0:nk], st[:, z + 6:z + 7], None, ALU.mult)
                    V(vec.scalar_tensor_tensor, out=p0[:, 0:nk], in0=p0[:, 0:nk], scalar=st[:, z:z + 1],
                      in1=p1[:, 0:nk], op0=ALU.mult, op1=ALU.add)
                state[n] = V.last

            def turn(n):
                h, s = jobs[n]
                kt0, nkt = (0, 4) if s == 0 else (2, 2)
                for qb in range(2):
                    pi = (n % 2) * 4 + qb * 2
                    b, br, bi = ps.take()
                    for k in range(nkt):
                        tp = transp(b[:, k * 128:k * 128 + 128], PA[pi][:, k * 128:k * 128 + 128],
                                    w=[state[n]] + br, sig=k == nkt - 1)
                    pa_rel[pi] = [tp]
                    pa_rel[pi + 1] = [state[n]]
                    t = A(act.copy, aT[n % 2][:, 0:nkt, qb * 128:qb * 128 + 128],
                          b[:, 0:nkt * 128].rearrange("p (a b) -> p a b", b=128), w=[tp] + at_rel[n % 2])
                    ps.give(bi, t)
                b, br, bi = ps.take()
                tp = group(b[:, 0:256], [(Vt[:, kt0 + k, h * 128:h * 128 + 128], aT[n % 2][:, k, :])
                                         for k in range(nkt)], w=[t, v_tok] + br)
                at_rel[n % 2] = [tp]
                t = A(act.copy, qT[:, h, s * 256:s * 256 + 256], b[:, 0:256], w=[tp])
                ps.give(bi, t)

            for n in range(len(jobs)):
                scores(n)
                if n:
                    turn(n - 1)
            turn(len(jobs) - 1)
            at_tok = A.last
            for h in range(8):
                q, r, qi = rot.take()
                t = A(act.activation, q[:, 0:qT_], qT[:, h, 0:qT_], ACT.Square, w=r)
                b, br, bi = ps.take()
                tp = group(b[:, 0:qT_], [(ones, q[:, 0:qT_])], w=[t] + br)
                t = A(act.activation, q[:, 0:qT_], b[:, 0:qT_], ACT.Sqrt, scale=1.0 / 128, bias=eps[:, :], w=[tp])
                ps.give(bi, t)
                V(vec.reciprocal, q[:, 0:qT_], q[:, 0:qT_], w=[t])
                an_tok = V(vec.scalar_tensor_tensor, out=qT[:, h, 0:qT_], in0=qT[:, h, 0:qT_], scalar=subg,
                           in1=q[:, 0:qT_], op0=ALU.mult, op1=ALU.mult)
                rot.give(qi, an_tok)
            frT = Vt[:, 0:2, :].rearrange("p a (b t) -> p (a b) t", t=512)
            fr_free = P.last
            cs = CA[:, 896:1408].rearrange("p (a b) -> p a b", b=256)
            ss = CA[:, 1408:1920].rearrange("p (a b) -> p a b", b=256)
            for s in range(len(segs)):
                for g in range(4):
                    b, br, bi = ps.take()
                    for tt in range(2):
                        tp = group(b[:, tt * 256:tt * 256 + 256],
                                   [(fT[:, g, s * 256 + tt * 128:s * 256 + tt * 128 + 128], CA[:, 640:896])],
                                   w=[f_tok] + br)
                    r, rr, ri = rot.take()
                    t = A(act.copy, r[:, :], b[:, :], w=[tp] + rr)
                    ps.give(bi, t)
                    b, br, bi = ps.take()
                    tp = group(b[:, 0:256], [(r[:, 0:128], cs[:, 0, :]), (r[:, 128:256], ss[:, 0, :]),
                                             (r[:, 256:384], cs[:, 1, :]), (r[:, 384:512], ss[:, 1, :])],
                               w=[t] + br)
                    rot.give(ri, tp)
                    fr_tok = A(act.copy, frT[:, g, s * 256:s * 256 + 256], b[:, 0:256], w=[tp, fr_free])
                    ps.give(bi, fr_tok)
            mg = kT
            T = qT_
            for jj in range(4):
                w1, t1, s1 = weight(("wgate", l, jj), 4096)
                w2, t2, s2 = weight(("wbr", l, jj), 3072)
                w1 = w1.rearrange("p (k n) -> p k n", k=8)
                w2 = w2.rearrange("p (k n) -> p k n", k=12)
                for q in range(2):
                    j = 2 * jj + q
                    cq = slice(q * 128, q * 128 + 128)
                    b, br, bi = ps.take()
                    t = group(b[:, 0:T], [(w1[:, k, cq], U[:, k, 0:T]) for k in range(8)], w=[t1] + br)
                    ga, gr, gi = rot.take()
                    t = A(act.activation, ga[:, 0:T], b[:, 0:T], ACT.Sigmoid, bias=col(f"bg{l}", j, 1), w=[t] + gr)
                    ps.give(bi, t)
                    b, br, bi = ps.take()
                    t = group(b[:, 0:T], [(w1[:, k, 256 + q * 128:384 + q * 128], U[:, k, 0:T]) for k in range(8)],
                              w=br)
                    gf, gr, gj = rot.take()
                    t = A(act.activation, gf[:, 0:T], b[:, 0:T], ACT.Sigmoid, bias=col(f"bg{l}", 8 + j, 1),
                          w=[t] + gr)
                    ps.give(bi, t)
                    b, br, bi = ps.take()
                    tp = group(b[:, 0:T], [(w2[:, k, cq], qT[:, k, 0:T]) for k in range(8)], w=[t2, an_tok] + br)
                    V(vec.tensor_tensor, ga[:, 0:T], b[:, 0:T], ga[:, 0:T], ALU.mult, w=[tp, t])
                    ps.give(bi, V.last)
                    b, br, bi = ps.take()
                    tp = group(b[:, 0:T], [(w2[:, 8 + k, cq], frT[:, k, 0:T]) for k in range(4)], w=[fr_tok] + br)
                    V(vec.tensor_tensor, gf[:, 0:T], b[:, 0:T], gf[:, 0:T], ALU.mult, w=[tp])
                    ps.give(bi, V.last)
                    m_tok = V(vec.tensor_tensor, mg[:, j, 0:T], ga[:, 0:T], gf[:, 0:T], ALU.add)
                    rot.give(gi, m_tok)
                    rot.give(gj, m_tok)
                    filler(2)
                used(s1, P.last)
                used(s2, P.last)
            u_rel[0] = P.last
            for c in range(2):
                wc, wt, slot = weight(("wo", l, c), 4096)
                wc = wc.rearrange("p (k n) -> p k n", k=8)
                for q in range(4):
                    b, br, bi = ps.take()
                    tp = group(b[:, 0:T], [(wc[:, k, q * 128:q * 128 + 128], mg[:, k, 0:T]) for k in range(8)],
                               w=[wt, m_tok] + br)
                    x_tok = add_x(4 * c + q, b, ml[:, :, 40:48], segs, [tp])
                    ps.give(bi, x_tok)
                    square(4 * c + q, T)
                used(slot, P.last)

        mark("mod0")
        fill[0] = layer_mod(0, 0, 6) if START == 1 else None
        drain_fill()
        if STOP > 0 and START == 1:
            fill[0] = layer_mod(0, 6, 18)
            mark("ffn00")
            ffn(0, 0, BOTH)
            drain_fill()
        if STOP > 1 and START == 1:
            mark("mix0")
            fill[0] = layer_mod(1, 0, 18)
            mixer(0)
        if STOP > 2 and START == 1:
            mark("ffn01")
            ffn(0, 1, BOTH, per=4)
            drain_fill()
            fill[0] = ada_mod()
            mark("ffn10")
            ffn(1, 0, BOTH, per=3)
            drain_fill()
            mark("mix1")
            mixer(1)
            mark("ffn11")
            ffn(1, 1, LAT)
            norm(col("fin"), None, None, LAT)
            for k in range(8):
                x_tok = V(vec.tensor_copy, X[:, k, 0:256], U[:, k, 0:256], w=[A.last])
            u_rel[0] = P.last
        if START == 2:
            fill[0] = ada_mod()
            drain_fill()

        if STOP > 3:
            S.dma(nc.sync.dma_start, CA[:, :], c2_d, s_c2, w=[P.last, V.last])
            c2t = (s_c2, 16)
            V.wait(c2t)
            P.wait(c2t)
            off[0] = 0
            qf = big(1024, 4, 256)
            kf = big(1024, 4, 256)
            ktok = big(1024, 2, 512)
            vtok = big(2048, 2, 1024)
            zf = big(1024, 4, 256)
            intra = big(4096, 8, 512)
            inv = off[0]
            LT = big(1536, 3, 512)
            TA = big(1536, 3, 512)
            TT = big(1536, 3, 512)
            UU = [big(512) for _ in range(3)]
            off[0] = max(off[0], inv + 4096 + 1024)
            uv = big(2048, 2, 2, 512)
            SP = big(2048, 4, 512)
            KD = [a_[:, :] for a_ in acc.tiles]
            kb = SP.rearrange("p a (b t) -> p (a b) t", t=256)
            oaT = big(1024, 4, 256)
            wT = X[:, :, 256:512]
            qg = U[:, :, 256:512]
            neg = CA[:, 0:256].rearrange("p (d i) -> p d i", d=2)
            strict = CA[:, 256:512].rearrange("p (d i) -> p d i", d=2)
            lvl = CA[:, 512:2048].rearrange("p (l d i) -> p l d i", l=6, d=2)
            CT = big(640, 2, 5, 64)
            EX = big(32, 8, 4)
            XP = Pool([big(260) for i in range(2)])
            R2 = big(256)[0:64, :]
            assert off[0] <= 24000, off[0]
            for xp in XP.tiles:
                V(vec.memset, xp[:, 0:2], 0.0)
                V(vec.memset, xp[:, 258:260], 0.0)
            rows8 = uv.rearrange("p a b c -> p (a b c)")[0:64, :].rearrange("p (r t) -> p r t", t=256)
            R = [rows8[:, i, :] for i in range(2)] + [R2] + [rows8[:, i, :] for i in range(2, 8)] \
                + [RS[0:64, 0:256], RS[0:64, 256:512]]
            m2 = M2[:, :].rearrange("p (a c k) -> p a c k", c=1, k=8)
            ut = norm(col("nmix"), m2[:, 1], m2[:, 0], LAT)

            def conv_tile(wc, q, wt, ck, j, dst, head_norm, scl):
                b, br, bi = ps.take()
                t = group(b[:, 0:256], [(wc[:, k, q * 128:q * 128 + 128], U[:, k, 0:256]) for k in range(8)],
                          w=[wt] + br, wk=ut)
                xp, xr, xi = XP.take()
                t = A(act.copy, xp[:, 2:258], b[:, 0:256], w=[t] + xr)
                ps.give(bi, t)
                r, rr, ri = rot.take()
                V(vec.tensor_scalar, r[:, 0:256], xp[:, 0:256], col(ck, j * 5, 1), None, ALU.mult, w=[t] + rr)
                for i in range(1, 5):
                    t = V(vec.scalar_tensor_tensor, out=r[:, 0:256], in0=xp[:, i:i + 256],
                          scalar=col(ck, j * 5 + i, 1), in1=r[:, 0:256], op0=ALU.mult, op1=ALU.add)
                XP.give(xi, t)
                t = A(act.activation, dst, r[:, 0:256], ACT.Silu, w=[t])
                if head_norm:
                    t = A(act.activation, r[:, 0:256], dst, ACT.Square)
                    yield
                    b, br, bi = ps.take()
                    t = group(b[:, 0:256], [(bones, r[:, 0:256])], w=[t] + br)
                    t = A(act.activation, r[:, 256:512], b[:, 0:256], ACT.Sqrt, bias=eps[:, :], w=[t])
                    ps.give(bi, t)
                    V(vec.reciprocal, r[:, 256:512], r[:, 256:512], w=[t])
                    t = V(vec.scalar_tensor_tensor, out=dst, in0=dst, scalar=scl, in1=r[:, 256:512],
                          op0=ALU.mult, op1=ALU.mult)
                elif scl != 1.0:
                    t = V(vec.tensor_scalar, dst, dst, scl, None, ALU.mult, w=[t])
                rot.give(ri, t)
                done[0] = t

            done = [None]

            def to_tokens(src, dst, w):
                for tt in range(2):
                    b, br, bi = ps.take()
                    for f in range(4):
                        tp = transp(b[:, f * 128:f * 128 + 128], src[:, f, tt * 128:tt * 128 + 128],
                                    w=w + br, sig=f == 3)
                    t = A(act.copy, dst(tt), b[:, :] if dst(tt).free_size() == 512 and len(dst(tt).shape) == 2
                          else b[:, :].rearrange("p (h e) -> p h e", e=64), w=[tp])
                    ps.give(bi, t)
                return t

            def gate_rows(kb_, dst, wc, wt):
                b, br, bi = ps.take()
                t = group(b[0:64, 0:256], [(wc[:, k, kb_ * 64:kb_ * 64 + 64], U[:, k, 0:256]) for k in range(8)],
                          w=[wt] + br, wk=ut)
                return b[0:64, 0:256], t, bi

            def softplus_rows(dst, src, tmp):
                V(vec.tensor_scalar, tmp, src, -1.0, None, ALU.mult)
                t = V(vec.tensor_tensor, tmp, tmp, src, ALU.min)
                A(act.activation, tmp, tmp, ACT.Exp, w=[t])
                t = A(act.activation, tmp, tmp, ACT.Ln, bias=1.0)
                V(vec.scalar_tensor_tensor, out=dst, in0=src, scalar=0.0, in1=tmp, op0=ALU.max, op1=ALU.add, w=[t])

            def scan(dst, src, op):
                for dr in range(2):
                    p = slice(32 * dr, 32 * dr + 32)
                    for n in range(4):
                        s, d_ = src[p, 64 * n:64 * n + 64], dst[p, 64 * n:64 * n + 64]
                        if dr:
                            s, d_ = s[:, ::-1], d_[:, ::-1]
                        if op is ALU.add:
                            V(vec.tensor_tensor_scan, d_, s, s, 0.0, ALU.add, ALU.bypass)
                        else:
                            V(vec.tensor_tensor_scan, d_, s, s, -3e38, ALU.max, ALU.max)

            def last_of(row, dr):
                r = row[32 * dr:32 * dr + 32, :].rearrange("p (n l) -> p n l", l=64)
                return r[:, :, 63:64] if dr == 0 else r[:, :, 0:1]

            def chunks(row, dr):
                return row[32 * dr:32 * dr + 32, :].rearrange("p (n l) -> p n l", l=64)

            def to_cols(rows, w):
                for tt in range(2):
                    b, br, bi = ps.take()
                    for i, r in enumerate(rows):
                        tp = transp(b[:, i * 64:i * 64 + 64], r[:, tt * 128:tt * 128 + 128], w=w + br,
                                    sig=i == len(rows) - 1)
                    t = A(act.copy, CT[:, tt, 0:len(rows), :],
                          b[:, 0:64 * len(rows)].rearrange("p (a b) -> p a b", b=64), w=[tp])
                    ps.give(bi, t)
                return t

            def row_all(out, row, dr, h, w, sig=True):
                r = 32 * dr + h
                return P(pe.matmul, out, CC[0:64, r:r + 1].to_broadcast([64, 128]), row, start=True, stop=True,
                         skip_group_check=True, w=w, sig=sig)

            def row_pair(out, row, dr, f, w, sig=True):
                r = 32 * dr + 2 * f
                P(pe.matmul, out[0:64], CC[0:64, r:r + 1].to_broadcast([64, 64]), row, start=True,
                  stop=True, skip_group_check=True, w=w, sig=False)
                return P(pe.matmul, out[64:128], CC[0:64, r + 1:r + 2].to_broadcast([64, 64]), row, start=True,
                         stop=True, skip_group_check=True, sig=sig)

            def decay_of(h, b, bi, ci, tp):
                r, rr, ri = rot.take()
                for dr in range(2):
                    for tt in range(2):
                        o = dr * 256 + tt * 128
                        t = V(vec.scalar_tensor_tensor, out=r[:, o:o + 128], in0=b[:, o:o + 128],
                              scalar=CT[:, tt, ci, 32 * dr + h:32 * dr + h + 1], in1=neg[:, dr, :],
                              op0=ALU.subtract, op1=ALU.add, w=[tp] + rr)
                ps.give(bi, t)
                t = A(act.activation, r[:, :], r[:, :], ACT.Exp, w=[t])
                return r, t, ri

            def scaled_pairs(dst, src, row, w, wd):
                for f in range(4):
                    b, br, bi = ps.take()
                    for dr in range(2):
                        tp = row_pair(b[:, dr * 256:dr * 256 + 256], row, dr, f, w + br, sig=dr == 1)
                    for dr in range(2):
                        t = V(vec.tensor_tensor, dst[:, 2 * f + dr, :], b[:, dr * 256:dr * 256 + 256], src[:, f, :],
                              ALU.mult, w=[tp] + wd)
                    ps.give(bi, t)
                return t

            mark("projA")
            gw, gt, gslot = weight(("gates2",), 2048)
            gw = gw.rearrange("p (k n) -> p k n", k=8)
            rw = COLS["rows"][0]
            rows = [K[0:64, rw + i:rw + i + 1] for i in range(4)]
            bg, t, bi = gate_rows(0, None, gw, gt)
            V(vec.tensor_scalar, R[0], bg, rows[1], None, ALU.add, w=[t])
            ps.give(bi, V.last)
            bg, t, bi = gate_rows(1, None, gw, gt)
            t = A(act.activation, R[1], bg, ACT.Sigmoid, w=[t])
            ps.give(bi, t)
            for i, dd in ((2, R[9]), (3, R[10])):
                bg, t, bi = gate_rows(i, None, gw, gt)
                V(vec.tensor_scalar, dd, bg, rows[i], None, ALU.add, w=[t])
                ps.give(bi, V.last)
            used(gslot, P.last)
            softplus_rows(R[2], R[0], R[3])
            t = A(act.activation, st[0:64, 8:9], rows[0], ACT.Exp)
            V(vec.tensor_scalar, R[0], R[2], st[0:64, 8:9], -1.0, ALU.mult, ALU.mult, w=[t])
            scan(R[2], R[0], ALU.add)
            for dr in range(2):
                V(vec.tensor_tensor, chunks(R[3], dr), last_of(R[2], dr).to_broadcast([32, 4, 64]), chunks(R[2], dr),
                  ALU.subtract)
            A(act.activation, R[4], R[2], ACT.Exp, w=[V.last])
            t = A(act.activation, R[3], R[3], ACT.Exp)
            V(vec.tensor_tensor, R[5], R[1], R[4], ALU.mult, w=[t])
            r_tok = V.last
            rows_done = [V.last, A.last]
            for c, (dst, hn, scl) in enumerate(((qf, True, 0.125), (kf, True, 1.0), (None, False, 1.0))):
                wc, wt, slot = weight(("win2", c * 512, 512), 4096)
                wc = wc.rearrange("p (k n) -> p k n", k=8)
                d_ = zf if dst is None else dst
                interleave((conv_tile(wc, q, wt, "cva", c * 4 + q, d_[:, q, :], hn, scl) for q in range(4)), 2)
                t = done[0]
                used(slot, P.last)
                if c == 1:
                    to_tokens(kf, lambda tt: ktok[:, tt, :], [t])
                if c == 2:
                    to_tokens(zf, lambda tt: vtok[:, tt, 0:512], [t])
            zt_rel = P.last
            wc, wt, slot = weight(("win2", 1536, 512), 4096)
            wc = wc.rearrange("p (k n) -> p k n", k=8)
            for q in range(4):
                b, br, bi = ps.take()
                t = group(b[:, 0:256], [(wc[:, k, q * 128:q * 128 + 128], U[:, k, 0:256]) for k in range(8)],
                          w=[wt] + br)
                t = A(act.activation, zf[:, q, :], b[:, 0:256], ACT.Silu, w=[t, zt_rel])
                ps.give(bi, t)
            used(slot, P.last)
            mark("gatesA")
            ct_tok = to_cols([R[2], R[1], R[5], R[3]], rows_done)
            V.wait(ct_tok)

            qg_tok = scaled_pairs(qg, qf, R[4], rows_done, [u_rel[0], A.last])
            kb_tok = scaled_pairs(kb, kf, R[1], rows_done, [])
            b, br, bi = ps.take()
            V(vec.tensor_copy, R[6][:, 0:4], R[4][:, 0:256:64])
            V(vec.tensor_copy, R[6][0:32, 0:4], R[4][0:32, 63:256:64])
            for dr in range(2):
                for f in range(4):
                    o = (dr * 4 + f) * 4
                    tp = row_pair(b[:, o:o + 4], R[6][:, 0:4], dr, f, [V.last] + br, sig=dr == 1 and f == 3)
            ex_tok = V(vec.tensor_copy, EX[:, :, :], b[:, 0:32].rearrange("p (a n) -> p a n", n=4), w=[tp])
            ps.give(bi, ex_tok)

            def idx(h):
                return h // 2, slice(64 * (h % 2), 64 * (h % 2) + 64)

            mark("inv")
            slot_rel = [[None] for _ in range(3)]

            def invert(h):
                hh = h % 3
                f, pp = idx(h)
                b, br, bi = ps.take()
                for dr in range(2):
                    tp = row_all(b[:, dr * 256:dr * 256 + 256], R[2], dr, h, [r_tok] + br, sig=dr == 1)
                bq, br, bqi = ps.take()
                for tt in range(2):
                    tk = slice(tt * 128, tt * 128 + 128)
                    tq = P(pe.matmul, bq[:, tk], kf[pp, f, tk], qf[pp, f, tk], start=True, stop=True,
                           skip_group_check=True, w=[qg_tok, kb_tok] + br, sig=tt == 1)
                dt_, dtt, ri = decay_of(h, b, bi, 0, tp)
                for dr in range(2):
                    V(vec.tensor_tensor, intra[:, h, dr * 256:dr * 256 + 256], bq[:, 0:256],
                      dt_[:, dr * 256:dr * 256 + 256], ALU.mult, w=[tq, dtt])
                ps.give(bqi, V.last)
                bk, br, bki = ps.take()
                for dr in range(2):
                    for tt in range(2):
                        tk = slice(tt * 128, tt * 128 + 128)
                        tp = P(pe.matmul, bk[:, dr * 256 + tt * 128:dr * 256 + tt * 128 + 128], kf[pp, f, tk],
                               kb[pp, 2 * f + dr, tk], start=True, stop=True, skip_group_check=True,
                               w=br, sig=dr == 1 and tt == 1)
                V(vec.tensor_tensor, dt_[:, :], bk[:, :], dt_[:, :], ALU.mult, w=[tp])
                ps.give(bki, V.last)
                lt = LT[:, hh, :].rearrange("p (d t i) -> p d t i", d=2, t=2)
                tt4 = TT[:, hh, :].rearrange("p (d t i) -> p d t i", d=2, t=2)
                for dr in range(2):
                    V(vec.tensor_tensor, lt[:, dr], dt_[:, dr * 256:dr * 256 + 256].rearrange(
                        "p (t i) -> p t i", t=2), strict[:, dr, :].unsqueeze(1).to_broadcast([128, 2, 128]),
                      ALU.mult, w=slot_rel[hh])
                rot.give(ri, V.last)
                for dr in range(2):
                    V(vec.tensor_tensor, tt4[:, dr], lt[:, dr],
                      lvl[:, 0, dr, :].unsqueeze(1).to_broadcast([128, 2, 128]), ALU.mult)
                t1_ = V(vec.tensor_tensor, TT[:, hh, :].rearrange("p (a i) -> p a i", i=128),
                        ident.unsqueeze(1).to_broadcast([128, 4, 128]),
                        TT[:, hh, :].rearrange("p (a i) -> p a i", i=128), ALU.subtract)
                yield
                b, br, bi = ps.take()
                for a in range(4):
                    tp = transp(b[:, a * 128:a * 128 + 128], TT[:, hh, a * 128:a * 128 + 128],
                                w=[t1_] + br, sig=a == 3)
                t_ = A(act.copy, TA[:, hh, :], b[:, :], w=[tp])
                ps.give(bi, t_)
                t2_ = None
                for lv in range(1, 6):
                    r, rr, ri = rot.take()
                    rv = r[:, :].rearrange("p (d t i) -> p d t i", d=2, t=2)
                    for dr in range(2):
                        tm = V(vec.tensor_tensor, rv[:, dr], lt[:, dr],
                               lvl[:, lv, dr, :].unsqueeze(1).to_broadcast([128, 2, 128]), ALU.mult, w=rr)
                    yield
                    b, br, bi = ps.take()
                    for a in range(4):
                        s_ = slice(a * 128, a * 128 + 128)
                        tp = P(pe.matmul, b[:, s_], r[:, s_], TA[:, hh, s_], start=True, stop=True,
                               skip_group_check=True, w=[tm, t_, t2_] + br, sig=a == 3)
                    rot.give(ri, tp)
                    uu = UU[hh]
                    tu = A(act.copy, uu, b[:, :], w=[tp])
                    ps.give(bi, tu)
                    yield
                    b2, br2, bi2 = ps.take()
                    for a in range(4):
                        s_ = slice(a * 128, a * 128 + 128)
                        tp2 = P(pe.matmul, b2[:, s_], uu[:, s_], TT[:, hh, s_], start=True, stop=True,
                                skip_group_check=True, w=[tu] + br2, sig=a == 3)
                    if lv < 5:
                        b, br, bi = ps.take()
                        for a in range(4):
                            s_ = slice(a * 128, a * 128 + 128)
                            tp = P(pe.matmul, b[:, s_], TT[:, hh, s_], uu[:, s_], start=True, stop=True,
                                   skip_group_check=True, w=br, sig=a == 3)
                    t2_ = V(vec.tensor_tensor, TT[:, hh, :], TT[:, hh, :], b2[:, :], ALU.subtract, w=[P.last])
                    ps.give(bi2, t2_)
                    if lv < 5:
                        t2_ = V(vec.tensor_tensor, TA[:, hh, :], TA[:, hh, :], b[:, :], ALU.subtract, w=[tp])
                        ps.give(bi, t2_)
                r, rr, ri = rot.take()
                rhs = r[:, :].rearrange("p (x d t e) -> p x d t e", x=2, d=2, t=2)
                for dr in range(2):
                    c_ = 32 * dr + h
                    for tt in range(2):
                        V(vec.tensor_scalar, rhs[:, 0, dr, tt, :], vtok[:, tt, h * 64:h * 64 + 64],
                          CT[:, tt, 1, c_:c_ + 1], None, ALU.mult, w=rr)
                        tr = V(vec.tensor_scalar, rhs[:, 1, dr, tt, :], ktok[:, tt, h * 64:h * 64 + 64],
                               CT[:, tt, 2, c_:c_ + 1], None, ALU.mult)
                yield
                b, br, bi = ps.take()
                b2, br2, bi2 = ps.take()
                for dr in range(2):
                    for tt in range(2):
                        a = dr * 2 + tt
                        s_ = slice(a * 128, a * 128 + 128)
                        P(pe.matmul, b[:, a * 64:a * 64 + 64], TT[:, hh, s_], rhs[:, 0, dr, tt, :], start=True,
                          stop=True, skip_group_check=True, w=[tr] + br, sig=False)
                        tp = P(pe.matmul, b2[pp, s_], rhs[:, 1, dr, tt, :], TT[:, hh, s_], start=True,
                               stop=True, skip_group_check=True, w=br2, sig=a == 3)
                rot.give(ri, tp)
                t = A(act.copy, uv[:, :, :, h * 64:h * 64 + 64].rearrange("p d t e -> p (d t) e"),
                      b[:, 0:256].rearrange("p (a e) -> p a e", e=64), w=[tp])
                ps.give(bi, t)
                t = A(act.copy, wT[pp, 2 * f:2 * f + 2, :], b2[pp, :].rearrange("p (d t) -> p d t", d=2))
                ps.give(bi2, t)
                slot_rel[hh] = [tp, t]

            A.wait(x_tok, V.last)
            interleave((invert(h) for h in range(8)), 3, 3)
            uv_tok = A.last
            mark("scanA")
            V(vec.memset, SP[:, 0, :], 0.0, w=[P.last])
            kd_rel = [[None], [None]]

            def kend(s, ci):
                kd = KD[s % 2]
                for dr in range(2):
                    n = s if dr == 0 else 3 - s
                    tt, pb = n // 2, slice(64 * (n % 2), 64 * (n % 2) + 64)
                    V(vec.tensor_tensor, kd[pb, :].rearrange("p (h e) -> p h e", e=64),
                      ktok[pb, tt, :].rearrange("p (h e) -> p h e", e=64),
                      CT[pb, tt, ci, 32 * dr:32 * dr + 8].unsqueeze(2).to_broadcast([64, 8, 64]), ALU.mult,
                      w=kd_rel[s % 2])
                return kd

            scan_tok = [None]

            def scan_a():
                for s in range(4):
                    kd = kend(s, 3)
                    if s > 0:
                        for par in range(2):
                            b, br, bi = ps.take()
                            for dr in range(2):
                                n = s if dr == 0 else 3 - s
                                pb = slice(64 * (n % 2), 64 * (n % 2) + 64)
                                pp = slice(64 * par, 64 * par + 64)
                                for f in range(4):
                                    tp = P(pe.matmul, b[pb, f * 64:f * 64 + 64], wT[pp, 2 * f + dr, 64 * n:64 * n + 64],
                                           SP[pp, s, (dr * 4 + f) * 64:(dr * 4 + f) * 64 + 64], start=True, stop=True,
                                           skip_group_check=True, w=[V.last, uv_tok] + br, sig=f == 3)
                            for dr in range(2):
                                n = s if dr == 0 else 3 - s
                                tt, pb = n // 2, slice(64 * (n % 2), 64 * (n % 2) + 64)
                                uh = uv[pb, dr, tt, :].rearrange("p (f r e) -> p f r e", r=2, e=64)[:, :, par, :]
                                V(vec.tensor_tensor, uh, uh, b[pb, 0:256].rearrange("p (f e) -> p f e", e=64),
                                  ALU.subtract, w=[tp])
                            ps.give(bi, V.last)
                    yield
                    if s < 3:
                        for dr in range(2):
                            b, br, bi = ps.take()
                            n = s if dr == 0 else 3 - s
                            tt, pb = n // 2, slice(64 * (n % 2), 64 * (n % 2) + 64)
                            for h in range(8):
                                f, pp = idx(h)
                                tp = P(pe.matmul, b[pp, f * 64:f * 64 + 64], kd[pb, h * 64:h * 64 + 64],
                                       uv[pb, dr, tt, h * 64:h * 64 + 64], start=True, stop=True,
                                       skip_group_check=True, w=[V.last, uv_tok] + br, sig=h == 7)
                            V(vec.tensor_tensor, SP[:, s + 1, dr * 256:dr * 256 + 256].rearrange("p (f e) -> p f e", e=64),
                              SP[:, s, dr * 256:dr * 256 + 256].rearrange("p (f e) -> p f e", e=64),
                              EX[:, dr * 4:dr * 4 + 4, n:n + 1].to_broadcast([128, 4, 64]), ALU.mult)
                            V(vec.tensor_tensor, SP[:, s + 1, dr * 256:dr * 256 + 256],
                              SP[:, s + 1, dr * 256:dr * 256 + 256], b[:, 0:256], ALU.add, w=[tp])
                            ps.give(bi, V.last)
                        kd_rel[s % 2] = [tp]
                    yield
                scan_tok[0] = V.last


            SB = BIG[:, inv:inv + 4096].rearrange("p (s x) -> p s x", s=4)
            hbT = BIG[:, inv + 4096:inv + 5120].rearrange("p (f t) -> p f t", t=256)
            rowsb = BIG[0:64, inv + 4096:inv + 6144].rearrange("p (r t) -> p r t", t=256)
            RB = [rowsb[:, i, :] for i in range(2)] + [R2] + [rowsb[:, i, :] for i in range(2, 8)] + R[9:11]
            vau = vtok.rearrange("p t (h e) -> p t h e", e=128)

            def proj_b():
                for c, (dst, scl) in enumerate(((qf, 1.0), (kf, 0.125))):
                    wc, wt, slot = weight(("win2", 2080 + c * 512, 512), 4096)
                    wc = wc.rearrange("p (k n) -> p k n", k=8)
                    for q in range(4):
                        yield from conv_tile(wc, q, wt, "cvb", c * 4 + q, dst[:, q, :], False, scl)
                        yield
                    used(slot, P.last)
                kf_tok = done[0]
                wc, wt, slot = weight(("win2", 3104, 512), 4096)
                wc = wc.rearrange("p (k n) -> p k n", k=8)
                for tt in range(2):
                    b, br, bi = ps.take()
                    t = group(b[:, :], [(U[:, k, tt * 128:tt * 128 + 128], wc[:, k, :]) for k in range(8)],
                              w=[wt] + br)
                    t = A(act.copy, vau[:, tt, :, 0:64], b[:, :].rearrange("p (h e) -> p h e", e=64), w=[t])
                    ps.give(bi, t)
                    V(vec.memset, vau[:, tt, :, 64:128], 1.0)
                    yield
                used(slot, P.last)

            gb_tok = []
            MP = RB[10]

            def gates_b():
                V(vec.tensor_scalar, RB[0], RB[10], -1.0, None, ALU.mult)
                softplus_rows(RB[2], RB[0], RB[3])
                V(vec.tensor_scalar, RB[0], RB[2], -1.0, None, ALU.mult)
                scan(RB[1], RB[0], ALU.add)
                V(vec.tensor_tensor, RB[2], RB[9], RB[1], ALU.subtract)
                scan(RB[3], RB[2], ALU.max)
                V(vec.memset, MP[:, 0:16], 0.0)
                for s in range(4):
                    for dr in range(2):
                        n = s if dr == 0 else 3 - s
                        p = slice(32 * dr, 32 * dr + 32)
                        lc = 64 * n + (63 if dr == 0 else 0)
                        V(vec.tensor_tensor, MP[p, 4 + n:5 + n], MP[p, n:n + 1], RB[3][p, lc:lc + 1], ALU.max)
                        V(vec.tensor_tensor, MP[p, 4 + n:5 + n], MP[p, 4 + n:5 + n], RB[1][p, lc:lc + 1], ALU.add)
                        nn = n + 1 if dr == 0 else n - 1
                        if 0 <= nn < 4:
                            V(vec.tensor_copy, MP[p, nn:nn + 1], MP[p, 4 + n:5 + n])

                def mb(o, p=slice(0, 64)):
                    return MP[p, o:o + 4].unsqueeze(2).to_broadcast([p.stop - p.start, 4, 64])

                def ch(r, p=slice(0, 64)):
                    return r[p, :].rearrange("p (n l) -> p n l", l=64)

                V(vec.tensor_tensor, ch(RB[3]), mb(0), ch(RB[3]), ALU.max)
                V(vec.tensor_tensor, ch(RB[4]), mb(0), ch(RB[3]), ALU.subtract)
                V(vec.tensor_tensor, RB[5], RB[1], RB[3], ALU.add)
                for dr in range(2):
                    p = slice(32 * dr, 32 * dr + 32)
                    V(vec.tensor_copy, MP[p, 8:12], last_of(RB[1], dr).rearrange("p n o -> p (n o)"))
                V(vec.tensor_tensor, MP[:, 12:16], MP[:, 8:12], MP[:, 4:8], ALU.subtract)
                V(vec.tensor_tensor, ch(RB[6]), mb(12), ch(RB[2]), ALU.add)
                V(vec.tensor_tensor, MP[:, 16:20], MP[:, 12:16], MP[:, 0:4], ALU.add)
                V(vec.tensor_scalar, RB[7], RB[3], -1.0, None, ALU.mult)
                V(vec.tensor_scalar, RB[8], RB[2], -1.0, None, ALU.mult)
                A(act.activation, RB[4], RB[4], ACT.Exp, w=[V.last])
                A(act.activation, RB[5], RB[5], ACT.Exp, scale=-1.0)
                A(act.activation, RB[6], RB[6], ACT.Exp)
                t = A(act.activation, MP[:, 20:24], MP[:, 16:20], ACT.Exp)
                gb_tok.extend([V.last, t])
                yield

            A.wait(P.last, V.last)
            V.wait(A.last)
            interleave([scan_a(), proj_b(), gates_b()], 3)
            sp_tok = scan_tok[0]
            mark("outA")
            for f in range(4):
                b, br, bi = ps.take()
                first = {0: True, 1: True}
                for par in range(2):
                    h = 2 * f + par
                    pp = slice(64 * par, 64 * par + 64)
                    for tt in range(2):
                        for dr in range(2):
                            P(pe.matmul, b[pp, tt * 128:tt * 128 + 128], uv[:, dr, tt, h * 64:h * 64 + 64],
                              intra[:, h, dr * 256 + tt * 128:dr * 256 + tt * 128 + 128],
                              start=(tt == 0 and dr == 0), stop=False, skip_group_check=True,
                              w=[sp_tok] + br, sig=False)
                    for dr in range(2):
                        for n in range(4):
                            s = n if dr == 0 else 3 - n
                            if s == 0:
                                continue
                            o = (dr * 4 + f) * 64
                            tp = P(pe.matmul, b[pp, 64 * n:64 * n + 64], SP[pp, s, o:o + 64],
                                   qg[pp, 2 * f + dr, 64 * n:64 * n + 64], start=False, stop=True,
                                   skip_group_check=True)
                r, rr, ri = rot.take()
                A(act.copy, oaT[:, f, :], b[:, 0:256], w=[tp] + rr)
                t = A(act.activation, r[:, 0:256], oaT[:, f, :], ACT.Square)
                ps.give(bi, t)
                b, br, bi = ps.take()
                t = group(b[:, 0:256], [(bones, r[:, 0:256])], w=[t] + br)
                t = A(act.activation, r[:, 256:512], b[:, 0:256], ACT.Sqrt, scale=1.0 / 64, bias=eps[:, :], w=[t])
                ps.give(bi, t)
                V(vec.reciprocal, r[:, 256:512], r[:, 256:512], w=[t])
                V(vec.scalar_tensor_tensor, out=oaT[:, f, :], in0=oaT[:, f, :], scalar=col("gdn"),
                  in1=r[:, 256:512], op0=ALU.mult, op1=ALU.mult)
                V(vec.tensor_tensor, oaT[:, f, :], oaT[:, f, :], zf[:, f, :], ALU.mult)
                rot.give(ri, V.last)
            a_done = [V.last, P.last, A.last]

            mark("projB")
            to_tokens(kf, lambda tt: ktok[:, tt, :], [done[0]])
            wc, wt, slot = weight(("win2", 3616, 512), 4096)
            wc = wc.rearrange("p (k n) -> p k n", k=8)
            for q in range(4):
                b, br, bi = ps.take()
                t = group(b[:, 0:256], [(wc[:, k, q * 128:q * 128 + 128], U[:, k, 0:256]) for k in range(8)],
                          w=[wt] + br)
                t = A(act.activation, zf[:, q, :], b[:, 0:256], ACT.Sigmoid, w=[t, a_done])
                ps.give(bi, t)
            used(slot, P.last)
            mark("gatesB")
            r_tok = gb_tok
            R = RB
            ct_tok = to_cols([R[8], R[6]], r_tok)
            V.wait(ct_tok)
            qi_tok = scaled_pairs(qg, qf, R[4], r_tok, [])
            b, br, bi = ps.take()
            for dr in range(2):
                for f in range(4):
                    o = (dr * 4 + f) * 4
                    tp = row_pair(b[:, o:o + 4], MP[:, 20:24], dr, f, r_tok + br, sig=dr == 1 and f == 3)
            V(vec.tensor_copy, EX[:, :, :], b[:, 0:32].rearrange("p (a n) -> p a n", n=4), w=[tp])
            ps.give(bi, V.last)
            for h in range(8):
                f, pp = idx(h)
                b, br, bi = ps.take()
                for dr in range(2):
                    tp = row_all(b[:, dr * 256:dr * 256 + 256], R[7], dr, h, r_tok + br, sig=dr == 1)
                dt_, dtt, ri = decay_of(h, b, bi, 0, tp)
                bq, br, bqi = ps.take()
                for tt in range(2):
                    tk = slice(tt * 128, tt * 128 + 128)
                    tp = P(pe.matmul, bq[:, tk], kf[pp, f, tk], qf[pp, f, tk], start=True, stop=True,
                           skip_group_check=True, w=[qi_tok] + br, sig=tt == 1)
                for dr in range(2):
                    V(vec.tensor_tensor, intra[:, h, dr * 256:dr * 256 + 256], bq[:, 0:256],
                      dt_[:, dr * 256:dr * 256 + 256], ALU.mult, w=[tp, dtt])
                ps.give(bqi, V.last)
                rot.give(ri, V.last)
            V(vec.memset, SB[:, 0, :], 0.0)
            mark("scanB")
            kd_rel = [[None], [None]]
            for s in range(3):
                kd = kend(s, 1)
                for dr in range(2):
                    n = s if dr == 0 else 3 - s
                    tt, pb = n // 2, slice(64 * (n % 2), 64 * (n % 2) + 64)
                    b, br, bi = ps.take()
                    for h in range(8):
                        f, pp = idx(h)
                        tp = P(pe.matmul, b[pp, f * 128:f * 128 + 128], kd[pb, h * 64:h * 64 + 64],
                               vau[pb, tt, h, :], start=True, stop=True, skip_group_check=True,
                               w=[V.last] + br, sig=h == 7)
                    V(vec.tensor_tensor, SB[:, s + 1, dr * 512:dr * 512 + 512].rearrange("p (f e) -> p f e", e=128),
                      SB[:, s, dr * 512:dr * 512 + 512].rearrange("p (f e) -> p f e", e=128),
                      EX[:, dr * 4:dr * 4 + 4, n:n + 1].to_broadcast([128, 4, 128]), ALU.mult)
                    V(vec.tensor_tensor, SB[:, s + 1, dr * 512:dr * 512 + 512],
                      SB[:, s + 1, dr * 512:dr * 512 + 512], b[:, :], ALU.add, w=[tp])
                    ps.give(bi, V.last)
                kd_rel[s % 2] = [tp]
            sp_tok = V.last
            mark("outB")
            for f in range(4):
                bg, br, bgi = ps.take()
                for dr in range(2):
                    tg = row_pair(bg[:, dr * 256:dr * 256 + 256], R[5], dr, f, r_tok + br, sig=dr == 1)
                for dr in range(2):
                    b, br, bi = ps.take()
                    for par in range(2):
                        h = 2 * f + par
                        pp = slice(64 * par, 64 * par + 64)
                        for x in range(2):
                            vs = slice(64 * x, 64 * x + 64)
                            for tt in range(2):
                                P(pe.matmul, b[pp, x * 256 + tt * 128:x * 256 + tt * 128 + 128], vau[:, tt, h, vs],
                                  intra[:, h, dr * 256 + tt * 128:dr * 256 + tt * 128 + 128],
                                  start=(x == 0 and tt == 0), stop=False, skip_group_check=True,
                                  w=[sp_tok] + br, sig=False)
                            for n in range(4):
                                s = n if dr == 0 else 3 - n
                                if s == 0:
                                    continue
                                o = dr * 512 + f * 128 + 64 * x
                                tp = P(pe.matmul, b[pp, x * 256 + 64 * n:x * 256 + 64 * n + 64],
                                       SB[pp, s, o:o + 64], qg[pp, 2 * f + dr, 64 * n:64 * n + 64],
                                       start=False, stop=True, skip_group_check=True)
                    r, rr, ri = rot.take()
                    t = A(act.activation, r[:, 0:256], b[:, 256:512], ACT.Abs, w=[tp] + rr)
                    V(vec.tensor_tensor, r[:, 0:256], bg[:, dr * 256:dr * 256 + 256], r[:, 0:256], ALU.max,
                      w=[t, tg])
                    V(vec.reciprocal, r[:, 0:256], r[:, 0:256])
                    dst = hbT[:, f, :] if dr == 0 else r[:, 0:256]
                    V(vec.tensor_tensor, dst, b[:, 0:256], r[:, 0:256], ALU.mult)
                    ps.give(bi, V.last)
                    if dr == 1:
                        V(vec.tensor_tensor, hbT[:, f, :], hbT[:, f, :], r[:, 0:256], ALU.add)
                    rot.give(ri, V.last)
                ps.give(bgi, V.last)
                b, br, bi = ps.take()
                tp = group(b[:, 0:256], [(bones, hbT[:, f, :])], w=[V.last] + br)
                V(vec.scalar_tensor_tensor, out=hbT[:, f, :], in0=b[:, 0:256], scalar=-1.0 / 64, in1=hbT[:, f, :],
                  op0=ALU.mult, op1=ALU.add, w=[tp])
                r, rr, ri = rot.take()
                t = A(act.activation, r[:, 0:256], hbT[:, f, :], ACT.Square, w=[V.last] + rr)
                tp = group(b[:, 256:512], [(bones, r[:, 0:256])], w=[t])
                t = A(act.activation, r[:, 256:512], b[:, 256:512], ACT.Sqrt, scale=1.0 / 64, bias=eps[:, :], w=[tp])
                ps.give(bi, t)
                V(vec.reciprocal, r[:, 256:512], r[:, 256:512], w=[t])
                V(vec.scalar_tensor_tensor, out=hbT[:, f, :], in0=hbT[:, f, :], scalar=col("mln", f, 1),
                  in1=r[:, 256:512], op0=ALU.mult, op1=ALU.mult)
                V(vec.tensor_tensor, hbT[:, f, :], hbT[:, f, :], zf[:, f, :], ALU.mult)
                rot.give(ri, V.last)
            b_tok = V.last
            mark("merge2")
            ym = BIG[:, 0:2048].rearrange("p (k t) -> p k t", t=256)
            for jj in range(4):
                w1, t1, s1 = weight(("gate2", jj), 4096)
                w2, t2, s2 = weight(("br2", jj), 2048)
                w1 = w1.rearrange("p (k n) -> p k n", k=8)
                w2 = w2.rearrange("p (k n) -> p k n", k=8)
                for q in range(2):
                    j = 2 * jj + q
                    gg = []
                    for x in range(2):
                        b, br, bi = ps.take()
                        t = group(b[:, 0:256], [(w1[:, k, 256 * x + q * 128:256 * x + q * 128 + 128],
                                                 U[:, k, 0:256]) for k in range(8)], w=[t1] + br)
                        g, gr, gi = rot.take()
                        t = A(act.activation, g[:, 0:256], b[:, 0:256], ACT.Sigmoid, w=[t] + gr)
                        ps.give(bi, t)
                        b, br, bi = ps.take()
                        src = oaT if x == 0 else hbT
                        tp = group(b[:, 0:256], [(w2[:, 4 * x + k, q * 128:q * 128 + 128], src[:, k, :])
                                                 for k in range(4)], w=[t2, b_tok] + br)
                        V(vec.tensor_tensor, g[:, 0:256], b[:, 0:256], g[:, 0:256], ALU.mult, w=[tp, t])
                        ps.give(bi, V.last)
                        gg.append((g, gi))
                    y_tok = V(vec.tensor_tensor, ym[:, j, :], gg[0][0][:, 0:256], gg[1][0][:, 0:256], ALU.add)
                    for g, gi in gg:
                        rot.give(gi, y_tok)
                used(s1, P.last)
                used(s2, P.last)
            u_rel[0] = P.last
            for c in range(2):
                wc, wt, slot = weight(("wout2", c), 4096)
                wc = wc.rearrange("p (k n) -> p k n", k=8)
                for q in range(4):
                    b, br, bi = ps.take()
                    tp = group(b[:, 0:256], [(wc[:, k, q * 128:q * 128 + 128], ym[:, k, :]) for k in range(8)],
                               w=[wt, y_tok] + br)
                    x_tok = add_x(4 * c + q, b, m2[:, 2], LAT, [tp])
                    ps.give(bi, x_tok)
                    square(4 * c + q, 256)
                used(slot, P.last)
        if STOP > 4:
            mark("router")
            ut = norm(col("nffn"), m2[:, 4], m2[:, 3], LAT)
            V.wait(P.last)
            off[0] = 0
            CB = big(32 * 256, 32, 256)
            AC = Pool([big(512, 2, 256) for _ in range(3)])
            rt = big(512)
            cmb = big(64, 2, 32)
            cT = big(256)
            wc, wt, slot = weight(("router",), 288)
            wc = wc.rearrange("p (k n) -> p k n", k=8)
            g8, g4 = CA[:, 2048:2056], CA[:, 2056:2060]
            for tt in range(2):
                b, br, bi = ps.take()
                tp = group(b[:, 0:36], [(U[:, k, tt * 128:tt * 128 + 128], wc[:, k, :]) for k in range(8)],
                           w=[wt] + br, wk=ut)
                L = rt[:, 0:36]
                V(vec.tensor_copy, L, b[:, 0:36], w=[tp])
                ps.give(bi, V.last)
                mx, nm, sm, pg = rt[:, 40:41], rt[:, 41:42], rt[:, 42:43], rt[:, 43:44]
                V(vec.tensor_reduce, mx, L[:, 0:4], AX.X, ALU.max)
                V(vec.tensor_scalar, nm, mx, -1.0, None, ALU.mult)
                t = A(act.activation, rt[:, 44:48], L[:, 0:4], ACT.Exp, bias=nm, accum_out=sm, w=[V.last])
                V(vec.reciprocal, pg, sm, w=[t])

                def first_max(dst, src, m, gn, n, tmp, tm):
                    V(vec.tensor_scalar, tmp, src, m, None, ALU.is_equal)
                    V(vec.tensor_tensor, tmp, tmp, gn, ALU.mult)
                    V(vec.tensor_reduce, tm, tmp, AX.X, ALU.max)
                    V(vec.tensor_scalar, dst, gn, tm, None, ALU.is_equal)

                gs = rt[:, 48:52]
                first_max(gs, L[:, 0:4], mx, g4, 4, rt[:, 52:56], rt[:, 56:57])
                ing = rt[:, 64:72]
                V(vec.tensor_scalar, ing, L[:, 4:12], gs[:, 0:1], None, ALU.mult)
                for g in range(1, 4):
                    V(vec.scalar_tensor_tensor, out=ing, in0=L[:, 4 + 8 * g:12 + 8 * g], scalar=gs[:, g:g + 1],
                      in1=ing, op0=ALU.mult, op1=ALU.add)
                v1, v2, o1, o2 = rt[:, 72:73], rt[:, 73:74], rt[:, 80:88], rt[:, 88:96]
                V(vec.tensor_reduce, v1, ing, AX.X, ALU.max)
                first_max(o1, ing, v1, g8, 8, rt[:, 96:104], rt[:, 104:105])
                rest = rt[:, 112:120]
                V(vec.scalar_tensor_tensor, out=rest, in0=o1, scalar=-3.0e38, in1=ing, op0=ALU.mult, op1=ALU.add)
                V(vec.tensor_reduce, v2, rest, AX.X, ALU.max)
                first_max(o2, rest, v2, g8, 8, rt[:, 96:104], rt[:, 104:105])
                e_, d1, w1_, w2_ = rt[:, 120:121], rt[:, 121:122], rt[:, 122:123], rt[:, 123:124]
                V(vec.tensor_tensor, e_, v2, v1, ALU.subtract)
                t = A(act.activation, e_, e_, ACT.Exp, w=[V.last])
                V(vec.tensor_scalar, d1, e_, 1.0, None, ALU.add, w=[t])
                V(vec.reciprocal, d1, d1)
                V(vec.tensor_tensor, w1_, d1, pg, ALU.mult)
                V(vec.tensor_tensor, w2_, w1_, e_, ALU.mult)
                V(vec.tensor_scalar, o1, o1, w1_, None, ALU.mult)
                V(vec.scalar_tensor_tensor, out=o1, in0=o2, scalar=w2_, in1=o1, op0=ALU.mult, op1=ALU.add)
                for g in range(4):
                    V(vec.tensor_scalar, cmb[:, tt, 8 * g:8 * g + 8], o1, gs[:, g:g + 1], None, ALU.mult)
                b, br, bi = ps.take()
                tp = transp(b[0:32, 0:128], cmb[:, tt, :], w=[V.last] + br)
                t = A(act.copy, cT[0:32, tt * 128:tt * 128 + 128], b[0:32, 0:128], w=[tp])
                ps.give(bi, t)
            used(slot, P.last)
            for e2 in range(16):
                b, br, bi = ps.take()
                for x in range(2):
                    e_ = 2 * e2 + x
                    tp = P(pe.matmul, b[:, x * 256:x * 256 + 256], CC[0:32, e_:e_ + 1].to_broadcast([32, 128]),
                           cT[0:32, 0:256], start=True, stop=True, skip_group_check=True, w=[t] + br, sig=x == 1)
                cb_tok = A(act.copy, CB[:, 2 * e2:2 * e2 + 2, :], b[:, :].rearrange("p (a t) -> p a t", a=2), w=[tp])
                ps.give(bi, cb_tok)
            accb = []
            for i in range(4):
                b, br, bi = ps.take()
                accb.append((b, br))
            pm = Pool([ps.tiles[(ps.i + i) % 7] for i in range(3)] + [NB])
            for i in range(3):
                pm.rel[i] = ps.rel[(ps.i + i) % 7]
            pm.rel[3] = [nb_rel[0]]
            accw = [r for _, r in accb]

            def down(e_, ac, ai, at, wd, s1, s2, w2t):
                for j in range(8):
                    o = (j % 2) * 256
                    for q in range(2):
                        tp = P(pe.matmul, accb[j // 2][0][:, o:o + 256], wd[:, q, j * 128:j * 128 + 128], ac[:, q, :],
                               start=(e_ == 0 and q == 0 and j % 2 == 0), stop=(e_ == 31 and q == 1),
                               skip_group_check=True, w=[at, w2t] + accw, sig=(j == 7 and q == 1))
                AC.give(ai, tp)
                if s2 is not None:
                    used(s2, tp)
                return tp

            pend = None
            mark("moe")
            for e_ in range(32):
                w1, t1, s1 = weight(("eup", e_), 4096)
                w1 = w1.rearrange("p (k n) -> p k n", k=8)
                if e_ % 2 == 0:
                    wdn, wdt, wds = weight(("edn", e_ // 2), 4096)
                    wdn = wdn.rearrange("p (x q n) -> p x q n", x=2, q=2)
                ac, acr, ai = AC.take()
                for q in range(2):
                    b, br, bi = pm.take()
                    group(b[:, 0:256], [(w1[:, k, q * 128:q * 128 + 128], U[:, k, 0:256]) for k in range(8)],
                          w=[t1] + br, wk=ut)
                    s, sr, si = rot.take()
                    t = A(act.activation, s[:, 0:256], b[:, 0:256], ACT.Silu, w=[P.last] + sr)
                    pm.give(bi, t)
                    V(vec.tensor_tensor, s[:, 0:256], s[:, 0:256], CB[:, e_, :], ALU.mult, w=[t, cb_tok])
                    b, br, bi = pm.take()
                    tp = group(b[:, 0:256], [(w1[:, k, 256 + q * 128:384 + q * 128], U[:, k, 0:256])
                                             for k in range(8)], w=br)
                    at = V(vec.tensor_tensor, ac[:, q, :], b[:, 0:256], s[:, 0:256], ALU.mult, w=[tp] + acr)
                    pm.give(bi, at)
                    rot.give(si, at)
                used(s1, P.last)
                if pend is not None:
                    down(*pend)
                pend = (e_, ac, ai, at, wdn[:, e_ % 2], s1, wds if e_ % 2 else None, wdt)
            tp = down(*pend)
            nb_rel[0] = pm.rel[3]
            for j in range(8):
                o = (j % 2) * 256
                x_tok = V(vec.scalar_tensor_tensor, out=X[:, j, 0:256], in0=accb[j // 2][0][:, o:o + 256],
                          scalar=m2[:, 5, 0, j:j + 1], in1=X[:, j, 0:256], op0=ALU.mult, op1=ALU.add, w=[tp])
                square(j, 256)
            u_rel[0] = P.last
            norm(col("fin2"), None, None, LAT)
        src = U if STOP > 4 else X
        S.dma(nc.sync.dma_start, out_d.rearrange("p (k t) -> p k t", k=8), src[:, :, 0:256], s_out,
              w=[V.last, A.last, P.last])
        S.wait((s_out, 16))

        block = ctx.enter_context(nc.Block())

        @block.sync
        def _(e):
            S.emit(e)

        @block.vector
        def _(e):
            V.emit(e)

        @block.scalar
        def _(e):
            A.emit(e)

        @block.tensor
        def _(e):
            P.emit(e)


def colv(v):
    return np.ascontiguousarray(v.reshape(-1, 128).T)


def tile(w, cs):
    return w.reshape(-1, 128, w.shape[-1])[:, :, cs].transpose(1, 0, 2)


def pack(key, I):
    k = key[0]
    if k == "x":
        x = I["x"][0].T.reshape(8, 128, 256)
        c = I["ctx"][0].T.reshape(8, 128, 256)
        return np.concatenate([x, c], axis=2).transpose(1, 0, 2)
    if k == "wmod":
        return tile(I["w_mod"][key[1]], slice(key[2] * 512, key[2] * 512 + 512))
    if k == "ada":
        return tile(I["ada_w_2"][0], slice(key[1] * 512, key[1] * 512 + 512))
    if k == "fin":
        w = I["ffn_w_in"][key[1], key[2]]
        c = key[3] * 256
        return np.concatenate([tile(w, slice(c, c + 256)), tile(w, slice(DFF + c, DFF + c + 256))], axis=2)
    if k == "fout":
        return tile(I["ffn_w_out"][key[1], key[2]], slice(key[3] * 128, key[3] * 128 + 128))
    if k == "win":
        return tile(I["w_in"][key[1]], slice(key[2], key[2] + key[3]))
    if k == "wgate":
        c = 3584 + key[2] * 256
        w = I["w_in"][key[1]]
        return np.concatenate([tile(w, slice(c, c + 256)), tile(w, slice(c + 1024, c + 1280))], axis=2)
    if k == "wbr":
        s = slice(key[2] * 256, key[2] * 256 + 256)
        return np.concatenate([tile(I["w_attn_out"][key[1]], s), tile(I["w_four_out"][key[1]], s)], axis=1)
    if k == "wo":
        return tile(I["w_o"][key[1]], slice(key[2] * 512, key[2] * 512 + 512))
    w2 = I["w_in_2"][0]
    if k == "win2":
        return tile(w2, slice(key[1], key[1] + key[2]))
    if k == "gates2":
        o = np.zeros((128, 8, 4, 64), np.float32)
        for kind, base in ((0, 2048), (1, 2056), (2, 4128), (3, 4136)):
            for dr in range(2):
                o[:, :, kind, 32 * dr:32 * dr + 8] = tile(w2, slice(base + 16 * dr, base + 16 * dr + 8))
        return o
    if k == "gate2":
        c = 4160 + key[1] * 256
        return np.concatenate([tile(w2, slice(c, c + 256)), tile(w2, slice(c + 1024, c + 1280))], axis=2)
    if k == "br2":
        s = slice(key[1] * 256, key[1] * 256 + 256)
        return np.concatenate([tile(I["w_branch_a_2"][0], s), tile(I["w_branch_b_2"][0], s)], axis=1)
    if k == "wout2":
        return tile(I["w_out_2"][0], slice(key[1] * 512, key[1] * 512 + 512))
    if k == "router":
        s = slice(None)
        return np.concatenate([tile(I["router_group_2"][0], s), tile(I["router_expert_2"][0], s)], axis=2)
    if k == "eup":
        s = slice(None)
        return np.concatenate([tile(I["w_gate_2"][0, key[1]], s), tile(I["w_up_2"][0, key[1]], s)], axis=2)
    if k == "edn":
        s = slice(None)
        return np.stack([tile(I["w_down_2"][0, 2 * key[1] + x], s) for x in range(2)], axis=1)
    raise KeyError(key)


def columns(I):
    o = np.zeros((128, NCOL), np.float32)

    def put(k, v):
        a, w = COLS[k]
        o[:v.shape[0], a:a + w] = v

    def rows(v):
        r = np.zeros((64, 1), np.float32)
        r[0:8, 0], r[32:40, 0] = v[0], v[1]
        return r

    put("c", colv(I["c"][0]))
    put("cx", colv(I["c_ctx"]))
    put("c2", colv(I["c_2"][0]))
    for l in range(2):
        put(f"bmod{l}", colv(I["b_mod"][l]))
        put(f"g{l}", colv(I["norm_g"][l]))
        put(f"bg{l}", colv(I["b_gate"][l]))
        put(f"sub{l}", colv(I["subln_g"][l]))
        put(f"lam{l}", I["lam_params"][l].T)
    put("fin", colv(I["final_g"]))
    put("ada", colv(I["ada_b_2"][0]))
    put("nmix", colv(I["norm_mix_g_2"][0]))
    put("nffn", colv(I["norm_ffn_g_2"][0]))
    put("cva", I["gdn_conv_w_2"][0].reshape(5, 12, 128).transpose(2, 1, 0).reshape(128, 60))
    put("cvb", I["mlstm_conv_w_2"][0].reshape(5, 8, 128).transpose(2, 1, 0).reshape(128, 40))
    put("gdn", np.concatenate([I["gdn_norm_g_2"][0]] * 2)[:, None])
    put("mln", colv(I["mlstm_norm_g_2"][0]))
    put("fin2", colv(I["final_norm_g_2"]))
    put("rows", np.concatenate([rows(I[n][0]) for n in ("gdn_a_log_2", "gdn_dt_bias_2", "mlstm_i_bias_2",
                                                        "mlstm_f_bias_2")], axis=1))
    return o


WORDS = 110923776


def kernel(**inputs):
    import concourse.bacc as _bacc
    from concourse.bass_utils import run_bass_kernel_spmd as _run

    I = {k: np.asarray(v) for k, v in inputs.items()}
    nc = _bacc.Bacc("TRN2", target_bir_lowering=False, num_devices=1, dynamic_dma_scratch_size=4096)
    small = {"cols": columns(I)}
    small["c0"], small["c1"], small["c2"] = consts()
    ws = nc.dram_tensor("ws", (WORDS,), F32, kind="ExternalInput").ap()
    aps = {k: nc.dram_tensor(k, v.shape, F32, kind="ExternalInput").ap() for k, v in small.items()}
    out = nc.dram_tensor("out", (128, 2048), F32, kind="ExternalOutput").ap()
    plan = []
    program(nc, ws, aps["cols"], aps["c0"], aps["c1"], aps["c2"], out, plan)
    w = np.empty((WORDS,), np.float32)
    n = 0
    for key in plan:
        a = pack(key, I)
        w[n:n + a.size] = a.reshape(-1)
        n += a.size
    assert n == WORDS or START == 2 or STOP < 99, n
    r = _run(nc, [{"ws": w, **small}], core_ids=[0])
    y = r.results[0]["out"].reshape(128, 8, 256).transpose(2, 1, 0).reshape(1, 256, 1024)
    return np.ascontiguousarray(y)
```

```python
import math
from contextlib import ExitStack

import numpy as np
import concourse.bass as bass
from concourse import mybir

ALU = mybir.AluOpType
ACT = mybir.ActivationFunctionType
AX = mybir.AxisListType
F32 = mybir.dt.float32
F32R = mybir.dt.float32r

D = 1024
DFF = 2816
SLOTS = 4
SLOTW = 4096
EPS = 1e-6
NEG = -1e30

COLS = {}
_n = 0
for _k, _w in (("c", 8), ("cx", 8), ("c2", 8), ("bmod0", 72), ("bmod1", 72), ("g0", 24), ("g1", 24),
               ("bg0", 16), ("bg1", 16), ("sub0", 1), ("sub1", 1), ("fin", 8), ("ada", 48), ("nmix", 8),
               ("nffn", 8), ("cva", 60), ("cvb", 40), ("gdn", 1), ("mln", 4), ("fin2", 8), ("rows", 4),
               ("lam0", 4), ("lam1", 4)):
    COLS[_k] = (_n, _w)
    _n += _w
NCOL = _n

C0 = {"ident": (0, 128), "ones": (128, 128), "bones": (256, 128)}
C1 = {"rot": (0, 128), "cos": (128, 256), "sin": (384, 256), "dft": (640, 256), "cs": (896, 512), "ss": (1408, 512)}
C2 = {"neg": (0, 256), "strict": (256, 256), "lvl": (512, 6 * 256), "g8": (2048, 8), "g4": (2056, 4)}
NC0, NC1, NC2 = 384, 1920, 2060


def consts():
    f = np.float32
    c0 = np.zeros((128, NC0), f)
    c0[:, 0:128] = np.eye(128)
    c0[:, 128:256] = 1
    c0[:64, 256:320] = 1
    c0[64:, 320:384] = 1
    c1 = np.zeros((128, NC1), f)
    r = np.zeros((128, 128), f)
    for b in range(0, 128, 32):
        for i in range(16):
            r[b + 16 + i, b + i] = -1
            r[b + i, b + 16 + i] = 1
    c1[:, 0:128] = r
    inv = (1.0 / (f(10000.0) ** (np.arange(0, 32, 2, dtype=f) / f(32)))).astype(f)
    t = np.arange(256)
    for half, pos in ((0, t // 64), (1, t % 64)):
        ang = pos.astype(f)[:, None] * inv[None, :]
        ang = np.concatenate([ang, ang], axis=-1).T
        for comp in (0, 64):
            c1[comp + 32 * half:comp + 32 * half + 32, 128:384] = np.cos(ang)
            c1[comp + 32 * half:comp + 32 * half + 32, 384:640] = np.sin(ang)
    d = np.arange(128)
    a = 2 * np.pi * ((d[:, None] * d[None, :]) % 128) / 128
    c1[:, 640:768] = np.cos(a)
    c1[:, 768:896] = np.sin(a)
    s = np.arange(256)
    b = 2 * np.pi * ((s[:, None] * s[None, :]) % 256) / 256
    sc = 1 / math.sqrt(256 * 128)
    c1[:, 896:1408] = (np.cos(b) * sc).reshape(2, 128, 256).transpose(1, 0, 2).reshape(128, 512)
    c1[:, 1408:1920] = (-np.sin(b) * sc).reshape(2, 128, 256).transpose(1, 0, 2).reshape(128, 512)
    c2 = np.zeros((128, NC2), f)
    j, i = np.meshgrid(np.arange(128), np.arange(128), indexing="ij")
    same = (i // 64) == (j // 64)
    for dr in range(2):
        ok = same & ((i >= j) if dr == 0 else (i <= j))
        c2[:, dr * 128:dr * 128 + 128] = np.where(ok, 0, NEG)
        c2[:, 256 + dr * 128:384 + dr * 128] = (ok & (i != j))
        for lv in range(6):
            w = 1 << lv
            blk = (i // (2 * w)) == (j // (2 * w))
            hi_i, hi_j = (i // w) % 2 == 1, (j // w) % 2 == 1
            m = blk & (hi_i & ~hi_j if dr == 0 else ~hi_i & hi_j)
            o = 512 + lv * 256 + dr * 128
            c2[:, o:o + 128] = m
    c2[:, 2048:2056] = np.arange(8, 0, -1)
    c2[:, 2056:2060] = np.arange(4, 0, -1)
    return c0, c1, c2


class Eng:

    def __init__(self, eng, sem, link):
        self.eng, self.sem, self.linked = eng, sem, link
        self.ops, self.n, self.seen, self.count = [], 0, {}, 0

    def wait(self, *toks):
        for t in toks:
            if t is None:
                continue
            if isinstance(t, list):
                self.wait(*t)
                continue
            s, v = t
            if self.seen.get(id(s), 0) < v:
                self.seen[id(s)] = v
                self.ops.append((None, s, v, None))

    @property
    def last(self):
        return (self.sem, self.n) if self.n else None

    def __call__(self, fn, *args, w=(), sig=True, **kw):
        self.wait(*w)
        if self.linked:
            self.wait(self.last)
        self.ops.append((fn, args, kw, (self.sem, 1) if sig else None))
        if not self.linked:
            self.count += 1 if args[1].dtype == F32R else 2
        if sig:
            self.n += 1
        return (self.sem, self.n)

    def dma(self, fn, out, in_, sem, w=()):
        self.wait(*w)
        self.ops.append((fn, (out, in_), {}, (sem, 16)))

    def emit(self, e):
        for fn, a, k, s in self.ops:
            if fn is None:
                e.wait_ge(a, k)
            else:
                ins = fn(*a, **k)
                if s is not None:
                    ins.then_inc(*s)


class Pool:

    def __init__(self, tiles):
        self.tiles, self.rel, self.i = tiles, [[] for _ in tiles], 0

    def take(self):
        b = self.i
        self.i = (b + 1) % len(self.tiles)
        r = self.rel[b]
        assert r is not None, "taken before it was given back"
        self.rel[b] = None
        return self.tiles[b], r, b

    def give(self, b, *toks):
        self.rel[b] = list(toks)


def program(nc, ws, cols_d, c0_d, c1_d, c2_d, out_d, plan):
    with ExitStack() as ctx:
        def sb(name, shape):
            return ctx.enter_context(nc.sbuf_tensor(name, shape, F32))

        def sem(name):
            return ctx.enter_context(nc.semaphore(name))

        V = Eng(nc.vector, sem("s_v"), True)
        A = Eng(nc.scalar, sem("s_a"), True)
        G = Eng(nc.gpsimd, sem("s_g"), True)
        P = Eng(nc.tensor, sem("s_p"), False)
        S = Eng(nc.sync, sem("s_s"), False)
        s_c = sem("s_c")
        s_c2 = sem("s_c2")
        s_out = sem("s_out")
        s_w = [sem(f"s_w{i}") for i in range(SLOTS)]

        vec, act, pe = nc.vector, nc.scalar, nc.tensor

        X = sb("X", [128, 8, 512])
        wr = [sb(f"wr{i}", [128, SLOTW]) for i in range(SLOTS)]
        arena = (nc.sbuf_base + 31) // 32 * 32
        U = sb("U", [128, 8, 512])
        BIG = sb("BIG", [128, 24576])
        CA = sb("CA", [128, NC2])
        CC = sb("CC", [128, NC0])
        K = sb("K", [128, NCOL])
        M = sb("M", [128, 2, 2, 72])
        M2 = sb("M2", [128, 48])
        SC = sb("SC", [128, 3, 8])
        AB = sb("AB", [128, 2, 8])
        GT = sb("GT", [128, 2, 8])
        RS = sb("RS", [128, 512])
        st = sb("st", [128, 64])
        eps = sb("eps", [128, 1])
        acc = Pool([sb(f"acc{i}", [128, 512]) for i in range(2)])
        rot = Pool([sb(f"rot{i}", [128, 512]) for i in range(4)])
        ps = Pool([ctx.enter_context(nc.psum_tensor(f"ps{i}", [128, 512], F32)) for i in range(7)])
        NB = ctx.enter_context(nc.psum_tensor("nb", [128, 512], F32))

        off = [0]

        def big(n, *shape):
            a = BIG[:, off[0]:off[0] + n]
            off[0] += n
            if len(shape) == 2:
                a = a.rearrange("p (a b) -> p a b", b=shape[1])
            elif len(shape) == 3:
                a = a.rearrange("p (a b c) -> p a b c", b=shape[1], c=shape[2])
            elif len(shape) == 4:
                a = a.rearrange("p (a b c d) -> p a b c d", b=shape[1], c=shape[2], d=shape[3])
            return a

        def col(k, i=0, n=None):
            o, w = COLS[k]
            return K[:, o + i:o + (w if n is None else i + n)]

        ident, ones, bones = CC[:, 0:128], CC[:, 128:256], CC[:, 256:384]

        def at(name, word, shape):
            return nc.alloc_sbuf_tensor_at(name, shape, F32R, offset=arena + 4 * word)

        UH, UL = at("UH", 4096, [128, 8, 512]), at("UL", 8192, [128, 8, 512])
        HH, HL = at("HH", 12288, [128, 11, 512]), at("HL", 17920, [128, 11, 512])
        FS = [(at(f"fh{i}", o, [128, 1024]), at(f"fl{i}", o + 1024, [128, 1024]))
              for i, o in enumerate((23552, 25600, 0, 2048))]
        MUH, MUL = at("MUH", 4096 + 20480, [128, 8, 512]), at("MUL", 0, [128, 8, 512])
        MGH, MGL = at("MGH", 4096 + 4096, [128, 8, 512]), at("MGL", 4096 + 10240, [128, 8, 512])
        MS = [(at(f"mh{i}", 4096 + 14336 + 2048 * i, [128, 1024]), at(f"ml{i}", 4096 + 15360 + 2048 * i, [128, 1024]))
              for i in range(3)]
        EH, EL = at("EH", 4096 + 9024, [128, 8, 256]), at("EL", 4096 + 11072, [128, 8, 256])
        ES = [(at(f"eh{i}", 4096 + 13120 + 2048 * i, [128, 1024]), at(f"el{i}", 4096 + 14144 + 2048 * i, [128, 1024]))
              for i in range(4)]
        EA = [(at(f"ah{i}", 1024 * i, [128, 2, 256]), at(f"al{i}", 1024 * i + 512, [128, 2, 256])) for i in range(3)]

        wn = [0, 0]
        wrel = [None] * SLOTS
        wtok = []

        def load(width):
            n = wn[0]
            wn[0] += 1
            s = n % SLOTS
            assert n < SLOTS or wrel[s] is not None, n
            S.dma(nc.sync.dma_start, wr[s][:, 0:width],
                  ws[wn[1]:wn[1] + 128 * width].rearrange("(p w) -> p w", p=128), s_w[s],
                  w=[wrel[s]] if n >= SLOTS else [])
            wrel[s] = None
            wn[1] += 128 * width
            wtok.append((s_w[s], 16 * (n // SLOTS + 1)))
            return n

        def weight(key, width):
            plan.append(key)
            n = load(width)
            return wr[n % SLOTS][:, 0:width], wtok[n], n % SLOTS

        def used(slot, *toks):
            wrel[slot] = list(toks)

        def group(out, pairs, w=(), wk=None):
            for n, (l, r) in enumerate(pairs):
                ww = list(w) if n == 0 else []
                if wk is not None:
                    ww.append(wk[n])
                t = P(pe.matmul, out, l, r, start=n == 0, stop=n == len(pairs) - 1,
                      skip_group_check=True, w=ww, sig=(n == len(pairs) - 1))
            return t

        def group3(out, prods, first, last, w, sig=False):
            P.wait(*w)
            for n, (l, r) in enumerate(prods):
                t = P(pe.matmul, out, l, r, start=first and n == 0, stop=last and n == 2, skip_group_check=True,
                      sig=(last or sig) and n == 2)
            return t

        def interleave(gens, window, apart=0):
            gens, live, turns = iter(gens), [], apart
            while True:
                turns += 1
                while len(live) < window and (turns > apart or not live):
                    turns = 0 if apart else turns
                    g = next(gens, None)
                    if g is None:
                        break
                    live.append(g)
                if not live:
                    return
                for g in list(live):
                    if next(g, "end") == "end":
                        live.remove(g)

        def transp(out, in_, w=(), sig=True):
            k = in_.shape[0]
            return P(pe.transpose, out, in_, CC[0:k, 0:k], w=w, sig=sig)

        S.dma(nc.sync.dma_start, K[:, :], cols_d, s_c)
        S.dma(nc.sync.dma_start, CC[:, :], c0_d, s_c)
        c_tok = (s_c, 16 * 4)
        ctok0 = c_tok
        S.dma(nc.sync.dma_start, CA[:, 0:NC1], c1_d, s_c)
        S.dma(nc.sync.dma_start, X[:, :, :].rearrange("p a b -> p (a b)"),
              ws[0:128 * 4096].rearrange("(p w) -> p w", p=128), s_c)
        wn[1] = 128 * 4096
        plan.append(("x",))

        V(vec.memset, eps[:, :], EPS)
        for i, k in enumerate(("c", "cx", "c2")):
            sc_tok = A(act.activation, SC[:, i, :], col(k), ACT.Silu, w=[c_tok])
        V.wait(c_tok)
        P.wait(c_tok)
        x_tok = c_tok

        def mod_steps(key, conds, dst, bias):
            wc, wt, slot = weight(key, 4096)
            wc = wc.rearrange("p (k n) -> p k n", k=8)
            for c in conds:
                if acc.rel[acc.i] is None:
                    folds.pop(0)()
                a, r, ab = acc.take()
                V(vec.tensor_scalar, a[:, :], wc[:, 0, :], SC[:, c, 0:1], None, ALU.mult, w=[wt, sc_tok] + r)
                yield
                for k in range(1, 8):
                    t = V(vec.scalar_tensor_tensor, out=a[:, :], in0=wc[:, k, :], scalar=SC[:, c, k:k + 1],
                          in1=a[:, :], op0=ALU.mult, op1=ALU.add)
                    if k == 7 and c == conds[-1]:
                        used(slot, t)
                    yield

                def fold(c=c, a=a, ab=ab, t=t):
                    b, br, bi = ps.take()
                    for q in range(4):
                        t = P(pe.matmul, b[:, q:q + 1], a[:, q * 128:q * 128 + 128], ones[:, 0:1], start=True,
                              stop=True, skip_group_check=True, w=[t] + br if q == 0 else (), sig=q == 3)
                    acc.give(ab, t)
                    t = V(vec.tensor_tensor, dst(c), b[:, 0:4], bias, ALU.add, w=[t])
                    ps.give(bi, t)

                folds.append(fold)

        def layer_mod(l, lo, hi):
            for ch in range(lo, hi):
                yield from mod_steps(("wmod", l, ch), [0, 1], lambda c, ch=ch: M[:, l, c, ch * 4:ch * 4 + 4],
                                     col(f"bmod{l}", ch * 4, 4))

        def ada_mod():
            for ch in range(12):
                yield from mod_steps(("ada", ch), [2], lambda c, ch=ch: M2[:, ch * 4:ch * 4 + 4],
                                     col("ada", ch * 4, 4))

        fill = [None]
        folds = []

        def filler(n=1):
            while folds:
                folds.pop(0)()
            for _ in range(n):
                if fill[0] is not None:
                    try:
                        next(fill[0])
                    except StopIteration:
                        fill[0] = None

        def drain_fill():
            while fill[0] is not None or folds:
                filler()

        u_rel = [None]

        sqs = [0]
        nb_rel = [None]
        sq_pend = []

        def flush_square():
            while sq_pend:
                sq_pend.pop(0)()

        def square(k, T):
            q, r, qi = rot.take()
            t = A(act.activation, q[:, 0:T], X[:, k, 0:T], ACT.Square, w=[x_tok] + r)

            def add():
                tp = P(pe.matmul, NB[:, 0:T], ones, q[:, 0:T], start=k == 0, stop=k == 7, skip_group_check=True,
                       w=[t, nb_rel[0]])
                rot.give(qi, tp)

            flush_square()
            sq_pend.append(add)
            sqs[0] = k + 1

        def parts(hi, lo, src, w=()):
            th = A(act.copy, hi, src, w=w)

            def low():
                return V(vec.tensor_tensor, lo, src, hi.bitcast(F32), ALU.subtract, w=[th])

            return low

        def three(hi, lo, xh, xl):
            return [(hi, xl), (lo, xh), (hi, xh)]

        class Splits:

            def __init__(self, pool, units, ahead):
                self.pool, self.units, self.ahead, self.q = pool, iter(units), ahead, []

            def more(self):
                u = next(self.units, None)
                if u is None:
                    return
                src, w, slot = u
                (h, l), r, i = self.pool.take()
                n = src.shape[1]
                m = src.shape[2]
                hv = h[:, 0:n * m].rearrange("p (k n) -> p k n", n=m)
                lv = l[:, 0:n * m].rearrange("p (k n) -> p k n", n=m)
                t = parts(hv, lv, src, [w] + r)()
                if slot is not None:
                    used(slot, t)
                self.q.append((hv, lv, t, i))

            def get(self):
                while len(self.q) < self.ahead + 1:
                    n = len(self.q)
                    self.more()
                    if len(self.q) == n:
                        break
                return self.q.pop(0)

        def norm(gcol, scale, shift, segs, split=None):
            T = segs[-1][1]
            for k in range(sqs[0], 8):
                square(k, T)
            flush_square()
            sqs[0] = 0
            q, r, qi = rot.take()
            t = A(act.activation, q[:, 0:T], NB[:, 0:T], ACT.Sqrt, scale=1.0 / D, bias=eps[:, :], w=[P.last] + r)
            nb_rel[0] = t
            V(vec.reciprocal, RS[:, 0:T], q[:, 0:T], w=[t])
            rot.give(qi, V.last)
            nseg = len(segs)
            if scale is not None:
                V(vec.scalar_tensor_tensor, out=AB[:, 0:nseg, :], in0=scale, scalar=1.0,
                  in1=gcol.unsqueeze(1).to_broadcast([128, nseg, 8]), op0=ALU.add, op1=ALU.mult, w=[u_rel[0]])
            toks = []
            lows = []
            for k in range(8):
                for c, (lo, hi) in enumerate(segs):
                    s = AB[:, c, k:k + 1] if scale is not None else gcol[:, k:k + 1]
                    t = V(vec.scalar_tensor_tensor, out=U[:, k, lo:hi], in0=X[:, k, lo:hi], scalar=s,
                          in1=RS[:, lo:hi], op0=ALU.mult, op1=ALU.mult, w=[u_rel[0]])
                    if shift is not None:
                        t = A(act.activation, U[:, k, lo:hi], U[:, k, lo:hi], ACT.Identity,
                              bias=shift[:, c, k:k + 1], w=[t])
                if split is None:
                    toks.append(t)
                else:
                    lows.append(parts(split[0][:, k, 0:T], split[1][:, k, 0:T], U[:, k, 0:T], [u_rel[0]]))
                    if k:
                        toks.append(lows.pop(0)())
            if split is not None:
                toks.append(lows.pop(0)())
            return toks

        def add_x(j, b, gate, segs, w):
            for c, (lo, hi) in enumerate(segs):
                t = V(vec.scalar_tensor_tensor, out=X[:, j, lo:hi], in0=b[:, lo:hi], scalar=gate[:, c, j:j + 1],
                      in1=X[:, j, lo:hi], op0=ALU.mult, op1=ALU.add, w=w)
            return t

        def ffn(l, f, segs, per=10):
            nonlocal x_tok
            T = segs[-1][1]
            n = len(segs)
            i = 2 * f
            ml = M[:, l, 0:n, :]
            ut = norm(col(f"g{l}", 8 * i, 8), ml[:, :, (3 * i + 1) * 8:(3 * i + 2) * 8],
                      ml[:, :, 3 * i * 8:(3 * i + 1) * 8], segs, (UH, UL))
            pool = Pool(FS)
            pool.rel[2] = pool.rel[3] = [ut[7]]

            def units():
                for half in range(2):
                    for c in range(6):
                        m = 2 if c < 5 else 1
                        wc, wt, slot = weight(("fin", l, f, half * 11 + 2 * c, m), 2048 * m)
                        wc = wc.rearrange("p (q x k n) -> p q x k n", q=m, x=2, k=8)
                        for q in range(m):
                            for x in range(2):
                                yield wc[:, q, x], wt, slot if (q, x) == (m - 1, 1) else None
                    for j2 in range(4):
                        wc, wt, slot = weight(("fout", l, f, half, j2), 2816)
                        wc = wc.rearrange("p (j k n) -> p j k n", j=2, k=11)
                        for q in range(2):
                            yield wc[:, q, 0:8], wt, None
                            yield wc[:, q, 8:11], wt, slot if q else None

            sp = Splits(pool, units(), 2)
            for half in range(2):
                h_rel = [P.last]
                lows, ht = [], []
                for p in range(11):
                    a, ar, ai = ps.take()
                    wh, wl, t, wi = sp.get()
                    for k in range(8):
                        tp = group3(a[:, 0:T], three(wh[:, k, :], wl[:, k, :], UH[:, k, 0:T], UL[:, k, 0:T]),
                                    k == 0, k == 7, [t, ut[k]] + ar)
                    pool.give(wi, tp)
                    s, sr, si = rot.take()
                    ts = A(act.activation, s[:, 0:T], a[:, 0:T], ACT.Silu, w=[tp] + sr)
                    ps.give(ai, ts)
                    filler(per // 2)
                    b, br, bi = ps.take()
                    wh, wl, t, wi = sp.get()
                    for k in range(8):
                        tp = group3(b[:, 0:T], three(wh[:, k, :], wl[:, k, :], UH[:, k, 0:T], UL[:, k, 0:T]),
                                    k == 0, k == 7, [t] + br)
                    pool.give(wi, tp)
                    th = V(vec.tensor_tensor, s[:, 0:T], b[:, 0:T], s[:, 0:T], ALU.mult, w=[ts, tp])
                    ps.give(bi, th)
                    lows.append((parts(HH[:, p, 0:T], HL[:, p, 0:T], s[:, 0:T], [th] + h_rel), si))
                    if p:
                        lo_, si_ = lows.pop(0)
                        ht.append(lo_())
                        rot.give(si_, ht[-1])
                    filler(per - per // 2)
                lo_, si_ = lows.pop(0)
                ht.append(lo_())
                rot.give(si_, ht[-1])
                if half:
                    u_rel[0] = P.last
                else:
                    V(vec.tensor_scalar, GT[:, 0:n, :], ml[:, :, (3 * i + 2) * 8:(3 * i + 3) * 8], 0.5, None,
                      ALU.mult)
                for j in range(8):
                    b, br, bi = ps.take()
                    for k0, k1 in ((0, 8), (8, 11)):
                        wh, wl, t, wi = sp.get()
                        for k in range(k0, k1):
                            tp = group3(b[:, 0:T], three(wh[:, k - k0, :], wl[:, k - k0, :], HH[:, k, 0:T],
                                                         HL[:, k, 0:T]), k == 0, k == 10, [t, ht[k]] + br, k == k1 - 1)
                        pool.give(wi, tp)
                        filler(per // 4)
                    x_tok = add_x(j, b, GT, segs, [tp])
                    ps.give(bi, x_tok)
                    if half:
                        square(j, T)
            u_rel[0] = P.last

        LAT = [(0, 256)]
        BOTH = [(0, 256), (256, 512)]

        def mixer(l):
            nonlocal x_tok
            last = l == 1
            lam_init = 0.8 - 0.6 * math.exp(-0.3 * l)
            ml = M[:, l, :, :]
            ut = norm(col(f"g{l}", 8, 8), ml[:, :, 32:40], ml[:, :, 24:32], BOTH, (MUH, MUL))
            pool = Pool(MS)
            for i in range(3):
                pool.rel[i] = [P.last]

            def units(kind):
                if kind == "in":
                    for c in range(4):
                        wc, wt, slot = weight(("win", l, c * 512, 512), 4096)
                        wc = wc.rearrange("p (q k n) -> p q k n", q=4, k=8)
                        for q in range(4):
                            yield wc[:, q], wt, slot if q == 3 else None
                    for c in range(2):
                        wc, wt, slot = weight(("winv", l, 2048 + c * 512, 512), 4096)
                        wc = wc.rearrange("p (k n) -> p k n", k=8)
                        for q in range(4):
                            yield wc[:, 2 * q:2 * q + 2, :], wt, slot if q == 3 else None
                    wc, wt, slot = weight(("win", l, 3072, 512), 4096)
                    wc = wc.rearrange("p (q k n) -> p q k n", q=4, k=8)
                    for q in range(4):
                        yield wc[:, q], wt, slot if q == 3 else None
                elif kind == "gate":
                    for jj in range(4):
                        wc, wt, slot = weight(("wgate", l, jj), 4096)
                        wc = wc.rearrange("p (q k n) -> p q k n", q=4, k=8)
                        for q in range(4):
                            yield wc[:, q], wt, slot if q == 3 else None
                    for c in range(2):
                        wc, wt, slot = weight(("wo", l, c), 4096)
                        wc = wc.rearrange("p (q k n) -> p q k n", q=4, k=8)
                        for q in range(4):
                            yield wc[:, q], wt, slot if q == 3 else None

            sp = Splits(pool, units("in"), 1)

            def tiles(out, T, xh, xl, w, xt=None):
                wh, wl, t, wi = sp.get()
                for k in range(8):
                    tp = group3(out, three(wh[:, k, :], wl[:, k, :], xh[:, k, 0:T], xl[:, k, 0:T]), k == 0, k == 7,
                                [t] + w + ([xt[k]] if xt is not None else []))
                pool.give(wi, tp)
                return tp

            qT_ = 256 if last else 512
            segs = LAT if last else BOTH
            off[0] = 0
            qT = big(4096, 8, 512)
            kT = big(4096, 8, 512)
            Vt = big(4096, 4, 1024)
            fT = big(2048, 4, 512)
            PA = [big(512) for _ in range(8)]
            aT = [big(1024, 4, 256) for _ in range(2)]
            assert off[0] == 20480
            cos, sin, rm = CA[:, 128:384], CA[:, 384:640], CA[:, 0:128]
            ls = st[:, 0:2]
            o = COLS[f"lam{l}"][0]
            V(vec.tensor_tensor, st[:, 0:2], K[:, o:o + 4:2], K[:, o + 1:o + 4:2], ALU.mult)
            b, br, bi = ps.take()
            t = group(b[:, 0:2], [(ones, ls)], w=[V.last] + br)
            t = A(act.activation, st[:, 2:4], b[:, 0:2], ACT.Exp, w=[t])
            ps.give(bi, t)
            V(vec.tensor_tensor, st[:, 4:5], st[:, 2:3], st[:, 3:4], ALU.subtract, w=[t])
            V(vec.tensor_scalar, st[:, 5:6], st[:, 4:5], lam_init, -1.0, ALU.add, ALU.mult)
            nlam = st[:, 5:6]
            V(vec.tensor_scalar, st[:, 6:7], col(f"sub{l}"), 1 - lam_init, None, ALU.mult)
            subg = st[:, 6:7]
            rope = []

            def rotate(h, dst, r, ri, t):
                b, br, bi = ps.take()
                tp = group(b[:, 0:256], [(rm, r[:, 0:256])], w=[t] + br)
                V(vec.tensor_tensor, dst[:, h, 0:256], r[:, 0:256], cos, ALU.mult, w=[t])
                V(vec.tensor_tensor, r[:, 256:512], b[:, 0:256], sin, ALU.mult, w=[tp])
                ps.give(bi, V.last)
                V(vec.tensor_tensor, dst[:, h, 0:256], dst[:, h, 0:256], r[:, 256:512], ALU.add)
                rot.give(ri, V.last)

            for qk, dst, T in ((0, qT, qT_), (1, kT, 512)):
                for h in range(8):
                    b, br, bi = ps.take()
                    t = tiles(b[:, 0:T], T, MUH, MUL, br, ut)
                    if rope:
                        rotate(*rope.pop())
                    r, rr, ri = rot.take()
                    t = A(act.copy, r[:, 0:256], b[:, 0:256], w=[t] + rr)
                    if T == 512:
                        t = A(act.copy, dst[:, h, 256:512], b[:, 256:512])
                    ps.give(bi, t)
                    rope.append((h, dst, r, ri, t))
                    filler(4)
            for c in range(2):
                bs = [ps.take() for _ in range(4)]
                for q in range(4):
                    wh, wl, t, wi = sp.get()
                    for tt in range(4):
                        for kk in range(2):
                            k = 2 * q + kk
                            ts_ = slice(tt * 128, tt * 128 + 128)
                            tp = group3(bs[tt][0][:, :], three(MUH[:, k, ts_], MUL[:, k, ts_], wh[:, kk, :],
                                                               wl[:, kk, :]), k == 0, k == 7, [t] + bs[tt][1],
                                        tt == 3 and kk == 1)
                    pool.give(wi, tp)
                    if rope:
                        rotate(*rope.pop())
                for tt in range(4):
                    t = A(act.copy, Vt[:, tt, c * 512:c * 512 + 512], bs[tt][0][:, :], w=[tp])
                    ps.give(bs[tt][2], t)
                filler(8)
            qk_tok = V.last
            v_tok = A.last
            for q in range(4):
                b, br, bi = ps.take()
                t = tiles(b[:, 0:qT_], qT_, MUH, MUL, br)
                t = A(act.copy, fT[:, q, 0:qT_], b[:, 0:qT_], w=[t])
                ps.give(bi, t)
            f_tok = A.last
            V.wait(P.last)
            jobs = [(h, s) for h in range(8) for s in range(len(segs))]
            p0_rel = [[P.last] for _ in range(6)]
            p1_rel = [[P.last], [P.last]]
            at_rel = [[P.last], [P.last]]
            soft, turned = {}, {}

            def scores(n):
                h, s = jobs[n]
                klo, khi = (0, 512) if s == 0 else (256, 512)
                nk = khi - klo
                soft[n] = []
                for qb in range(2):
                    i0 = (n % 3) * 2 + qb
                    p0, p1 = PA[i0], PA[6 + qb]
                    z = 16 + (n % 2) * 16 + qb * 8
                    for c in range(2):
                        b, br, bi = ps.take()
                        q0 = s * 256 + qb * 128
                        tp = group(b[:, 0:nk], [(qT[64 * c:64 * c + 64, h, q0:q0 + 128],
                                                 kT[64 * c:64 * c + 64, h, klo:khi])], w=[qk_tok] + br)
                        V(vec.tensor_reduce, st[:, z + c:z + c + 1], b[:, 0:nk], AX.X, ALU.max, w=[tp])
                        V(vec.tensor_scalar, st[:, z + 2 + c:z + 3 + c], st[:, z + c:z + c + 1], -0.125, None,
                          ALU.mult)
                        t = A(act.activation, (p0, p1)[c][:, 0:nk], b[:, 0:nk], ACT.Exp,
                              bias=st[:, z + 2 + c:z + 3 + c], scale=0.125, accum_out=st[:, z + 4 + c:z + 5 + c],
                              w=[V.last] + (p0_rel[i0] if c == 0 else p1_rel[qb]))
                        ps.give(bi, t)
                    tq = t
                    soft[n].append((z, p0, p1, nk, tq))

            def combine(n):
                for qb, (z, p0, p1, nk, tq) in enumerate(soft[n]):
                    V(vec.reciprocal, st[:, z:z + 2], st[:, z + 4:z + 6], w=[tq])
                    V(vec.tensor_tensor, st[:, z + 6:z + 7], st[:, z + 1:z + 2], nlam, ALU.mult)
                    V(vec.tensor_scalar, p1[:, 0:nk], p1[:, 0:nk], st[:, z + 6:z + 7], None, ALU.mult)
                    t = V(vec.scalar_tensor_tensor, out=p0[:, 0:nk], in0=p0[:, 0:nk], scalar=st[:, z:z + 1],
                          in1=p1[:, 0:nk], op0=ALU.mult, op1=ALU.add)
                    p1_rel[qb] = [t]
                soft[n] = t

            def turn(n):
                h, s = jobs[n]
                nkt = 4 if s == 0 else 2
                for qb in range(2):
                    i0 = (n % 3) * 2 + qb
                    b, br, bi = ps.take()
                    for k in range(nkt):
                        tp = transp(b[:, k * 128:k * 128 + 128], PA[i0][:, k * 128:k * 128 + 128],
                                    w=[soft[n]] + br, sig=k == nkt - 1)
                    p0_rel[i0] = [tp]
                    t = A(act.copy, aT[n % 2][:, 0:nkt, qb * 128:qb * 128 + 128],
                          b[:, 0:nkt * 128].rearrange("p (a b) -> p a b", b=128), w=[tp] + at_rel[n % 2])
                    ps.give(bi, t)
                turned[n] = t

            def apply(n):
                h, s = jobs[n]
                kt0, nkt = (0, 4) if s == 0 else (2, 2)
                b, br, bi = ps.take()
                tp = group(b[:, 0:256], [(Vt[:, kt0 + k, h * 128:h * 128 + 128], aT[n % 2][:, k, :])
                                         for k in range(nkt)], w=[turned[n], v_tok] + br)
                at_rel[n % 2] = [tp]
                t = A(act.copy, qT[:, h, s * 256:s * 256 + 256], b[:, 0:256], w=[tp])
                ps.give(bi, t)

            N = len(jobs)
            for n in range(N + 3):
                if n < N:
                    scores(n)
                if 0 <= n - 2 < N:
                    turn(n - 2)
                if n < N:
                    combine(n)
                if 0 <= n - 3 < N:
                    apply(n - 3)
            at_tok = A.last
            for h in range(8):
                q, r, qi = rot.take()
                t = A(act.activation, q[:, 0:qT_], qT[:, h, 0:qT_], ACT.Square, w=r)
                b, br, bi = ps.take()
                tp = group(b[:, 0:qT_], [(ones, q[:, 0:qT_])], w=[t] + br)
                t = A(act.activation, q[:, 0:qT_], b[:, 0:qT_], ACT.Sqrt, scale=1.0 / 128, bias=eps[:, :], w=[tp])
                ps.give(bi, t)
                V(vec.reciprocal, q[:, 0:qT_], q[:, 0:qT_], w=[t])
                an_tok = V(vec.scalar_tensor_tensor, out=qT[:, h, 0:qT_], in0=qT[:, h, 0:qT_], scalar=subg,
                           in1=q[:, 0:qT_], op0=ALU.mult, op1=ALU.mult)
                rot.give(qi, an_tok)
            frT = Vt[:, 0:2, :].rearrange("p a (b t) -> p (a b) t", t=512)
            fr_free = P.last
            cs = CA[:, 896:1408].rearrange("p (a b) -> p a b", b=256)
            ss = CA[:, 1408:1920].rearrange("p (a b) -> p a b", b=256)
            for s in range(len(segs)):
                for g in range(4):
                    b, br, bi = ps.take()
                    for tt in range(2):
                        tp = group(b[:, tt * 256:tt * 256 + 256],
                                   [(fT[:, g, s * 256 + tt * 128:s * 256 + tt * 128 + 128], CA[:, 640:896])],
                                   w=[f_tok] + br)
                    r, rr, ri = rot.take()
                    t = A(act.copy, r[:, :], b[:, :], w=[tp] + rr)
                    ps.give(bi, t)
                    b, br, bi = ps.take()
                    tp = group(b[:, 0:256], [(r[:, 0:128], cs[:, 0, :]), (r[:, 128:256], ss[:, 0, :]),
                                             (r[:, 256:384], cs[:, 1, :]), (r[:, 384:512], ss[:, 1, :])],
                               w=[t] + br)
                    rot.give(ri, tp)
                    fr_tok = A(act.copy, frT[:, g, s * 256:s * 256 + 256], b[:, 0:256], w=[tp, fr_free])
                    ps.give(bi, fr_tok)
            T = qT_
            for i in range(3):
                pool.rel[i] = [P.last, A.last, V.last]
            sp = Splits(pool, units("gate"), 2)
            mt = []
            for jj in range(4):
                for q in range(2):
                    j = 2 * jj + q
                    cq = slice(q * 128, q * 128 + 128)
                    b, br, bi = ps.take()
                    t = tiles(b[:, 0:T], T, MUH, MUL, br)
                    ga, gr, gi = rot.take()
                    t = A(act.activation, ga[:, 0:T], b[:, 0:T], ACT.Sigmoid, bias=col(f"bg{l}", j, 1), w=[t] + gr)
                    ps.give(bi, t)
                    b, br, bi = ps.take()
                    t = tiles(b[:, 0:T], T, MUH, MUL, br)
                    gf, gr, gj = rot.take()
                    t = A(act.activation, gf[:, 0:T], b[:, 0:T], ACT.Sigmoid, bias=col(f"bg{l}", 8 + j, 1),
                          w=[t] + gr)
                    ps.give(bi, t)
                    if q == 0:
                        w2, t2, s2 = weight(("wbr", l, jj), 3072)
                        w2 = w2.rearrange("p (k n) -> p k n", k=12)
                    b, br, bi = ps.take()
                    tp = group(b[:, 0:T], [(w2[:, k, cq], qT[:, k, 0:T]) for k in range(8)], w=[t2, an_tok] + br)
                    V(vec.tensor_tensor, ga[:, 0:T], b[:, 0:T], ga[:, 0:T], ALU.mult, w=[tp, t])
                    ps.give(bi, V.last)
                    b, br, bi = ps.take()
                    tp = group(b[:, 0:T], [(w2[:, 8 + k, cq], frT[:, k, 0:T]) for k in range(4)], w=[fr_tok] + br)
                    V(vec.tensor_tensor, gf[:, 0:T], b[:, 0:T], gf[:, 0:T], ALU.mult, w=[tp])
                    ps.give(bi, V.last)
                    m_tok = V(vec.tensor_tensor, ga[:, 0:T], ga[:, 0:T], gf[:, 0:T], ALU.add)
                    rot.give(gj, m_tok)
                    m_tok = parts(MGH[:, j, 0:T], MGL[:, j, 0:T], ga[:, 0:T], [m_tok])()
                    mt.append(m_tok)
                    rot.give(gi, m_tok)
                    filler(8)
                used(s2, P.last)
            u_rel[0] = P.last
            for j in range(8):
                b, br, bi = ps.take()
                tp = tiles(b[:, 0:T], T, MGH, MGL, br, mt)
                x_tok = add_x(j, b, ml[:, :, 40:48], segs, [tp])
                ps.give(bi, x_tok)
                square(j, T)

        fill[0] = layer_mod(0, 0, 1)
        for ch in (1, 2, 3):
            if ch == 2:
                drain_fill()
                fill[0] = layer_mod(0, 2, 3)
                filler(5)
                continue
            wc, wt, slot = weight(("wmod", 0, ch), 4096)
            wc = wc.rearrange("p (k n) -> p k n", k=8)
            b, br, bi = ps.take()
            for q in range(4):
                t = group(b[:, 2 * q:2 * q + 2], [(wc[:, k, q * 128:q * 128 + 128], SC[:, 0:2, k])
                                                  for k in range(8)], w=[wt, sc_tok] + br)
            used(slot, t)
            filler(12)
            for c in range(2):
                t = V(vec.tensor_tensor, M[:, 0, c, ch * 4:ch * 4 + 4], b[:, c:8:2], col("bmod0", ch * 4, 4),
                      ALU.add, w=[t])
            ps.give(bi, t)
        drain_fill()
        fill[0] = layer_mod(0, 4, 18)
        ffn(0, 0, BOTH)
        drain_fill()
        fill[0] = layer_mod(1, 0, 18)
        mixer(0)
        ffn(0, 1, BOTH)
        drain_fill()
        fill[0] = ada_mod()
        ffn(1, 0, BOTH)
        drain_fill()
        mixer(1)
        ffn(1, 1, LAT)
        norm(col("fin"), None, None, LAT)
        for k in range(8):
            x_tok = V(vec.tensor_copy, X[:, k, 0:256], U[:, k, 0:256], w=[A.last])
        u_rel[0] = P.last
        S.dma(nc.sync.dma_start, CA[:, :], c2_d, s_c2, w=[P.last, V.last])
        c2t = (s_c2, 16)
        V.wait(c2t)
        P.wait(c2t)
        off[0] = 0
        qf = big(1024, 4, 256)
        kf = big(1024, 4, 256)
        ktok = big(1024, 2, 512)
        vtok = big(2048, 2, 1024)
        zf = big(1024, 4, 256)
        intra = big(4096, 8, 512)
        inv = off[0]
        LT = big(1536, 3, 512)
        TA = big(1536, 3, 512)
        TT = big(1536, 3, 512)
        UU = [big(512) for _ in range(3)]
        off[0] = max(off[0], inv + 4096 + 1024)
        uv = big(2048, 2, 2, 512)
        SP = big(2048, 4, 512)
        KD = [a_[:, :] for a_ in acc.tiles]
        kb = SP.rearrange("p a (b t) -> p (a b) t", t=256)
        oaT = big(1024, 4, 256)
        wT = X[:, :, 256:512]
        qg = U[:, :, 256:512]
        neg = CA[:, 0:256].rearrange("p (d i) -> p d i", d=2)
        strict = CA[:, 256:512].rearrange("p (d i) -> p d i", d=2)
        lvl = CA[:, 512:2048].rearrange("p (l d i) -> p l d i", l=6, d=2)
        CT = big(640, 2, 5, 64)
        EX = big(32, 8, 4)
        XP = Pool([big(260) for i in range(2)])
        R2 = big(256)[0:64, :]
        assert off[0] <= 24000, off[0]
        for xp in XP.tiles:
            V(vec.memset, xp[:, 0:2], 0.0)
            V(vec.memset, xp[:, 258:260], 0.0)
        rows8 = uv.rearrange("p a b c -> p (a b c)")[0:64, :].rearrange("p (r t) -> p r t", t=256)
        R = [rows8[:, i, :] for i in range(2)] + [R2] + [rows8[:, i, :] for i in range(2, 8)] \
            + [RS[0:64, 0:256], RS[0:64, 256:512]]
        m2 = M2[:, :].rearrange("p (a c k) -> p a c k", c=1, k=8)
        ut = norm(col("nmix"), m2[:, 1], m2[:, 0], LAT)

        def conv_tile(wc, q, wt, ck, j, dst, head_norm, scl):
            b, br, bi = ps.take()
            t = group(b[:, 0:256], [(wc[:, k, q * 128:q * 128 + 128], U[:, k, 0:256]) for k in range(8)],
                      w=[wt] + br, wk=ut)
            xp, xr, xi = XP.take()
            t = A(act.copy, xp[:, 2:258], b[:, 0:256], w=[t] + xr)
            ps.give(bi, t)
            r, rr, ri = rot.take()
            V(vec.tensor_scalar, r[:, 0:256], xp[:, 0:256], col(ck, j * 5, 1), None, ALU.mult, w=[t] + rr)
            for i in range(1, 5):
                t = V(vec.scalar_tensor_tensor, out=r[:, 0:256], in0=xp[:, i:i + 256],
                      scalar=col(ck, j * 5 + i, 1), in1=r[:, 0:256], op0=ALU.mult, op1=ALU.add)
            XP.give(xi, t)
            t = A(act.activation, dst, r[:, 0:256], ACT.Silu, w=[t])
            if head_norm:
                t = A(act.activation, r[:, 0:256], dst, ACT.Square)
                yield
                b, br, bi = ps.take()
                t = group(b[:, 0:256], [(bones, r[:, 0:256])], w=[t] + br)
                t = A(act.activation, r[:, 256:512], b[:, 0:256], ACT.Sqrt, bias=eps[:, :], w=[t])
                ps.give(bi, t)
                V(vec.reciprocal, r[:, 256:512], r[:, 256:512], w=[t])
                t = V(vec.scalar_tensor_tensor, out=dst, in0=dst, scalar=scl, in1=r[:, 256:512],
                      op0=ALU.mult, op1=ALU.mult)
            elif scl != 1.0:
                t = V(vec.tensor_scalar, dst, dst, scl, None, ALU.mult, w=[t])
            rot.give(ri, t)
            done[0] = t

        done = [None]

        def to_tokens(src, dst, w):
            for tt in range(2):
                b, br, bi = ps.take()
                for f in range(4):
                    tp = transp(b[:, f * 128:f * 128 + 128], src[:, f, tt * 128:tt * 128 + 128],
                                w=w + br, sig=f == 3)
                t = A(act.copy, dst(tt), b[:, :] if dst(tt).free_size() == 512 and len(dst(tt).shape) == 2
                      else b[:, :].rearrange("p (h e) -> p h e", e=64), w=[tp])
                ps.give(bi, t)
            return t

        def gate_rows(kb_, dst, wc, wt):
            b, br, bi = ps.take()
            t = group(b[0:64, 0:256], [(wc[:, k, kb_ * 64:kb_ * 64 + 64], U[:, k, 0:256]) for k in range(8)],
                      w=[wt] + br, wk=ut)
            return b[0:64, 0:256], t, bi

        def softplus_rows(dst, src, tmp):
            V(vec.tensor_scalar, tmp, src, -1.0, None, ALU.mult)
            t = V(vec.tensor_tensor, tmp, tmp, src, ALU.min)
            A(act.activation, tmp, tmp, ACT.Exp, w=[t])
            t = A(act.activation, tmp, tmp, ACT.Ln, bias=1.0)
            V(vec.scalar_tensor_tensor, out=dst, in0=src, scalar=0.0, in1=tmp, op0=ALU.max, op1=ALU.add, w=[t])

        def scan(dst, src, op):
            for dr in range(2):
                p = slice(32 * dr, 32 * dr + 32)
                for n in range(4):
                    s, d_ = src[p, 64 * n:64 * n + 64], dst[p, 64 * n:64 * n + 64]
                    if dr:
                        s, d_ = s[:, ::-1], d_[:, ::-1]
                    if op is ALU.add:
                        V(vec.tensor_tensor_scan, d_, s, s, 0.0, ALU.add, ALU.bypass)
                    else:
                        V(vec.tensor_tensor_scan, d_, s, s, -3e38, ALU.max, ALU.max)

        def last_of(row, dr):
            r = row[32 * dr:32 * dr + 32, :].rearrange("p (n l) -> p n l", l=64)
            return r[:, :, 63:64] if dr == 0 else r[:, :, 0:1]

        def chunks(row, dr):
            return row[32 * dr:32 * dr + 32, :].rearrange("p (n l) -> p n l", l=64)

        def to_cols(rows, w):
            for tt in range(2):
                b, br, bi = ps.take()
                for i, r in enumerate(rows):
                    tp = transp(b[:, i * 64:i * 64 + 64], r[:, tt * 128:tt * 128 + 128], w=w + br,
                                sig=i == len(rows) - 1)
                t = A(act.copy, CT[:, tt, 0:len(rows), :],
                      b[:, 0:64 * len(rows)].rearrange("p (a b) -> p a b", b=64), w=[tp])
                ps.give(bi, t)
            return t

        def row_all(out, row, dr, h, w, sig=True):
            r = 32 * dr + h
            return P(pe.matmul, out, CC[0:64, r:r + 1].to_broadcast([64, 128]), row, start=True, stop=True,
                     skip_group_check=True, w=w, sig=sig)

        def row_pair(out, row, dr, f, w, sig=True):
            r = 32 * dr + 2 * f
            P(pe.matmul, out[0:64], CC[0:64, r:r + 1].to_broadcast([64, 64]), row, start=True,
              stop=True, skip_group_check=True, w=w, sig=False)
            return P(pe.matmul, out[64:128], CC[0:64, r + 1:r + 2].to_broadcast([64, 64]), row, start=True,
                     stop=True, skip_group_check=True, sig=sig)

        def decay_of(h, b, bi, ci, tp):
            r, rr, ri = rot.take()
            for dr in range(2):
                for tt in range(2):
                    o = dr * 256 + tt * 128
                    t = V(vec.scalar_tensor_tensor, out=r[:, o:o + 128], in0=b[:, o:o + 128],
                          scalar=CT[:, tt, ci, 32 * dr + h:32 * dr + h + 1], in1=neg[:, dr, :],
                          op0=ALU.subtract, op1=ALU.add, w=[tp] + rr)
            ps.give(bi, t)
            t = A(act.activation, r[:, :], r[:, :], ACT.Exp, w=[t])
            return r, t, ri

        def scaled_pairs(dst, src, row, w, wd):
            for f in range(4):
                b, br, bi = ps.take()
                for dr in range(2):
                    tp = row_pair(b[:, dr * 256:dr * 256 + 256], row, dr, f, w + br, sig=dr == 1)
                for dr in range(2):
                    t = V(vec.tensor_tensor, dst[:, 2 * f + dr, :], b[:, dr * 256:dr * 256 + 256], src[:, f, :],
                          ALU.mult, w=[tp] + wd)
                ps.give(bi, t)
            return t

        gw, gt, gslot = weight(("gates2",), 2048)
        gw = gw.rearrange("p (k n) -> p k n", k=8)
        rw = COLS["rows"][0]
        rows = [K[0:64, rw + i:rw + i + 1] for i in range(4)]
        bg, t, bi = gate_rows(0, None, gw, gt)
        V(vec.tensor_scalar, R[0], bg, rows[1], None, ALU.add, w=[t])
        ps.give(bi, V.last)
        bg, t, bi = gate_rows(1, None, gw, gt)
        t = A(act.activation, R[1], bg, ACT.Sigmoid, w=[t])
        ps.give(bi, t)
        for i, dd in ((2, R[9]), (3, R[10])):
            bg, t, bi = gate_rows(i, None, gw, gt)
            V(vec.tensor_scalar, dd, bg, rows[i], None, ALU.add, w=[t])
            ps.give(bi, V.last)
        used(gslot, P.last)
        softplus_rows(R[2], R[0], R[3])
        t = A(act.activation, st[0:64, 8:9], rows[0], ACT.Exp)
        V(vec.tensor_scalar, R[0], R[2], st[0:64, 8:9], -1.0, ALU.mult, ALU.mult, w=[t])
        scan(R[2], R[0], ALU.add)
        for dr in range(2):
            V(vec.tensor_tensor, chunks(R[3], dr), last_of(R[2], dr).to_broadcast([32, 4, 64]), chunks(R[2], dr),
              ALU.subtract)
        A(act.activation, R[4], R[2], ACT.Exp, w=[V.last])
        t = A(act.activation, R[3], R[3], ACT.Exp)
        V(vec.tensor_tensor, R[5], R[1], R[4], ALU.mult, w=[t])
        r_tok = V.last
        rows_done = [V.last, A.last]
        for c, (dst, hn, scl) in enumerate(((qf, True, 0.125), (kf, True, 1.0), (None, False, 1.0))):
            wc, wt, slot = weight(("win2", c * 512, 512), 4096)
            wc = wc.rearrange("p (k n) -> p k n", k=8)
            d_ = zf if dst is None else dst
            interleave((conv_tile(wc, q, wt, "cva", c * 4 + q, d_[:, q, :], hn, scl) for q in range(4)), 2)
            t = done[0]
            used(slot, P.last)
            if c == 1:
                to_tokens(kf, lambda tt: ktok[:, tt, :], [t])
            if c == 2:
                to_tokens(zf, lambda tt: vtok[:, tt, 0:512], [t])
        zt_rel = P.last
        wc, wt, slot = weight(("win2", 1536, 512), 4096)
        wc = wc.rearrange("p (k n) -> p k n", k=8)
        for q in range(4):
            b, br, bi = ps.take()
            t = group(b[:, 0:256], [(wc[:, k, q * 128:q * 128 + 128], U[:, k, 0:256]) for k in range(8)],
                      w=[wt] + br)
            t = A(act.activation, zf[:, q, :], b[:, 0:256], ACT.Silu, w=[t, zt_rel])
            ps.give(bi, t)
        used(slot, P.last)
        ct_tok = to_cols([R[2], R[1], R[5], R[3]], rows_done)
        V.wait(ct_tok)

        qg_tok = scaled_pairs(qg, qf, R[4], rows_done, [u_rel[0], A.last])
        kb_tok = scaled_pairs(kb, kf, R[1], rows_done, [])
        b, br, bi = ps.take()
        V(vec.tensor_copy, R[6][:, 0:4], R[4][:, 0:256:64])
        V(vec.tensor_copy, R[6][0:32, 0:4], R[4][0:32, 63:256:64])
        for dr in range(2):
            for f in range(4):
                o = (dr * 4 + f) * 4
                tp = row_pair(b[:, o:o + 4], R[6][:, 0:4], dr, f, [V.last] + br, sig=dr == 1 and f == 3)
        ex_tok = V(vec.tensor_copy, EX[:, :, :], b[:, 0:32].rearrange("p (a n) -> p a n", n=4), w=[tp])
        ps.give(bi, ex_tok)

        def idx(h):
            return h // 2, slice(64 * (h % 2), 64 * (h % 2) + 64)

        slot_rel = [[None] for _ in range(3)]

        def invert(h):
            hh = h % 3
            f, pp = idx(h)
            b, br, bi = ps.take()
            for dr in range(2):
                tp = row_all(b[:, dr * 256:dr * 256 + 256], R[2], dr, h, [r_tok] + br, sig=dr == 1)
            bq, br, bqi = ps.take()
            for tt in range(2):
                tk = slice(tt * 128, tt * 128 + 128)
                tq = P(pe.matmul, bq[:, tk], kf[pp, f, tk], qf[pp, f, tk], start=True, stop=True,
                       skip_group_check=True, w=[qg_tok, kb_tok] + br, sig=tt == 1)
            dt_, dtt, ri = decay_of(h, b, bi, 0, tp)
            for dr in range(2):
                V(vec.tensor_tensor, intra[:, h, dr * 256:dr * 256 + 256], bq[:, 0:256],
                  dt_[:, dr * 256:dr * 256 + 256], ALU.mult, w=[tq, dtt])
            ps.give(bqi, V.last)
            bk, br, bki = ps.take()
            for dr in range(2):
                for tt in range(2):
                    tk = slice(tt * 128, tt * 128 + 128)
                    tp = P(pe.matmul, bk[:, dr * 256 + tt * 128:dr * 256 + tt * 128 + 128], kf[pp, f, tk],
                           kb[pp, 2 * f + dr, tk], start=True, stop=True, skip_group_check=True,
                           w=br, sig=dr == 1 and tt == 1)
            V(vec.tensor_tensor, dt_[:, :], bk[:, :], dt_[:, :], ALU.mult, w=[tp])
            ps.give(bki, V.last)
            lt = LT[:, hh, :].rearrange("p (d t i) -> p d t i", d=2, t=2)
            tt4 = TT[:, hh, :].rearrange("p (d t i) -> p d t i", d=2, t=2)
            for dr in range(2):
                V(vec.tensor_tensor, lt[:, dr], dt_[:, dr * 256:dr * 256 + 256].rearrange(
                    "p (t i) -> p t i", t=2), strict[:, dr, :].unsqueeze(1).to_broadcast([128, 2, 128]),
                  ALU.mult, w=slot_rel[hh])
            lt_tok = V.last
            rot.give(ri, lt_tok)
            for dr in range(2):
                V(vec.tensor_tensor, tt4[:, dr], lt[:, dr],
                  lvl[:, 0, dr, :].unsqueeze(1).to_broadcast([128, 2, 128]), ALU.mult)
            t1_ = V(vec.tensor_tensor, TT[:, hh, :].rearrange("p (a i) -> p a i", i=128),
                    ident.unsqueeze(1).to_broadcast([128, 4, 128]),
                    TT[:, hh, :].rearrange("p (a i) -> p a i", i=128), ALU.subtract)
            yield
            b, br, bi = ps.take()
            for a in range(4):
                tp = transp(b[:, a * 128:a * 128 + 128], TT[:, hh, a * 128:a * 128 + 128],
                            w=[t1_] + br, sig=a == 3)
            t_ = A(act.copy, TA[:, hh, :], b[:, :], w=[tp])
            ps.give(bi, t_)
            t2_ = None
            for lv in range(1, 6):
                r, rr, ri = rot.take()
                rv = r[:, :].rearrange("p (d t i) -> p d t i", d=2, t=2)
                for dr in range(2):
                    tm = G(nc.gpsimd.tensor_tensor, rv[:, dr], lt[:, dr],
                           lvl[:, lv, dr, :].unsqueeze(1).to_broadcast([128, 2, 128]), ALU.mult,
                           w=rr + [lt_tok])
                yield
                b, br, bi = ps.take()
                for a in range(4):
                    s_ = slice(a * 128, a * 128 + 128)
                    tp = P(pe.matmul, b[:, s_], r[:, s_], TA[:, hh, s_], start=True, stop=True,
                           skip_group_check=True, w=[tm, t_] + br, sig=a == 3)
                rot.give(ri, tp)
                uu = UU[hh]
                tu = A(act.copy, uu, b[:, :], w=[tp])
                ps.give(bi, tu)
                yield
                if lv < 5:
                    b, br, bi = ps.take()
                    for a in range(4):
                        s_ = slice(a * 128, a * 128 + 128)
                        tp = P(pe.matmul, b[:, s_], TT[:, hh, s_], uu[:, s_], start=True, stop=True,
                               skip_group_check=True, w=[tu, t2_] + br, sig=a == 3)
                    t_ = V(vec.tensor_tensor, TA[:, hh, :], TA[:, hh, :], b[:, :], ALU.subtract, w=[tp])
                    ps.give(bi, t_)
                b2, br2, bi2 = ps.take()
                for a in range(4):
                    s_ = slice(a * 128, a * 128 + 128)
                    tp2 = P(pe.matmul, b2[:, s_], uu[:, s_], TT[:, hh, s_], start=True, stop=True,
                            skip_group_check=True, w=[tu, t2_] + br2, sig=a == 3)
                t2_ = V(vec.tensor_tensor, TT[:, hh, :], TT[:, hh, :], b2[:, :], ALU.subtract, w=[tp2])
                ps.give(bi2, t2_)
            r, rr, ri = rot.take()
            rhs = r[:, :].rearrange("p (x d t e) -> p x d t e", x=2, d=2, t=2)
            for dr in range(2):
                c_ = 32 * dr + h
                for tt in range(2):
                    V(vec.tensor_scalar, rhs[:, 0, dr, tt, :], vtok[:, tt, h * 64:h * 64 + 64],
                      CT[:, tt, 1, c_:c_ + 1], None, ALU.mult, w=rr)
                    tr = V(vec.tensor_scalar, rhs[:, 1, dr, tt, :], ktok[:, tt, h * 64:h * 64 + 64],
                           CT[:, tt, 2, c_:c_ + 1], None, ALU.mult)
            yield
            b, br, bi = ps.take()
            b2, br2, bi2 = ps.take()
            for dr in range(2):
                for tt in range(2):
                    a = dr * 2 + tt
                    s_ = slice(a * 128, a * 128 + 128)
                    P(pe.matmul, b[:, a * 64:a * 64 + 64], TT[:, hh, s_], rhs[:, 0, dr, tt, :], start=True,
                      stop=True, skip_group_check=True, w=[tr, t2_] + br, sig=False)
                    tp = P(pe.matmul, b2[pp, s_], rhs[:, 1, dr, tt, :], TT[:, hh, s_], start=True,
                           stop=True, skip_group_check=True, w=br2, sig=a == 3)
            rot.give(ri, tp)
            t = A(act.copy, uv[:, :, :, h * 64:h * 64 + 64].rearrange("p d t e -> p (d t) e"),
                  b[:, 0:256].rearrange("p (a e) -> p a e", e=64), w=[tp])
            ps.give(bi, t)
            t = A(act.copy, wT[pp, 2 * f:2 * f + 2, :], b2[pp, :].rearrange("p (d t) -> p d t", d=2))
            ps.give(bi2, t)
            slot_rel[hh] = [tp, t]

        A.wait(x_tok, V.last)
        interleave((invert(h) for h in range(8)), 3, 3)
        uv_tok = A.last
        V(vec.memset, SP[:, 0, :], 0.0, w=[P.last])
        kd_rel = [[None], [None]]

        def kend(s, ci):
            kd = KD[s % 2]
            for dr in range(2):
                n = s if dr == 0 else 3 - s
                tt, pb = n // 2, slice(64 * (n % 2), 64 * (n % 2) + 64)
                V(vec.tensor_tensor, kd[pb, :].rearrange("p (h e) -> p h e", e=64),
                  ktok[pb, tt, :].rearrange("p (h e) -> p h e", e=64),
                  CT[pb, tt, ci, 32 * dr:32 * dr + 8].unsqueeze(2).to_broadcast([64, 8, 64]), ALU.mult,
                  w=kd_rel[s % 2])
            return kd

        scan_tok = [None]

        def scan_a():
            for s in range(4):
                kd = kend(s, 3)
                if s > 0:
                    for par in range(2):
                        b, br, bi = ps.take()
                        for dr in range(2):
                            n = s if dr == 0 else 3 - s
                            pb = slice(64 * (n % 2), 64 * (n % 2) + 64)
                            pp = slice(64 * par, 64 * par + 64)
                            for f in range(4):
                                tp = P(pe.matmul, b[pb, f * 64:f * 64 + 64], wT[pp, 2 * f + dr, 64 * n:64 * n + 64],
                                       SP[pp, s, (dr * 4 + f) * 64:(dr * 4 + f) * 64 + 64], start=True, stop=True,
                                       skip_group_check=True, w=[V.last, uv_tok] + br, sig=f == 3)
                        for dr in range(2):
                            n = s if dr == 0 else 3 - s
                            tt, pb = n // 2, slice(64 * (n % 2), 64 * (n % 2) + 64)
                            uh = uv[pb, dr, tt, :].rearrange("p (f r e) -> p f r e", r=2, e=64)[:, :, par, :]
                            V(vec.tensor_tensor, uh, uh, b[pb, 0:256].rearrange("p (f e) -> p f e", e=64),
                              ALU.subtract, w=[tp])
                        ps.give(bi, V.last)
                yield
                if s < 3:
                    for dr in range(2):
                        b, br, bi = ps.take()
                        n = s if dr == 0 else 3 - s
                        tt, pb = n // 2, slice(64 * (n % 2), 64 * (n % 2) + 64)
                        for h in range(8):
                            f, pp = idx(h)
                            tp = P(pe.matmul, b[pp, f * 64:f * 64 + 64], kd[pb, h * 64:h * 64 + 64],
                                   uv[pb, dr, tt, h * 64:h * 64 + 64], start=True, stop=True,
                                   skip_group_check=True, w=[V.last, uv_tok] + br, sig=h == 7)
                        V(vec.tensor_tensor, SP[:, s + 1, dr * 256:dr * 256 + 256].rearrange("p (f e) -> p f e", e=64),
                          SP[:, s, dr * 256:dr * 256 + 256].rearrange("p (f e) -> p f e", e=64),
                          EX[:, dr * 4:dr * 4 + 4, n:n + 1].to_broadcast([128, 4, 64]), ALU.mult)
                        V(vec.tensor_tensor, SP[:, s + 1, dr * 256:dr * 256 + 256],
                          SP[:, s + 1, dr * 256:dr * 256 + 256], b[:, 0:256], ALU.add, w=[tp])
                        ps.give(bi, V.last)
                    kd_rel[s % 2] = [tp]
                yield
            scan_tok[0] = V.last


        SB = BIG[:, inv:inv + 4096].rearrange("p (s x) -> p s x", s=4)
        hbT = BIG[:, inv + 4096:inv + 5120].rearrange("p (f t) -> p f t", t=256)
        rowsb = BIG[0:64, inv + 4096:inv + 6144].rearrange("p (r t) -> p r t", t=256)
        RB = [rowsb[:, i, :] for i in range(2)] + [R2] + [rowsb[:, i, :] for i in range(2, 8)] + R[9:11]
        vau = vtok.rearrange("p t (h e) -> p t h e", e=128)

        def proj_b():
            for c, (dst, scl) in enumerate(((qf, 1.0), (kf, 0.125))):
                wc, wt, slot = weight(("win2", 2080 + c * 512, 512), 4096)
                wc = wc.rearrange("p (k n) -> p k n", k=8)
                for q in range(4):
                    yield from conv_tile(wc, q, wt, "cvb", c * 4 + q, dst[:, q, :], False, scl)
                    yield
                used(slot, P.last)
            kf_tok = done[0]
            wc, wt, slot = weight(("win2", 3104, 512), 4096)
            wc = wc.rearrange("p (k n) -> p k n", k=8)
            for tt in range(2):
                b, br, bi = ps.take()
                t = group(b[:, :], [(U[:, k, tt * 128:tt * 128 + 128], wc[:, k, :]) for k in range(8)],
                          w=[wt] + br)
                t = A(act.copy, vau[:, tt, :, 0:64], b[:, :].rearrange("p (h e) -> p h e", e=64), w=[t])
                ps.give(bi, t)
                V(vec.memset, vau[:, tt, :, 64:128], 1.0)
                yield
            used(slot, P.last)

        gb_tok = []
        MP = RB[10]

        def gates_b():
            V(vec.tensor_scalar, RB[0], RB[10], -1.0, None, ALU.mult)
            softplus_rows(RB[2], RB[0], RB[3])
            V(vec.tensor_scalar, RB[0], RB[2], -1.0, None, ALU.mult)
            scan(RB[1], RB[0], ALU.add)
            V(vec.tensor_tensor, RB[2], RB[9], RB[1], ALU.subtract)
            scan(RB[3], RB[2], ALU.max)
            V(vec.memset, MP[:, 0:16], 0.0)
            for s in range(4):
                for dr in range(2):
                    n = s if dr == 0 else 3 - s
                    p = slice(32 * dr, 32 * dr + 32)
                    lc = 64 * n + (63 if dr == 0 else 0)
                    V(vec.tensor_tensor, MP[p, 4 + n:5 + n], MP[p, n:n + 1], RB[3][p, lc:lc + 1], ALU.max)
                    V(vec.tensor_tensor, MP[p, 4 + n:5 + n], MP[p, 4 + n:5 + n], RB[1][p, lc:lc + 1], ALU.add)
                    nn = n + 1 if dr == 0 else n - 1
                    if 0 <= nn < 4:
                        V(vec.tensor_copy, MP[p, nn:nn + 1], MP[p, 4 + n:5 + n])

            def mb(o, p=slice(0, 64)):
                return MP[p, o:o + 4].unsqueeze(2).to_broadcast([p.stop - p.start, 4, 64])

            def ch(r, p=slice(0, 64)):
                return r[p, :].rearrange("p (n l) -> p n l", l=64)

            V(vec.tensor_tensor, ch(RB[3]), mb(0), ch(RB[3]), ALU.max)
            V(vec.tensor_tensor, ch(RB[4]), mb(0), ch(RB[3]), ALU.subtract)
            V(vec.tensor_tensor, RB[5], RB[1], RB[3], ALU.add)
            for dr in range(2):
                p = slice(32 * dr, 32 * dr + 32)
                V(vec.tensor_copy, MP[p, 8:12], last_of(RB[1], dr).rearrange("p n o -> p (n o)"))
            V(vec.tensor_tensor, MP[:, 12:16], MP[:, 8:12], MP[:, 4:8], ALU.subtract)
            V(vec.tensor_tensor, ch(RB[6]), mb(12), ch(RB[2]), ALU.add)
            V(vec.tensor_tensor, MP[:, 16:20], MP[:, 12:16], MP[:, 0:4], ALU.add)
            V(vec.tensor_scalar, RB[7], RB[3], -1.0, None, ALU.mult)
            V(vec.tensor_scalar, RB[8], RB[2], -1.0, None, ALU.mult)
            A(act.activation, RB[4], RB[4], ACT.Exp, w=[V.last])
            A(act.activation, RB[5], RB[5], ACT.Exp, scale=-1.0)
            A(act.activation, RB[6], RB[6], ACT.Exp)
            t = A(act.activation, MP[:, 20:24], MP[:, 16:20], ACT.Exp)
            gb_tok.extend([V.last, t])
            yield

        A.wait(P.last, V.last)
        V.wait(A.last)
        interleave([scan_a(), proj_b(), gates_b()], 3)
        sp_tok = scan_tok[0]
        for f in range(4):
            b, br, bi = ps.take()
            first = {0: True, 1: True}
            for par in range(2):
                h = 2 * f + par
                pp = slice(64 * par, 64 * par + 64)
                for tt in range(2):
                    for dr in range(2):
                        P(pe.matmul, b[pp, tt * 128:tt * 128 + 128], uv[:, dr, tt, h * 64:h * 64 + 64],
                          intra[:, h, dr * 256 + tt * 128:dr * 256 + tt * 128 + 128],
                          start=(tt == 0 and dr == 0), stop=False, skip_group_check=True,
                          w=[sp_tok] + br, sig=False)
                for dr in range(2):
                    for n in range(4):
                        s = n if dr == 0 else 3 - n
                        if s == 0:
                            continue
                        o = (dr * 4 + f) * 64
                        tp = P(pe.matmul, b[pp, 64 * n:64 * n + 64], SP[pp, s, o:o + 64],
                               qg[pp, 2 * f + dr, 64 * n:64 * n + 64], start=False, stop=True,
                               skip_group_check=True)
            r, rr, ri = rot.take()
            A(act.copy, oaT[:, f, :], b[:, 0:256], w=[tp] + rr)
            t = A(act.activation, r[:, 0:256], oaT[:, f, :], ACT.Square)
            ps.give(bi, t)
            b, br, bi = ps.take()
            t = group(b[:, 0:256], [(bones, r[:, 0:256])], w=[t] + br)
            t = A(act.activation, r[:, 256:512], b[:, 0:256], ACT.Sqrt, scale=1.0 / 64, bias=eps[:, :], w=[t])
            ps.give(bi, t)
            V(vec.reciprocal, r[:, 256:512], r[:, 256:512], w=[t])
            V(vec.scalar_tensor_tensor, out=oaT[:, f, :], in0=oaT[:, f, :], scalar=col("gdn"),
              in1=r[:, 256:512], op0=ALU.mult, op1=ALU.mult)
            V(vec.tensor_tensor, oaT[:, f, :], oaT[:, f, :], zf[:, f, :], ALU.mult)
            rot.give(ri, V.last)
        a_done = [V.last, P.last, A.last]

        to_tokens(kf, lambda tt: ktok[:, tt, :], [done[0]])
        wc, wt, slot = weight(("win2", 3616, 512), 4096)
        wc = wc.rearrange("p (k n) -> p k n", k=8)
        for q in range(4):
            b, br, bi = ps.take()
            t = group(b[:, 0:256], [(wc[:, k, q * 128:q * 128 + 128], U[:, k, 0:256]) for k in range(8)],
                      w=[wt] + br)
            t = A(act.activation, zf[:, q, :], b[:, 0:256], ACT.Sigmoid, w=[t, a_done])
            ps.give(bi, t)
        used(slot, P.last)
        r_tok = gb_tok
        R = RB
        ct_tok = to_cols([R[8], R[6]], r_tok)
        V.wait(ct_tok)
        qi_tok = scaled_pairs(qg, qf, R[4], r_tok, [])
        b, br, bi = ps.take()
        for dr in range(2):
            for f in range(4):
                o = (dr * 4 + f) * 4
                tp = row_pair(b[:, o:o + 4], MP[:, 20:24], dr, f, r_tok + br, sig=dr == 1 and f == 3)
        V(vec.tensor_copy, EX[:, :, :], b[:, 0:32].rearrange("p (a n) -> p a n", n=4), w=[tp])
        ps.give(bi, V.last)
        for h in range(8):
            f, pp = idx(h)
            b, br, bi = ps.take()
            for dr in range(2):
                tp = row_all(b[:, dr * 256:dr * 256 + 256], R[7], dr, h, r_tok + br, sig=dr == 1)
            dt_, dtt, ri = decay_of(h, b, bi, 0, tp)
            bq, br, bqi = ps.take()
            for tt in range(2):
                tk = slice(tt * 128, tt * 128 + 128)
                tp = P(pe.matmul, bq[:, tk], kf[pp, f, tk], qf[pp, f, tk], start=True, stop=True,
                       skip_group_check=True, w=[qi_tok] + br, sig=tt == 1)
            for dr in range(2):
                V(vec.tensor_tensor, intra[:, h, dr * 256:dr * 256 + 256], bq[:, 0:256],
                  dt_[:, dr * 256:dr * 256 + 256], ALU.mult, w=[tp, dtt])
            ps.give(bqi, V.last)
            rot.give(ri, V.last)
        V(vec.memset, SB[:, 0, :], 0.0)
        kd_rel = [[None], [None]]
        for s in range(3):
            kd = kend(s, 1)
            for dr in range(2):
                n = s if dr == 0 else 3 - s
                tt, pb = n // 2, slice(64 * (n % 2), 64 * (n % 2) + 64)
                b, br, bi = ps.take()
                for h in range(8):
                    f, pp = idx(h)
                    tp = P(pe.matmul, b[pp, f * 128:f * 128 + 128], kd[pb, h * 64:h * 64 + 64],
                           vau[pb, tt, h, :], start=True, stop=True, skip_group_check=True,
                           w=[V.last] + br, sig=h == 7)
                V(vec.tensor_tensor, SB[:, s + 1, dr * 512:dr * 512 + 512].rearrange("p (f e) -> p f e", e=128),
                  SB[:, s, dr * 512:dr * 512 + 512].rearrange("p (f e) -> p f e", e=128),
                  EX[:, dr * 4:dr * 4 + 4, n:n + 1].to_broadcast([128, 4, 128]), ALU.mult)
                V(vec.tensor_tensor, SB[:, s + 1, dr * 512:dr * 512 + 512],
                  SB[:, s + 1, dr * 512:dr * 512 + 512], b[:, :], ALU.add, w=[tp])
                ps.give(bi, V.last)
            kd_rel[s % 2] = [tp]
        sp_tok = V.last
        for f in range(4):
            bg, br, bgi = ps.take()
            for dr in range(2):
                tg = row_pair(bg[:, dr * 256:dr * 256 + 256], R[5], dr, f, r_tok + br, sig=dr == 1)
            for dr in range(2):
                b, br, bi = ps.take()
                for par in range(2):
                    h = 2 * f + par
                    pp = slice(64 * par, 64 * par + 64)
                    for x in range(2):
                        vs = slice(64 * x, 64 * x + 64)
                        for tt in range(2):
                            P(pe.matmul, b[pp, x * 256 + tt * 128:x * 256 + tt * 128 + 128], vau[:, tt, h, vs],
                              intra[:, h, dr * 256 + tt * 128:dr * 256 + tt * 128 + 128],
                              start=(x == 0 and tt == 0), stop=False, skip_group_check=True,
                              w=[sp_tok] + br, sig=False)
                        for n in range(4):
                            s = n if dr == 0 else 3 - n
                            if s == 0:
                                continue
                            o = dr * 512 + f * 128 + 64 * x
                            tp = P(pe.matmul, b[pp, x * 256 + 64 * n:x * 256 + 64 * n + 64],
                                   SB[pp, s, o:o + 64], qg[pp, 2 * f + dr, 64 * n:64 * n + 64],
                                   start=False, stop=True, skip_group_check=True)
                r, rr, ri = rot.take()
                t = A(act.activation, r[:, 0:256], b[:, 256:512], ACT.Abs, w=[tp] + rr)
                V(vec.tensor_tensor, r[:, 0:256], bg[:, dr * 256:dr * 256 + 256], r[:, 0:256], ALU.max,
                  w=[t, tg])
                V(vec.reciprocal, r[:, 0:256], r[:, 0:256])
                dst = hbT[:, f, :] if dr == 0 else r[:, 0:256]
                V(vec.tensor_tensor, dst, b[:, 0:256], r[:, 0:256], ALU.mult)
                ps.give(bi, V.last)
                if dr == 1:
                    V(vec.tensor_tensor, hbT[:, f, :], hbT[:, f, :], r[:, 0:256], ALU.add)
                rot.give(ri, V.last)
            ps.give(bgi, V.last)
            b, br, bi = ps.take()
            tp = group(b[:, 0:256], [(bones, hbT[:, f, :])], w=[V.last] + br)
            V(vec.scalar_tensor_tensor, out=hbT[:, f, :], in0=b[:, 0:256], scalar=-1.0 / 64, in1=hbT[:, f, :],
              op0=ALU.mult, op1=ALU.add, w=[tp])
            r, rr, ri = rot.take()
            t = A(act.activation, r[:, 0:256], hbT[:, f, :], ACT.Square, w=[V.last] + rr)
            tp = group(b[:, 256:512], [(bones, r[:, 0:256])], w=[t])
            t = A(act.activation, r[:, 256:512], b[:, 256:512], ACT.Sqrt, scale=1.0 / 64, bias=eps[:, :], w=[tp])
            ps.give(bi, t)
            V(vec.reciprocal, r[:, 256:512], r[:, 256:512], w=[t])
            V(vec.scalar_tensor_tensor, out=hbT[:, f, :], in0=hbT[:, f, :], scalar=col("mln", f, 1),
              in1=r[:, 256:512], op0=ALU.mult, op1=ALU.mult)
            V(vec.tensor_tensor, hbT[:, f, :], hbT[:, f, :], zf[:, f, :], ALU.mult)
            rot.give(ri, V.last)
        b_tok = V.last
        ym = BIG[:, 0:2048].rearrange("p (k t) -> p k t", t=256)
        for jj in range(4):
            w1, t1, s1 = weight(("gate2", jj), 4096)
            w2, t2, s2 = weight(("br2", jj), 2048)
            w1 = w1.rearrange("p (k n) -> p k n", k=8)
            w2 = w2.rearrange("p (k n) -> p k n", k=8)
            for q in range(2):
                j = 2 * jj + q
                gg = []
                for x in range(2):
                    b, br, bi = ps.take()
                    t = group(b[:, 0:256], [(w1[:, k, 256 * x + q * 128:256 * x + q * 128 + 128],
                                             U[:, k, 0:256]) for k in range(8)], w=[t1] + br)
                    g, gr, gi = rot.take()
                    t = A(act.activation, g[:, 0:256], b[:, 0:256], ACT.Sigmoid, w=[t] + gr)
                    ps.give(bi, t)
                    b, br, bi = ps.take()
                    src = oaT if x == 0 else hbT
                    tp = group(b[:, 0:256], [(w2[:, 4 * x + k, q * 128:q * 128 + 128], src[:, k, :])
                                             for k in range(4)], w=[t2, b_tok] + br)
                    V(vec.tensor_tensor, g[:, 0:256], b[:, 0:256], g[:, 0:256], ALU.mult, w=[tp, t])
                    ps.give(bi, V.last)
                    gg.append((g, gi))
                y_tok = V(vec.tensor_tensor, ym[:, j, :], gg[0][0][:, 0:256], gg[1][0][:, 0:256], ALU.add)
                for g, gi in gg:
                    rot.give(gi, y_tok)
            used(s1, P.last)
            used(s2, P.last)
        u_rel[0] = P.last
        for c in range(2):
            wc, wt, slot = weight(("wout2", c), 4096)
            wc = wc.rearrange("p (k n) -> p k n", k=8)
            for q in range(4):
                b, br, bi = ps.take()
                tp = group(b[:, 0:256], [(wc[:, k, q * 128:q * 128 + 128], ym[:, k, :]) for k in range(8)],
                           w=[wt, y_tok] + br)
                x_tok = add_x(4 * c + q, b, m2[:, 2], LAT, [tp])
                ps.give(bi, x_tok)
                square(4 * c + q, 256)
            used(slot, P.last)
        ut = norm(col("nffn"), m2[:, 4], m2[:, 3], LAT)
        V.wait(P.last)
        A.wait(V.last)
        lows = []
        for k in range(8):
            lows.append(parts(EH[:, k, :], EL[:, k, :], U[:, k, 0:256], [P.last]))
        for low in lows:
            et = low()
        off[0] = 0
        CB = big(32 * 256, 32, 256)
        rt = big(512)
        cmb = big(64, 2, 32)
        cT = big(256)
        wc, wt, slot = weight(("router",), 288)
        wc = wc.rearrange("p (k n) -> p k n", k=8)
        g8, g4 = CA[:, 2048:2056], CA[:, 2056:2060]
        for tt in range(2):
            b, br, bi = ps.take()
            tp = group(b[:, 0:36], [(U[:, k, tt * 128:tt * 128 + 128], wc[:, k, :]) for k in range(8)],
                       w=[wt] + br, wk=ut)
            L = rt[:, 0:36]
            V(vec.tensor_copy, L, b[:, 0:36], w=[tp])
            ps.give(bi, V.last)
            mx, nm, sm, pg = rt[:, 40:41], rt[:, 41:42], rt[:, 42:43], rt[:, 43:44]
            V(vec.tensor_reduce, mx, L[:, 0:4], AX.X, ALU.max)
            V(vec.tensor_scalar, nm, mx, -1.0, None, ALU.mult)
            t = A(act.activation, rt[:, 44:48], L[:, 0:4], ACT.Exp, bias=nm, accum_out=sm, w=[V.last])
            V(vec.reciprocal, pg, sm, w=[t])

            def first_max(dst, src, m, gn, n, tmp, tm):
                V(vec.tensor_scalar, tmp, src, m, None, ALU.is_equal)
                V(vec.tensor_tensor, tmp, tmp, gn, ALU.mult)
                V(vec.tensor_reduce, tm, tmp, AX.X, ALU.max)
                V(vec.tensor_scalar, dst, gn, tm, None, ALU.is_equal)

            gs = rt[:, 48:52]
            first_max(gs, L[:, 0:4], mx, g4, 4, rt[:, 52:56], rt[:, 56:57])
            ing = rt[:, 64:72]
            V(vec.tensor_scalar, ing, L[:, 4:12], gs[:, 0:1], None, ALU.mult)
            for g in range(1, 4):
                V(vec.scalar_tensor_tensor, out=ing, in0=L[:, 4 + 8 * g:12 + 8 * g], scalar=gs[:, g:g + 1],
                  in1=ing, op0=ALU.mult, op1=ALU.add)
            v1, v2, o1, o2 = rt[:, 72:73], rt[:, 73:74], rt[:, 80:88], rt[:, 88:96]
            V(vec.tensor_reduce, v1, ing, AX.X, ALU.max)
            first_max(o1, ing, v1, g8, 8, rt[:, 96:104], rt[:, 104:105])
            rest = rt[:, 112:120]
            V(vec.scalar_tensor_tensor, out=rest, in0=o1, scalar=-3.0e38, in1=ing, op0=ALU.mult, op1=ALU.add)
            V(vec.tensor_reduce, v2, rest, AX.X, ALU.max)
            first_max(o2, rest, v2, g8, 8, rt[:, 96:104], rt[:, 104:105])
            e_, d1, w1_, w2_ = rt[:, 120:121], rt[:, 121:122], rt[:, 122:123], rt[:, 123:124]
            V(vec.tensor_tensor, e_, v2, v1, ALU.subtract)
            t = A(act.activation, e_, e_, ACT.Exp, w=[V.last])
            V(vec.tensor_scalar, d1, e_, 1.0, None, ALU.add, w=[t])
            V(vec.reciprocal, d1, d1)
            V(vec.tensor_tensor, w1_, d1, pg, ALU.mult)
            V(vec.tensor_tensor, w2_, w1_, e_, ALU.mult)
            V(vec.tensor_scalar, o1, o1, w1_, None, ALU.mult)
            V(vec.scalar_tensor_tensor, out=o1, in0=o2, scalar=w2_, in1=o1, op0=ALU.mult, op1=ALU.add)
            for g in range(4):
                V(vec.tensor_scalar, cmb[:, tt, 8 * g:8 * g + 8], o1, gs[:, g:g + 1], None, ALU.mult)
            b, br, bi = ps.take()
            tp = transp(b[0:32, 0:128], cmb[:, tt, :], w=[V.last] + br)
            t = A(act.copy, cT[0:32, tt * 128:tt * 128 + 128], b[0:32, 0:128], w=[tp])
            ps.give(bi, t)
        used(slot, P.last)
        u_rel[0] = [P.last, A.last, V.last]
        for e2 in range(16):
            b, br, bi = ps.take()
            for x in range(2):
                e_ = 2 * e2 + x
                tp = P(pe.matmul, b[:, x * 256:x * 256 + 256], CC[0:32, e_:e_ + 1].to_broadcast([32, 128]),
                       cT[0:32, 0:256], start=True, stop=True, skip_group_check=True, w=[t] + br, sig=x == 1)
            cb_tok = A(act.copy, CB[:, 2 * e2:2 * e2 + 2, :], b[:, :].rearrange("p (a t) -> p a t", a=2), w=[tp])
            ps.give(bi, cb_tok)
        accb = []
        for i in range(4):
            b, br, bi = ps.take()
            accb.append((b, br))
        pm = Pool([ps.tiles[(ps.i + i) % 7] for i in range(3)] + [NB])
        for i in range(3):
            pm.rel[i] = ps.rel[(ps.i + i) % 7]
        pm.rel[3] = [nb_rel[0]]
        accw = [r for _, r in accb]

        pool = Pool(ES)
        acts = Pool(EA)
        for i in range(3):
            acts.rel[i] = [u_rel[0]]
        for i in range(4):
            pool.rel[i] = [P.last]

        def units():
            for e_ in range(32):
                wc, wt, slot = weight(("eup", e_), 4096)
                wc = wc.rearrange("p (q x k n) -> p q x k n", q=2, x=2, k=8)
                for q in range(2):
                    for x in range(2):
                        yield wc[:, q, x], wt, slot if (q, x) == (1, 1) else None
                if e_:
                    yield from downs(e_ - 1)
            yield from downs(31)

        dn = [None]

        def downs(e_):
            if e_ % 2 == 0:
                dn[0] = weight(("edn", e_ // 2), 4096)
            wc, wt, slot = dn[0]
            wc = wc.rearrange("p (e q n) -> p e q n", e=2, q=2)
            for q in range(2):
                yield wc[:, e_ % 2, q:q + 1, :], wt, slot if (e_ % 2, q) == (1, 1) else None

        sp = Splits(pool, units(), 2)

        def down(e_, ah, al, ai, at):
            for q in range(2):
                wh, wl, t, wi = sp.get()
                for j in range(8):
                    o = (j % 2) * 256
                    js = slice(j * 128, j * 128 + 128)
                    P.wait(t, at, accw)
                    for n, (l_, r_) in enumerate(three(wh[:, 0, js], wl[:, 0, js], ah[:, q, :], al[:, q, :])):
                        tp = P(pe.matmul, accb[j // 2][0][:, o:o + 256], l_, r_,
                               start=(e_ == 0 and q == 0 and j % 2 == 0 and n == 0),
                               stop=(e_ == 31 and q == 1 and n == 2), skip_group_check=True,
                               sig=(j == 7 and n == 2))
                pool.give(wi, tp)
            acts.give(ai, tp)
            return tp

        pend = None
        for e_ in range(32):
            (ah, al), acr, ai = acts.take()
            for q in range(2):
                b, br, bi = pm.take()
                wh, wl, t, wi = sp.get()
                for k in range(8):
                    tp = group3(b[:, 0:256], three(wh[:, k, :], wl[:, k, :], EH[:, k, :], EL[:, k, :]),
                                k == 0, k == 7, [t, et] + br)
                pool.give(wi, tp)
                s, sr, si = rot.take()
                t = A(act.activation, s[:, 0:256], b[:, 0:256], ACT.Silu, w=[tp] + sr)
                pm.give(bi, t)
                V(vec.tensor_tensor, s[:, 0:256], s[:, 0:256], CB[:, e_, :], ALU.mult, w=[t, cb_tok])
                b, br, bi = pm.take()
                wh, wl, t, wi = sp.get()
                for k in range(8):
                    tp = group3(b[:, 0:256], three(wh[:, k, :], wl[:, k, :], EH[:, k, :], EL[:, k, :]),
                                k == 0, k == 7, [t] + br)
                pool.give(wi, tp)
                t = V(vec.tensor_tensor, s[:, 0:256], b[:, 0:256], s[:, 0:256], ALU.mult, w=[tp])
                pm.give(bi, t)
                at = parts(ah[:, q, :], al[:, q, :], s[:, 0:256], [t] + acr)()
                rot.give(si, at)
            if pend is not None:
                down(*pend)
            pend = (e_, ah, al, ai, at)
        tp = down(*pend)
        nb_rel[0] = pm.rel[3]
        for j in range(8):
            o = (j % 2) * 256
            x_tok = V(vec.scalar_tensor_tensor, out=X[:, j, 0:256], in0=accb[j // 2][0][:, o:o + 256],
                      scalar=m2[:, 5, 0, j:j + 1], in1=X[:, j, 0:256], op0=ALU.mult, op1=ALU.add, w=[tp])
            square(j, 256)
        u_rel[0] = P.last
        norm(col("fin2"), None, None, LAT)
        src = U
        S.dma(nc.sync.dma_start, out_d.rearrange("p (k t) -> p k t", k=8), src[:, :, 0:256], s_out,
              w=[V.last, A.last, P.last])
        S.wait((s_out, 16))

        block = ctx.enter_context(nc.Block())

        @block.sync
        def _(e):
            S.emit(e)

        @block.vector
        def _(e):
            V.emit(e)

        @block.gpsimd
        def _(e):
            G.emit(e)

        @block.scalar
        def _(e):
            A.emit(e)

        @block.tensor
        def _(e):
            P.emit(e)


def colv(v):
    return np.ascontiguousarray(v.reshape(-1, 128).T)


def tile(w, cs):
    return w.reshape(-1, 128, w.shape[-1])[:, :, cs].transpose(1, 0, 2)


def units4(w):
    return w.reshape(128, 8, 4, 128).transpose(0, 2, 1, 3)


def pack(key, I):
    k = key[0]
    if k == "x":
        x = I["x"][0].T.reshape(8, 128, 256)
        c = I["ctx"][0].T.reshape(8, 128, 256)
        return np.concatenate([x, c], axis=2).transpose(1, 0, 2)
    if k == "wmod":
        return tile(I["w_mod"][key[1]], slice(key[2] * 512, key[2] * 512 + 512))
    if k == "ada":
        return tile(I["ada_w_2"][0], slice(key[1] * 512, key[1] * 512 + 512))
    if k == "fin":
        w = I["ffn_w_in"][key[1], key[2]]
        c = [(key[3] + q) * 128 for q in range(key[4])]
        return np.stack([np.stack([tile(w, slice(o, o + 128)), tile(w, slice(DFF + o, DFF + o + 128))], axis=1)
                         for o in c], axis=1)
    if k == "fout":
        w = I["ffn_w_out"][key[1], key[2]][key[3] * 1408:key[3] * 1408 + 1408]
        return np.stack([tile(w, slice(j * 128, j * 128 + 128)) for j in (2 * key[4], 2 * key[4] + 1)], axis=1)
    if k == "win":
        return units4(tile(I["w_in"][key[1]], slice(key[2], key[2] + key[3])))
    if k == "winv":
        return tile(I["w_in"][key[1]], slice(key[2], key[2] + key[3]))
    if k == "wgate":
        c = 3584 + key[2] * 256
        w = I["w_in"][key[1]]
        return np.stack([tile(w, slice(o, o + 128)) for o in (c, c + 1024, c + 128, c + 1152)], axis=1)
    if k == "wbr":
        s = slice(key[2] * 256, key[2] * 256 + 256)
        return np.concatenate([tile(I["w_attn_out"][key[1]], s), tile(I["w_four_out"][key[1]], s)], axis=1)
    if k == "wo":
        return units4(tile(I["w_o"][key[1]], slice(key[2] * 512, key[2] * 512 + 512)))
    w2 = I["w_in_2"][0]
    if k == "win2":
        return tile(w2, slice(key[1], key[1] + key[2]))
    if k == "gates2":
        o = np.zeros((128, 8, 4, 64), np.float32)
        for kind, base in ((0, 2048), (1, 2056), (2, 4128), (3, 4136)):
            for dr in range(2):
                o[:, :, kind, 32 * dr:32 * dr + 8] = tile(w2, slice(base + 16 * dr, base + 16 * dr + 8))
        return o
    if k == "gate2":
        c = 4160 + key[1] * 256
        return np.concatenate([tile(w2, slice(c, c + 256)), tile(w2, slice(c + 1024, c + 1280))], axis=2)
    if k == "br2":
        s = slice(key[1] * 256, key[1] * 256 + 256)
        return np.concatenate([tile(I["w_branch_a_2"][0], s), tile(I["w_branch_b_2"][0], s)], axis=1)
    if k == "wout2":
        return tile(I["w_out_2"][0], slice(key[1] * 512, key[1] * 512 + 512))
    if k == "router":
        s = slice(None)
        return np.concatenate([tile(I["router_group_2"][0], s), tile(I["router_expert_2"][0], s)], axis=2)
    if k == "eup":
        g, u = I["w_gate_2"][0, key[1]], I["w_up_2"][0, key[1]]
        return np.stack([np.stack([tile(w, slice(q * 128, q * 128 + 128)) for w in (g, u)], axis=1)
                         for q in range(2)], axis=1)
    if k == "edn":
        s = slice(None)
        return np.stack([tile(I["w_down_2"][0, 2 * key[1] + x], s) for x in range(2)], axis=1)
    raise KeyError(key)


def columns(I):
    o = np.zeros((128, NCOL), np.float32)

    def put(k, v):
        a, w = COLS[k]
        o[:v.shape[0], a:a + w] = v

    def rows(v):
        r = np.zeros((64, 1), np.float32)
        r[0:8, 0], r[32:40, 0] = v[0], v[1]
        return r

    put("c", colv(I["c"][0]))
    put("cx", colv(I["c_ctx"]))
    put("c2", colv(I["c_2"][0]))
    for l in range(2):
        put(f"bmod{l}", colv(I["b_mod"][l]))
        put(f"g{l}", colv(I["norm_g"][l]))
        put(f"bg{l}", colv(I["b_gate"][l]))
        put(f"sub{l}", colv(I["subln_g"][l]))
        put(f"lam{l}", I["lam_params"][l].T)
    put("fin", colv(I["final_g"]))
    put("ada", colv(I["ada_b_2"][0]))
    put("nmix", colv(I["norm_mix_g_2"][0]))
    put("nffn", colv(I["norm_ffn_g_2"][0]))
    put("cva", I["gdn_conv_w_2"][0].reshape(5, 12, 128).transpose(2, 1, 0).reshape(128, 60))
    put("cvb", I["mlstm_conv_w_2"][0].reshape(5, 8, 128).transpose(2, 1, 0).reshape(128, 40))
    put("gdn", np.concatenate([I["gdn_norm_g_2"][0]] * 2)[:, None])
    put("mln", colv(I["mlstm_norm_g_2"][0]))
    put("fin2", colv(I["final_norm_g_2"]))
    put("rows", np.concatenate([rows(I[n][0]) for n in ("gdn_a_log_2", "gdn_dt_bias_2", "mlstm_i_bias_2",
                                                        "mlstm_f_bias_2")], axis=1))
    return o


WORDS = 110923776


def kernel(**inputs):
    import concourse.bacc as _bacc
    from concourse.bass_utils import run_bass_kernel_spmd as _run

    I = {k: np.asarray(v) for k, v in inputs.items()}
    nc = _bacc.Bacc("TRN2", target_bir_lowering=False, num_devices=1, dynamic_dma_scratch_size=4096)
    small = {"cols": columns(I)}
    small["c0"], small["c1"], small["c2"] = consts()
    ws = nc.dram_tensor("ws", (WORDS,), F32, kind="ExternalInput").ap()
    aps = {k: nc.dram_tensor(k, v.shape, F32, kind="ExternalInput").ap() for k, v in small.items()}
    out = nc.dram_tensor("out", (128, 2048), F32, kind="ExternalOutput").ap()
    plan = []
    program(nc, ws, aps["cols"], aps["c0"], aps["c1"], aps["c2"], out, plan)
    w = np.empty((WORDS,), np.float32)
    n = 0
    for key in plan:
        a = pack(key, I)
        w[n:n + a.size] = a.reshape(-1)
        n += a.size
    assert n == WORDS, n
    r = _run(nc, [{"ws": w, **small}], core_ids=[0])
    y = r.results[0]["out"].reshape(128, 8, 256).transpose(2, 1, 0).reshape(1, 256, 1024)
    return np.ascontiguousarray(y)
```
